# Optimizing a Trainium2 kernel written in Bass

```python
import math, functools
import jax, jax.numpy as jnp
from jax import lax
import numpy as np

D_MODEL = 1024
BATCH = 1
SEQ = 1024
DEPTH = 1
DEC_BATCH = 8
DEC_SEQ = 1
PAST_LEN = 256
PAGE_SIZE = 128

N_HEADS = 8
HEAD_DIM = 64
ATT_WIDTH = N_HEADS * HEAD_DIM
IDX_HEADS = 4
IDX_DIM = 64
TOPK_MAX = 256
Q_BLOCK = 128
N_BUCKETS = 32
MAX_DISTANCE = 128
SSM_WIDTH = 512
GROUP = 16
N_GROUPS = SSM_WIDTH // GROUP
STATE_DIM = 64
DT_MIN = 0.001
DT_MAX = 0.1
D_FF = 4 * D_MODEL
CONV_W = 3
EPS = 1e-6
SPLITS = (ATT_WIDTH, ATT_WIDTH, ATT_WIDTH, IDX_HEADS * IDX_DIM, IDX_DIM, IDX_HEADS, SSM_WIDTH, D_MODEL, D_MODEL)
IN_WIDTH = sum(SPLITS)

kernel_name = "dsa_s5_gated_hybrid_step"

def rmsnorm(x, g):
    xf = x.astype(jnp.float32)
    inv = lax.rsqrt(jnp.mean(xf * xf, axis=-1, keepdims=True) + EPS)
    return (xf * inv).astype(x.dtype) * g

def t5_bucket(rel):
    n = jnp.maximum(-rel, 0)
    max_exact = N_BUCKETS // 2
    nf = jnp.maximum(n, 1).astype(jnp.float32)
    large = max_exact + (jnp.log(nf / max_exact) / math.log(MAX_DISTANCE / max_exact)
                         * (N_BUCKETS - max_exact)).astype(jnp.int32)
    large = jnp.minimum(large, N_BUCKETS - 1)
    return jnp.where(n < max_exact, n, large)

def indexer_scores(q_idx, w_idx, k_idx):
    s = jnp.einsum('bthd,bsd->bths', q_idx, k_idx).astype(jnp.float32) * IDX_DIM ** -0.5
    return jnp.einsum('bths,bth->bts', jax.nn.relu(s), w_idx.astype(jnp.float32))

def sparse_attend(q, k_sel, v_sel, sel, q_pos, valid, rel_bias):
    logits = jnp.einsum('bthd,btkhd->bthk', q, k_sel).astype(jnp.float32) * HEAD_DIM ** -0.5
    bias = rel_bias[t5_bucket(sel - q_pos[None, :, None])]
    logits = logits + jnp.moveaxis(bias, -1, -2).astype(jnp.float32)
    logits = jnp.where(valid[:, :, None, :], logits, -jnp.inf)
    p = jax.nn.softmax(logits, axis=-1).astype(v_sel.dtype)
    return jnp.einsum('bthk,btkhd->bthd', p, v_sel)

def prompt_attention(q, k, v, q_idx, w_idx, k_idx, rel_bias):
    bsz, t = q.shape[:2]
    topk = min(TOPK_MAX, t // 4)
    key_pos = jnp.arange(t)
    bidx = jnp.arange(bsz)[:, None, None]

    def block(i):
        s0 = i * Q_BLOCK
        qb = lax.dynamic_slice_in_dim(q, s0, Q_BLOCK, axis=1)
        qib = lax.dynamic_slice_in_dim(q_idx, s0, Q_BLOCK, axis=1)
        wib = lax.dynamic_slice_in_dim(w_idx, s0, Q_BLOCK, axis=1)
        q_pos = s0 + jnp.arange(Q_BLOCK)
        score = indexer_scores(qib, wib, k_idx)
        causal = key_pos[None, :] <= q_pos[:, None]
        score = jnp.where(causal[None], score, -jnp.inf)
        _, sel = lax.top_k(score, topk)
        valid = sel <= q_pos[None, :, None]
        return sparse_attend(qb, k[bidx, sel], v[bidx, sel], sel, q_pos, valid, rel_bias)

    out = lax.map(block, jnp.arange(t // Q_BLOCK))
    return jnp.moveaxis(out, 0, 1).reshape(bsz, t, ATT_WIDTH)

def sample_attention(q, k, v, q_idx, w_idx, k_idx, cache_k, cache_v, cache_kidx, page_table, rel_bias):
    db, tq = q.shape[:2]
    past = page_table.shape[1] * PAGE_SIZE
    n_keys = past + tq
    topk = min(TOPK_MAX, n_keys // 4)
    kidx_past = cache_kidx[page_table].reshape(db, past, IDX_DIM)
    kidx_all = jnp.concatenate([kidx_past, k_idx.astype(kidx_past.dtype)], axis=1)
    q_pos = past + jnp.arange(tq)
    score = indexer_scores(q_idx, w_idx, kidx_all)
    causal = jnp.arange(n_keys)[None, :] <= q_pos[:, None]
    score = jnp.where(causal[None], score, -jnp.inf)
    _, sel = lax.top_k(score, topk)
    valid = sel <= q_pos[None, :, None]
    bidx = jnp.arange(db)[:, None, None]
    is_past = (sel < past)[..., None, None]
    sp = jnp.minimum(sel, past - 1)
    phys = page_table[bidx, sp // PAGE_SIZE]
    off = sp % PAGE_SIZE
    sn = jnp.clip(sel - past, 0, tq - 1)
    k_sel = jnp.where(is_past, cache_k[phys, off], k[bidx, sn].astype(cache_k.dtype))
    v_sel = jnp.where(is_past, cache_v[phys, off], v[bidx, sn].astype(cache_v.dtype))
    return sparse_attend(q, k_sel, v_sel, sel, q_pos, valid, rel_bias).reshape(db, tq, ATT_WIDTH)

def ssm_branch(u, x0_re, x0_im, lam_re, lam_im, log_dt, b_re, b_im, c_re, c_im, d_skip, w_glu, b_glu):
    f32 = jnp.float32
    bsz, t, _ = u.shape
    lam = lax.complex(lam_re.astype(f32), lam_im.astype(f32))
    dt = jnp.exp(log_dt.astype(f32))[:, None]
    lam_bar = jnp.exp(lam * dt)
    b = lax.complex(b_re.astype(f32), b_im.astype(f32))
    b_bar = ((lam_bar - 1.0) / lam)[..., None] * b
    uf = u.astype(f32)
    ug = uf.reshape(bsz, t, N_GROUPS, GROUP).astype(jnp.complex64)
    bu = jnp.einsum('gpc,btgc->btgp', b_bar, ug)
    x0 = lax.complex(x0_re.astype(f32), x0_im.astype(f32))
    bu = bu.at[:, 0].add(lam_bar * x0)
    a = jnp.broadcast_to(lam_bar, bu.shape)

    def combine(e1, e2):
        a1, b1 = e1
        a2, b2 = e2
        return a2 * a1, a2 * b1 + b2

    _, xs = lax.associative_scan(combine, (a, bu), axis=1)
    c = lax.complex(c_re.astype(f32), c_im.astype(f32))
    y = jnp.einsum('gcp,btgp->btgc', c, xs).real.reshape(bsz, t, SSM_WIDTH) + d_skip.astype(f32) * uf
    g = jax.nn.gelu(y)
    y = g * jax.nn.sigmoid(g @ w_glu.astype(f32) + b_glu.astype(f32))
    x_last = xs[:, -1]
    return y.astype(u.dtype), jnp.real(x_last), jnp.imag(x_last)

def conv_ffn(h, conv_prev, w_up, conv_w, conv_b, w_down):
    up = h @ w_up
    t = up.shape[1]
    ext = jnp.concatenate([conv_prev.astype(up.dtype), up], axis=1)
    acc = conv_b + ext[:, 0:t] * conv_w[0]
    for j in range(1, CONV_W):
        acc = acc + ext[:, j:j + t] * conv_w[j]
    a, b = jnp.split(acc, 2, axis=-1)
    out = (jax.nn.gelu(a) * b) @ w_down
    return out, ext[:, -(CONV_W - 1):]

def trunk_layer(x, attend, x0_re, x0_im, conv_prev, lw):
    (w_in, g_pre_mix, g_post_mix, lam_re, lam_im, log_dt, b_re, b_im, c_re, c_im, d_skip,
     w_glu, b_glu, w_att_out, w_ssm_out, w_o, g_pre_ffn, g_post_ffn, w_up, conv_w, conv_b, w_down) = lw
    bsz, t, _ = x.shape
    h = rmsnorm(x, g_pre_mix)
    points = np.cumsum(SPLITS)[:-1].tolist()
    q, k, v, q_idx, k_idx, w_idx, u, g_att, g_ssm = jnp.split(h @ w_in, points, axis=-1)
    q = q.reshape(bsz, t, N_HEADS, HEAD_DIM)
    k = k.reshape(bsz, t, N_HEADS, HEAD_DIM)
    v = v.reshape(bsz, t, N_HEADS, HEAD_DIM)
    q_idx = q_idx.reshape(bsz, t, IDX_HEADS, IDX_DIM)
    w_idx = w_idx * IDX_HEADS ** -0.5
    y_att = attend(q, k, v, q_idx, w_idx, k_idx)
    y_ssm, s_re, s_im = ssm_branch(u, x0_re, x0_im, lam_re, lam_im, log_dt, b_re, b_im,
                                   c_re, c_im, d_skip, w_glu, b_glu)
    merged = jax.nn.sigmoid(g_att) * (y_att @ w_att_out) + jax.nn.sigmoid(g_ssm) * (y_ssm @ w_ssm_out)
    x = x + rmsnorm(merged @ w_o, g_post_mix)
    f, conv_new = conv_ffn(rmsnorm(x, g_pre_ffn), conv_prev, w_up, conv_w, conv_b, w_down)
    x = x + rmsnorm(f, g_post_ffn)
    return x, (k, v, k_idx, s_re, s_im, conv_new)

def setup_inputs(seed: int = 0) -> dict:
    key = jax.random.key(seed)
    keys = list(jax.random.split(key, 40))

    def nrm(i, shape, scale):
        return jax.random.normal(keys[i], shape, jnp.float32) * scale

    n_pages = PAST_LEN // PAGE_SIZE
    n_used = DEC_BATCH * n_pages
    n_pool = n_used + n_used // 4
    page_table = jax.random.permutation(keys[0], n_pool)[:n_used].reshape(DEC_BATCH, n_pages).astype(jnp.int32)
    lam_im = (math.pi * jnp.arange(STATE_DIM, dtype=jnp.float32))[None, None, :] + nrm(13, (DEPTH, N_GROUPS, STATE_DIM), 0.01)
    return {
        "x_prompt": nrm(1, (BATCH, SEQ, D_MODEL), 1.0),
        "x_sample": nrm(2, (DEC_BATCH, DEC_SEQ, D_MODEL), 1.0),
        "cache_k": nrm(3, (DEPTH, n_pool, PAGE_SIZE, N_HEADS, HEAD_DIM), 1.0),
        "cache_v": nrm(4, (DEPTH, n_pool, PAGE_SIZE, N_HEADS, HEAD_DIM), 1.0),
        "cache_kidx": nrm(5, (DEPTH, n_pool, PAGE_SIZE, IDX_DIM), 1.0),
        "state_ssm_re": nrm(6, (DEPTH, DEC_BATCH, N_GROUPS, STATE_DIM), 1.0),
        "state_ssm_im": nrm(7, (DEPTH, DEC_BATCH, N_GROUPS, STATE_DIM), 1.0),
        "state_conv": nrm(8, (DEPTH, DEC_BATCH, CONV_W - 1, 2 * D_FF), 1.0),
        "page_table": page_table,
        "rel_bias": nrm(9, (N_BUCKETS, N_HEADS), 0.5),
        "w_in": nrm(10, (DEPTH, D_MODEL, IN_WIDTH), D_MODEL ** -0.5),
        "g_pre_mix": 1.0 + nrm(11, (DEPTH, D_MODEL), 0.1),
        "g_post_mix": 1.0 + nrm(12, (DEPTH, D_MODEL), 0.1),
        "lam_re": -0.5 + nrm(14, (DEPTH, N_GROUPS, STATE_DIM), 0.01),
        "lam_im": lam_im,
        "log_dt": jax.random.uniform(keys[15], (DEPTH, N_GROUPS), jnp.float32, math.log(DT_MIN), math.log(DT_MAX)),
        "b_re": nrm(16, (DEPTH, N_GROUPS, STATE_DIM, GROUP), (2 * GROUP) ** -0.5),
        "b_im": nrm(17, (DEPTH, N_GROUPS, STATE_DIM, GROUP), (2 * GROUP) ** -0.5),
        "c_re": nrm(18, (DEPTH, N_GROUPS, GROUP, STATE_DIM), (2 * STATE_DIM) ** -0.5),
        "c_im": nrm(19, (DEPTH, N_GROUPS, GROUP, STATE_DIM), (2 * STATE_DIM) ** -0.5),
        "d_skip": nrm(20, (DEPTH, SSM_WIDTH), 1.0),
        "w_glu": nrm(21, (DEPTH, SSM_WIDTH, SSM_WIDTH), SSM_WIDTH ** -0.5),
        "b_glu": nrm(22, (DEPTH, SSM_WIDTH), 0.01),
        "w_att_out": nrm(23, (DEPTH, ATT_WIDTH, D_MODEL), ATT_WIDTH ** -0.5),
        "w_ssm_out": nrm(24, (DEPTH, SSM_WIDTH, D_MODEL), SSM_WIDTH ** -0.5),
        "w_o": nrm(25, (DEPTH, D_MODEL, D_MODEL), D_MODEL ** -0.5),
        "g_pre_ffn": 1.0 + nrm(26, (DEPTH, D_MODEL), 0.1),
        "g_post_ffn": 1.0 + nrm(27, (DEPTH, D_MODEL), 0.1),
        "w_up": nrm(28, (DEPTH, D_MODEL, 2 * D_FF), D_MODEL ** -0.5),
        "conv_w": nrm(29, (DEPTH, CONV_W, 2 * D_FF), CONV_W ** -0.5),
        "conv_b": nrm(30, (DEPTH, 2 * D_FF), 0.01),
        "w_down": nrm(31, (DEPTH, D_FF, D_MODEL), D_FF ** -0.5),
    }

def reference(x_prompt, x_sample, cache_k, cache_v, cache_kidx, state_ssm_re, state_ssm_im, state_conv,
              page_table, rel_bias, w_in, g_pre_mix, g_post_mix, lam_re, lam_im, log_dt, b_re, b_im,
              c_re, c_im, d_skip, w_glu, b_glu, w_att_out, w_ssm_out, w_o, g_pre_ffn, g_post_ffn,
              w_up, conv_w, conv_b, w_down):
    bp = x_prompt.shape[0]
    y_p, y_s = x_prompt, x_sample
    outs_p, outs_s = [], []
    for l in range(DEPTH):
        lw = (w_in[l], g_pre_mix[l], g_post_mix[l], lam_re[l], lam_im[l], log_dt[l], b_re[l], b_im[l],
              c_re[l], c_im[l], d_skip[l], w_glu[l], b_glu[l], w_att_out[l], w_ssm_out[l], w_o[l],
              g_pre_ffn[l], g_post_ffn[l], w_up[l], conv_w[l], conv_b[l], w_down[l])
        zero_ssm = jnp.zeros((bp, N_GROUPS, STATE_DIM), jnp.float32)
        zero_conv = jnp.zeros((bp, CONV_W - 1, 2 * D_FF), x_prompt.dtype)
        attend_p = functools.partial(prompt_attention, rel_bias=rel_bias)
        y_p, st_p = trunk_layer(y_p, attend_p, zero_ssm, zero_ssm, zero_conv, lw)
        attend_s = functools.partial(sample_attention, cache_k=cache_k[l], cache_v=cache_v[l],
                                     cache_kidx=cache_kidx[l], page_table=page_table, rel_bias=rel_bias)
        y_s, st_s = trunk_layer(y_s, attend_s, state_ssm_re[l], state_ssm_im[l], state_conv[l], lw)
        outs_p.append(st_p)
        outs_s.append(st_s)
    k_p, v_p, ki_p, sr_p, si_p, cv_p = [jnp.stack(a) for a in zip(*outs_p)]
    k_s, v_s, ki_s, sr_s, si_s, cv_s = [jnp.stack(a) for a in zip(*outs_s)]
    return (y_p, y_s, k_p, v_p, ki_p, sr_p, si_p, cv_p, k_s, v_s, ki_s, sr_s, si_s, cv_s)


_drawn_inputs = setup_inputs


def setup_inputs(seed=0):
    import zlib

    import numpy as np

    out = dict(_drawn_inputs(seed))
    spreads = {}
    factors = {'lam_re': 3.942, 'b_glu': 8.0, 'conv_b': 6.698}
    for name, (base, spread) in spreads.items():
        noise = np.random.default_rng([zlib.crc32(name.encode()), seed]).standard_normal(out[name].shape)
        drawn = base * np.exp(spread * noise) if base else spread * noise
        out[name] = __import__('jax').numpy.asarray(drawn.astype(out[name].dtype))
    for name, factor in factors.items():
        out[name] = (out[name] * factor).astype(out[name].dtype)
    return out
```

```python
from contextlib import ExitStack
import math

import numpy as np
import concourse.bass as bass
from concourse import mybir

ALU = mybir.AluOpType
ACT = mybir.ActivationFunctionType
AX = mybir.AxisListType
F32 = mybir.dt.float32
F32R = mybir.dt.float32r
I32 = mybir.dt.int32

P = 128
D = 1024
KD = D // P
NP = 1024
NS = 8
T = NP + NS
NT = NP // P
TILES = [(i * P, P) for i in range(NT)] + [(NP, NS)]
CH = T // 3
BANK = 512
H, HD = 8, 64
AW = H * HD
JH, ID = 4, 64
TOPK = 256
PAST, PAGE = 256, 128
SK = PAST + 1
STOPK = SK // 4
NB = 32
SW, GC, NG, ST = 512, 16, 32, 64
L = 8
NC = NP // L
FF = 4096
EPS = 1e-6
NOT_CAUSAL = -3.0e38
LATE_ROUNDS = 16
TAKEN = -3.4e38
HIDE = -1.0e30
Q0, K0, V0, QI0, KI0, U0, GA0, GS0 = 0, 512, 1024, 1536, 1792, 1860, 2372, 3396


def split3(pe, out, wh, wl, xh, xl, first, last):
    pe.matmul(out, wh, xh, start=first, stop=False)
    pe.matmul(out, wh, xl, start=False, stop=False)
    return pe.matmul(out, wl, xh, start=False, stop=last)


def project(pe, ps, slot, wh, wl, xh, xl, kt, m=P):
    for k in range(kt):
        for n, (w, x) in enumerate(((wh, xh), (wh, xl), (wl, xh))):
            for c in range(3):
                mm = pe.matmul(ps[0:m, 3 * slot + c, 0:CH], w[:, k, 0:m], x[:, k, c * CH:(c + 1) * CH],
                               start=(k == 0 and n == 0), stop=(k == kt - 1 and n == 2))
    return mm


def thirds(ps, slot, m=P):
    return ps[0:m, 3 * slot:3 * slot + 3, 0:CH]


def as_thirds(ap):
    return ap.rearrange("p (c t) -> p c t", c=3)


def newton_rstd(dve, rstd, std, var, done, base=0):
    dve.reciprocal(rstd[:, :], std[:, :]).then_inc(done, 1)
    dve.wait_ge(done, base + 1)
    dve.tensor_tensor(std[:, :], rstd[:, :], rstd[:, :], ALU.mult).then_inc(done, 1)
    dve.wait_ge(done, base + 2)
    dve.tensor_tensor(std[:, :], std[:, :], var[:, :], ALU.mult).then_inc(done, 1)
    dve.wait_ge(done, base + 3)
    dve.tensor_scalar(std[:, :], std[:, :], -0.5, 1.5, ALU.mult, ALU.add).then_inc(done, 1)
    dve.wait_ge(done, base + 4)
    dve.tensor_tensor(rstd[:, :], rstd[:, :], std[:, :], ALU.mult).then_inc(done, 1)
    dve.wait_ge(done, base + 5)


def phase_norm(nc, g):
    with ExitStack() as ctx:
        sb = lambda n, s, d=F32: ctx.enter_context(nc.sbuf_tensor(n, s, d))
        x_all = sb("n_x", [P, 9, D])
        gain = sb("n_gain", [P, D])
        junk = sb("n_junk", [P, D])
        xn = sb("n_xn", [P, 2, D])
        ss = sb("n_ss", [P, 9])
        var = sb("n_var", [P, 9])
        std = sb("n_std", [P, 9])
        rstd = sb("n_rstd", [P, 9])
        psf = g.ps[:, :, :].rearrange("p b c -> p (b c)")
        sem = g.sem
        x_in = [sem(f"n_x_in{i}") for i in range(3)]
        gain_in, ident_in = sem("n_gain_in"), sem("n_ident_in")
        ss_zero, ss_done, var_done, std_done, rstd_done = (sem("n_" + s) for s in
                                                           ("ss_zero", "ss_done", "var_done", "std_done", "rstd_done"))
        xn_done, turned, hi_done, lo_done = (sem("n_" + s) for s in ("xn_done", "turned", "hi_done", "lo_done"))
        block = ctx.enter_context(nc.Block())

        @block.sync
        def _(sp):
            xv = g.x_prompt.rearrange("b (i p) d -> p (b i) d", p=P)
            sp.dma_start(x_all[:, 0:4, :], xv[:, 0:4, :]).then_inc(x_in[0], 16)
            sp.dma_start(x_all[:, 4:8, :], xv[:, 4:8, :]).then_inc(x_in[1], 16)
            sp.dma_start(x_all[0:NS, 8, :], g.x_sample.rearrange("b t d -> (b t) d")).then_inc(x_in[2], 16)
            sp.dma_start(gain[:, :], g.g_pre_mix.partition_broadcast(P)).then_inc(gain_in, 16)
            sp.dma_start(g.ident[:, :], g.c_ident).then_inc(ident_in, 16)

        @block.scalar
        def _(act):
            act.wait_ge(ss_zero, 1)
            for i, (_, n) in enumerate(TILES):
                if i % 4 == 0:
                    act.wait_ge(x_in[i // 4], 16)
                if i:
                    act.wait_ge(ss_done, i)
                act.activation(junk[0:n, :], x_all[0:n, i, :], ACT.Square,
                               accum_out=ss[0:n, i:i + 1]).then_inc(ss_done, 1)
            act.wait_ge(var_done, 1)
            act.activation(std[:, :], var[:, :], ACT.Sqrt).then_inc(std_done, 1)
            for i, (t0, n) in enumerate(TILES):
                act.wait_ge(turned, i + 1)
                act.activation(g.hT_h[:, :, t0:t0 + n],
                               psf[:, (i % 2) * 1024:(i % 2) * 1024 + 1024].rearrange(
                                   "p (k t) -> p k t", k=KD)[:, :, 0:n], ACT.Copy).then_inc(hi_done, 1)

        @block.vector
        def _(dve):
            dve.memset(ss[:, :], 1.0).then_inc(ss_zero, 1)
            dve.wait_ge(ss_done, 9)
            dve.tensor_scalar(var[:, :], ss[:, :], 1.0 / D, EPS, ALU.mult, ALU.add).then_inc(var_done, 1)
            dve.wait_ge(std_done, 1)
            newton_rstd(dve, rstd, std, var, rstd_done)
            dve.wait_ge(gain_in, 16)

            def low_part(i):
                t0, n = TILES[i]
                dve.wait_ge(hi_done, i + 1)
                dve.tensor_tensor(g.hT_l[:, :, t0:t0 + n],
                                  psf[:, (i % 2) * 1024:(i % 2) * 1024 + 1024].rearrange(
                                      "p (k t) -> p k t", k=KD)[:, :, 0:n],
                                  g.hT_h[:, :, t0:t0 + n].bitcast(F32), ALU.subtract).then_inc(lo_done, 1)

            for i, (_, n) in enumerate(TILES):
                if i >= 2:
                    dve.wait_ge(turned, i - 1)
                dve.scalar_tensor_tensor(out=xn[0:n, i % 2, :], in0=x_all[0:n, i, :], scalar=rstd[0:n, i:i + 1],
                                         in1=gain[0:n, :], op0=ALU.mult, op1=ALU.mult).then_inc(xn_done, 1)
                if i:
                    low_part(i - 1)
            low_part(8)

        @block.tensor
        def _(pe):
            pe.wait_ge(ident_in, 16)
            for i, (_, n) in enumerate(TILES):
                pe.wait_ge(xn_done, i + 1)
                if i >= 2:
                    pe.wait_ge(lo_done, i - 1)
                for k in range(KD):
                    o = (i % 2) * 1024 + k * P
                    mm = pe.transpose(psf[:, o:o + n], xn[0:n, i % 2, k * P:(k + 1) * P], g.ident[0:n, 0:n])
                mm.then_inc(turned, 1)


def phase_project(nc, g):
    with ExitStack() as ctx:
        sb = lambda n, s, d=F32: ctx.enter_context(nc.sbuf_tensor(n, s, d))
        ps, sem = g.ps, g.sem
        wst = sb("j_wst", [P, 2, KD, P])
        wh = sb("j_wh", [P, 2, KD, P], F32R)
        wl = sb("j_wl", [P, 2, KD, P], F32R)
        ring = sb("j_ring", [P, 2, T])
        tok = sb("j_tok", [P, 2, NT, P])
        tok_s = sb("j_tok_s", [NS, 3, AW])
        kvs = sb("j_kvs", [P, 3, 4, NS])
        kw_tok = sb("j_kw_tok", [P, 9, 68])
        rel = sb("j_rel", [P, 2, NP])
        m8 = sb("j_m8", [P, 8])
        nci = sb("j_nci", [P, P])
        psf = ps[:, :, :].rearrange("p b c -> p (b c)")

        units = [(QI0, P, "qi"), (QI0 + P, P, "qi"), (KI0, 68, "kw")]
        units += [(Q0 + m * P, P, "q") for m in range(4)]
        units += [(GA0 + m * P, P, "g") for m in range(4)]
        NLEAD = len(units)
        NLOOP = 12
        tail = [(base + m * P, P, kind) for base, kind in ((K0, "k"), (V0, "v"), (U0, "u")) for m in range(4)]
        NU = NLEAD + NLOOP + len(tail)
        TAIL0 = NLEAD + NLOOP
        GATE0 = 7

        w_in = [sem(f"j_w_in{i}") for i in range(2)]
        w_hi, w_lo, unit_done, evac = (sem("j_" + s) for s in ("w_hi", "w_lo", "unit_done", "evac"))
        gate_out = [sem(f"j_gate_out{i}") for i in range(2)]
        kw_turned, kw_copied, kw_out = sem("j_kw_turned"), sem("j_kw_copied"), sem("j_kw_out")
        s_done, rel_done, acc_done, dve_step = (sem("j_" + s) for s in ("s_done", "rel_done", "acc_done", "dve_step"))
        tok_turned, tok_copied, sam_turned, sam_copied = (sem("j_" + s) for s in
                                                          ("tok_turned", "tok_copied", "sam_turned", "sam_copied"))
        tok_out = [sem(f"j_tok_out{i}") for i in range(2)]
        sam_out, nci_in = sem("j_sam_out"), sem("j_nci_in")
        kvs_done = sem("j_kvs_done")
        block = ctx.enter_context(nc.Block())

        wv = g.w_in.rearrange("(k p) n -> p k n", p=P)
        scores = [(i, h) for i in range(2, NT) for h in range(JH)]
        SU = 4

        def scores_of(u):
            return [s for s in range(4 * (u - SU), 4 * (u - SU) + 4) if 0 <= s < len(scores)]

        def kvs_count(n):
            return n + 1 + min(n + 1, 4)

        @block.sync
        def _(sp):
            sp.dma_start(nci[:, :], g.c_not_causal).then_inc(nci_in, 16)

            def load_w(u, s, cols, n):
                sp.dma_start(wst[:, s, :, 0:n], cols).then_inc(w_in[s], 16)

            def gate_store(gt, u, s):
                sp.wait_ge(evac, u + 1)
                sp.dma_start(gt, ring[:, s, :]).then_inc(gate_out[s], 16)

            for u in range(NLEAD):
                if u >= 2:
                    sp.wait_ge(w_lo, u - 1)
                load_w(u, u % 2, wv[:, :, units[u][0]:units[u][0] + units[u][1]], units[u][1])
                if u - 1 >= GATE0:
                    gate_store(g.d_gates[:, u - 1 - GATE0, :], u - 1, (u - 1) % 2)
            with sp.Fori(0, NLOOP // 2) as j:
                for e in range(2):
                    u = NLEAD + e
                    sp.wait_ge(w_lo, j * 2 + (u - 1))
                    load_w(u, u % 2, wv[:, :, bass.ds(GA0 + 4 * P + j * (2 * P) + e * P, P)], P)
                    gate_store(g.d_gates[:, bass.ds(j * 2 + (u - 1 - GATE0), 1), :].rearrange("p a t -> p (a t)"),
                               j * 2 + (u - 1), (u - 1) % 2)
            outs = {"k": (g.k_prompt, g.k_sample, 0), "v": (g.v_prompt, g.v_sample, 1)}

            def tok_store(n):
                _, _, kind = tail[n]
                m = n % 4
                sp.wait_ge(tok_copied, n + 1)
                if kind == "u":
                    dst = g.d_u.rearrange("(k l) c -> k l c", l=L)[:, :, m * P:(m + 1) * P]
                else:
                    dst = outs[kind][0].rearrange("(i p) c -> p i c", p=P)[:, :, m * P:(m + 1) * P]
                sp.dma_start(dst, tok[:, n % 2, :, :]).then_inc(tok_out[n % 2], 16)
                if m == 3:
                    q = n // 4
                    sp.wait_ge(sam_copied, q + 1)
                    dst = g.d_us if kind == "u" else outs[kind][1]
                    sp.dma_start(dst, tok_s[:, q, :]).then_inc(sam_out, 16)

            for n in range(len(tail)):
                u = TAIL0 + n
                sp.wait_ge(w_lo, u - 1)
                load_w(u, u % 2, wv[:, :, tail[n][0]:tail[n][0] + P], P)
                if n == 0:
                    gate_store(g.d_gates[:, u - 1 - GATE0, :], u - 1, (u - 1) % 2)
                if n == 1:
                    sp.wait_ge(kw_copied, 2)
                    sp.dma_start(g.kidx_prompt.rearrange("(i p) c -> p i c", p=P),
                                 kw_tok[:, 0:NT, 0:ID]).then_inc(kw_out, 16)
                    sp.dma_start(g.kidx_sample, kw_tok[0:NS, NT, 0:ID]).then_inc(kw_out, 16)
                if n >= 2:
                    tok_store(n - 2)
            tok_store(len(tail) - 2)
            tok_store(len(tail) - 1)
            for s in range(2):
                sp.wait_ge(gate_out[s], 16 * 8)
                sp.wait_ge(tok_out[s], 16 * 6)
            sp.wait_ge(sam_out, 48)
            sp.wait_ge(kw_out, 32)

        @block.gpsimd
        def _(pool):
            def low(u, s, n):
                pool.wait_ge(w_hi, u + 1)
                pool.tensor_tensor(wl[:, s, :, 0:n], wst[:, s, :, 0:n], wh[:, s, :, 0:n].bitcast(F32),
                                   ALU.subtract).then_inc(w_lo, 1)
            for u in range(NLEAD):
                low(u, u % 2, units[u][1])
            with pool.Fori(0, NLOOP // 2) as j:
                for e in range(2):
                    low(j * 2 + (NLEAD + e), (NLEAD + e) % 2, P)
            for n in range(len(tail)):
                u = TAIL0 + n
                if n == 0:
                    low(u, u % 2, P)
                if n + 1 < len(tail):
                    low(u + 1, (u + 1) % 2, P)
                pool.wait_ge(evac, u + 1)
                if tail[n][2] == "k":
                    pool.tensor_copy(g.kT[:, n % 4, :], ring[:, u % 2, :]).then_inc(kvs_done, 1)
                pool.tensor_copy(kvs[:, n // 4, n % 4, :], ring[:, u % 2, NP:T]).then_inc(kvs_done, 1)

        @block.scalar
        def _(act):
            def high(u, s, n, half):
                act.wait_ge(w_in[s], half)
                if not isinstance(u, int) or u >= 2:
                    act.wait_ge(unit_done, u - 1)
                act.activation(wh[:, s, :, 0:n], wst[:, s, :, 0:n], ACT.Copy).then_inc(w_hi, 1)

            def relu(s):
                i, _ = scores[s]
                n = (i + 1) * P
                act.wait_ge(s_done, s + 1)
                if s >= 2:
                    act.wait_ge(acc_done, s - 1)
                act.activation(rel[:, s % 2, 0:n], psf[:, 6 * BANK:6 * BANK + n], ACT.Relu).then_inc(rel_done, 1)

            def gate_evac(u, s, uses):
                act.wait_ge(unit_done, u + 1)
                if uses is not None:
                    act.wait_ge(gate_out[s], uses)
                act.activation(as_thirds(ring[:, s, :]), thirds(ps, s), ACT.Sigmoid).then_inc(evac, 1)

            high(0, 0, P, 16)
            for u in range(NLEAD):
                col, n, kind = units[u]
                for s in scores_of(u)[0:2]:
                    relu(s)
                nxt = u + 1
                high(nxt, nxt % 2, units[nxt][1] if nxt < NLEAD else P, 16 * (nxt // 2 + 1))
                for s in scores_of(u)[2:]:
                    relu(s)
                if kind == "g":
                    gate_evac(u, u % 2, 16 * ((u - GATE0) // 2) if u - GATE0 >= 2 else None)
                    continue
                act.wait_ge(unit_done, u + 1)
                dst = {"qi": lambda: g.qiT[:, u, :], "kw": lambda: g.kwT[:, :], "q": lambda: g.qT[:, u - 3, :]}[kind]()
                if kind == "kw":
                    act.activation(as_thirds(g.kiT2[ID:P, :]), thirds(ps, u % 2, ID), ACT.Copy)
                act.activation(as_thirds(dst), thirds(ps, u % 2, n), ACT.Copy).then_inc(evac, 1)
                if u == 3:
                    act.wait_ge(kw_turned, 1)
                    act.activation(kw_tok[:, 0:7, :], ps[:, 6, 0:7 * 68].rearrange("p (i c) -> p i c", c=68),
                                   ACT.Copy).then_inc(kw_copied, 1)
                    act.activation(kw_tok[:, 7, :], ps[:, 7, 0:68], ACT.Copy)
                    act.activation(kw_tok[0:NS, 8, :], ps[0:NS, 7, 68:2 * 68], ACT.Copy).then_inc(kw_copied, 1)
            with act.Fori(0, NLOOP // 2) as j:
                for e in range(2):
                    u = NLEAD + e
                    nxt = u + 1
                    high(j * 2 + nxt, nxt % 2, P, j * 16 + 16 * (nxt // 2 + 1))
                    gate_evac(j * 2 + u, u % 2, j * 16 + 16 * ((u - GATE0) // 2))

            def tok_copy(n):
                act.wait_ge(tok_turned, n + 1)
                if n >= 2:
                    act.wait_ge(tok_out[n % 2], 16 * ((n - 2) // 2 + 1))
                act.activation(tok[:, n % 2, :, :].rearrange("p i c -> p (i c)"), psf[:, 6 * BANK:8 * BANK],
                               ACT.Copy).then_inc(tok_copied, 1)
                if n % 4 == 3:
                    q = n // 4
                    act.wait_ge(sam_turned, q + 1)
                    act.activation(tok_s[:, q, :], ps[0:NS, 6, 0:AW], ACT.Copy).then_inc(sam_copied, 1)

            for n in range(len(tail)):
                u = TAIL0 + n
                kind = tail[n][2]
                if n + 1 < len(tail):
                    high(u + 1, (u + 1) % 2, P, 16 * ((u + 1) // 2 + 1))
                act.wait_ge(unit_done, u + 1)
                if n < 2:
                    act.wait_ge(gate_out[u % 2], 16 * 8)
                if n >= 2:
                    act.wait_ge(tok_turned, n - 1)
                    act.wait_ge(kvs_done, kvs_count(n - 2))
                act.activation(as_thirds(ring[:, u % 2, :]), thirds(ps, u % 2), ACT.Copy).then_inc(evac, 1)
                if n:
                    tok_copy(n - 1)
            tok_copy(len(tail) - 1)

        @block.vector
        def _(dve):
            steps = [0]

            def step(ins):
                ins.then_inc(dve_step, 1)
                steps[0] += 1
                dve.wait_ge(dve_step, steps[0])

            at = [2, 0]

            def top_rounds(n, last):
                while n > 0 and at[0] <= last:
                    sc = g.mask[at[0] - 2]
                    rounds = TOPK // 8 - (LATE_ROUNDS if at[0] == NT - 1 else 0)
                    m = min(n, rounds - at[1])
                    for _ in range(m):
                        step(dve.max(m8[:, :], sc))
                        step(dve.match_replace(out=sc, in_to_replace=m8[:, :], in_values=sc, imm_value=TAKEN))
                    n -= m
                    at[1] += m
                    if at[1] == rounds:
                        if rounds == TOPK // 8:
                            step(dve.tensor_scalar(sc, sc, -3.2e38, HIDE, ALU.is_gt, ALU.mult))
                        at[0] += 1
                        at[1] = 0

            dve.wait_ge(kw_copied, 2)
            dve.wait_ge(nci_in, 16)
            for s, (i, h) in enumerate(scores):
                sc, n = g.mask[i - 2], (i + 1) * P
                w = kw_tok[:, i, ID + h:ID + h + 1]
                dve.wait_ge(rel_done, s + 1)
                if h == 0:
                    ins = dve.tensor_scalar(sc, rel[:, s % 2, 0:n], w, None, ALU.mult)
                else:
                    ins = dve.scalar_tensor_tensor(out=sc, in0=rel[:, s % 2, 0:n], scalar=w, in1=sc,
                                                   op0=ALU.mult, op1=ALU.add)
                ins.then_inc(acc_done, 1)
                dve.wait_ge(acc_done, s + 1)
                if h == JH - 1:
                    step(dve.scalar_tensor_tensor(out=sc[:, i * P:n], in0=nci[:, :], scalar=NOT_CAUSAL,
                                                  in1=sc[:, i * P:n], op0=ALU.mult, op1=ALU.add))
                top_rounds(2, i if h == JH - 1 else i - 1)
            top_rounds(10 ** 6, NT - 1)

        @block.tensor
        def _(pe):
            def unit(u, s, n):
                pe.wait_ge(w_lo, u + 1)
                if not isinstance(u, int) or u >= 2:
                    pe.wait_ge(evac, u - 1)
                for k in range(KD):
                    if isinstance(u, int) and k % 2 == 0 and k // 2 < len(scores_of(u)):
                        score(scores_of(u)[k // 2])
                    for q, (w, x) in enumerate(((wh, g.hT_h), (wh, g.hT_l), (wl, g.hT_h))):
                        for c in range(3):
                            mm = pe.matmul(ps[0:n, 3 * s + c, 0:CH], w[:, s, k, 0:n], x[:, k, c * CH:(c + 1) * CH],
                                           start=(k == 0 and q == 0), stop=(k == KD - 1 and q == 2))
                mm.then_inc(unit_done, 1)

            def score(s):
                i, h = scores[s]
                if s >= 1:
                    pe.wait_ge(rel_done, s)
                else:
                    pe.wait_ge(kw_copied, 2)
                r = (h % 2) * ID
                keys = g.kwT if h % 2 == 0 else g.kiT2
                for c in range(0, (i + 1) * P, BANK):
                    n = min(BANK, (i + 1) * P - c)
                    mm = pe.matmul(psf[:, 6 * BANK + c:6 * BANK + c + n], g.qiT[r:r + ID, h // 2, i * P:(i + 1) * P],
                                   keys[r:r + ID, c:c + n], start=True, stop=True)
                mm.then_inc(s_done, 1)

            for u in range(NLEAD):
                unit(u, u % 2, units[u][1])
                if u == 3:
                    pe.wait_ge(evac, 3)
                    for i, (t0, n) in enumerate(TILES):
                        o = (6 if i < 7 else 7) * BANK + (i if i < 7 else i - 7) * 68
                        mm = pe.transpose(psf[0:n, o:o + 68], g.kwT[:, t0:t0 + n], g.ident[0:68, 0:68])
                    mm.then_inc(kw_turned, 1)
            with pe.Fori(0, NLOOP // 2) as j:
                for e in range(2):
                    unit(j * 2 + (NLEAD + e), (NLEAD + e) % 2, P)

            def turn(n):
                u = TAIL0 + n
                kind = tail[n][2]
                pe.wait_ge(evac, u + 1)
                if n >= 1:
                    pe.wait_ge(tok_copied, n)
                    if n % 4 == 0:
                        pe.wait_ge(sam_copied, n // 4)
                else:
                    pe.wait_ge(rel_done, len(scores))
                for i in range(NT):
                    src = ring[:, u % 2, i:NP:L] if kind == "u" else ring[:, u % 2, i * P:(i + 1) * P]
                    o = 6 * BANK + i * P
                    mm = pe.transpose(psf[:, o:o + P], src, g.ident[:, :])
                mm.then_inc(tok_turned, 1)
                if n % 4 == 3:
                    pe.wait_ge(tok_copied, n + 1)
                    pe.wait_ge(kvs_done, kvs_count(n))
                    for m in range(4):
                        mm = pe.transpose(ps[0:NS, 6, m * P:(m + 1) * P], kvs[:, n // 4, m, :], g.ident[:, :])
                    mm.then_inc(sam_turned, 1)

            for n in range(len(tail)):
                u = TAIL0 + n
                unit(u, u % 2, P)
                if n:
                    turn(n - 1)
            turn(len(tail) - 1)


def over(ap, n):
    return ap.unsqueeze(len(ap.shape)).broadcast_to([*ap.shape, n])


def mid(ap, n):
    p, gg, c = ap.shape
    return ap.unsqueeze(2).broadcast_to([p, gg, n, c])


def phase_ssm(nc, g):
    GB, NBATCH = 8, NG // 8
    with ExitStack() as ctx:
        sb = lambda n, s, d=F32: ctx.enter_context(nc.sbuf_tensor("s_" + n, s, d))
        ps, sem0 = g.ps, g.sem
        sem = lambda n: sem0("s_" + n)
        psf = ps[:, :, :].rearrange("p b c -> p (b c)")
        lam_st = sb("lam_st", [NG, 2, 2, ST])
        lr, li = sb("lr", [P, NG]), sb("li", [P, NG])
        dt = sb("dt", [P, NG])
        v = sb("v", [P, 16, NG])
        ki = sb("ki", [P, NG], I32)
        sgn, swap = sb("sgn", [P, 1]), sb("swap", [P, P])
        b_x, b_s = sb("b_x", [P, NG, GC]), sb("b_s", [P, NG, GC])
        bb_x, bb_s = sb("bb_x", [P, NG, GC]), sb("bb_s", [P, NG, GC])
        bt = sb("bt", [P, NG, GC])
        c_st = sb("c_st", [P, 2, 4, P])
        c_x, c_s = sb("c_x", [P, NG, GC]), sb("c_s", [P, NG, GC])
        pr, pi = sb("pr", [P, NG, L + 1]), sb("pi", [P, NG, L + 1])
        qr, qi = sb("qr", [P, NG, L]), sb("qi", [P, NG, L])
        wr, wi = sb("wr", [P, NG]), sb("wi", [P, NG])
        rad = sb("rad", [P, NG])
        t1, t2 = sb("t1", [P, NG, L // 2]), sb("t2", [P, NG, L // 2])
        dsk = sb("dsk", [GC, NG])

        u_tok = sb("u_tok", [P, L, P])
        us_tok = sb("us_tok", [NS, L, P])
        u_grp, us_grp = sb("u_grp", [P, GB, L, GC]), sb("us_grp", [NS, GB, L, GC])
        u = sb("u", [P, GB, P + NS])
        bl, cl = sb("bl", [P, GB, L, GC]), sb("cl", [P, GB, L + 1, GC])
        ta = sb("ta", [P, GB, L + 1, GC])
        bst = sb("bst", [P, GB, P])
        kt = sb("kt", [GC, GB, L, GC])
        mi = sb("mi", [P, GB, P])
        tc, ts = sb("tc", [P, GB, NC]), sb("ts", [P, GB, NC])
        xin = sb("xin", [P, GB, P + NS])
        z = sb("z", [P, GB, NC])
        tb = sb("tb", [P, GB, NC])
        xall = sb("xall", [P, GB, NC + 1])
        st_x = sb("st_x", [GB * NS, 2, P])
        x0, x0s, x1 = (sb(n, [P, NS, GB]) for n in ("x0", "x0s", "x1"))
        x1t = sb("x1t", [GB * NS, P])
        xlt = sb("xlt", [GB, P])
        y, ys = sb("y", [P, L, P]), sb("ys", [NS, P])

        par_in, bc_in, lam_turned, c_turned, par_ready = (sem(n) for n in ("par_in", "bc_in", "lam_turned", "c_turned",
                                                                           "par_ready"))
        act_par, dve_par, c_ready = sem("act_par"), sem("dve_par"), sem("c_ready")
        zeroed = sem("zeroed")
        u_grouped = sem("u_grouped")
        u_in, st_in, us_in = sem("u_in"), sem("st_in"), sem("us_in")
        u_turned, u_copied, st_turned, st_copied = (sem(n) for n in ("u_turned", "u_copied", "st_turned", "st_copied"))
        bl_ready, cl_ready, b_turned, b_copied = (sem(n) for n in ("bl_ready", "cl_ready", "b_turned", "b_copied"))
        kt_done, kt_copied, kt_ready, mi_in = (sem(n) for n in ("kt_done", "kt_copied", "kt_ready", "mi_in"))
        tab_ready, xin_done, xin_copied, xs_done, z_ready, zs_done, x_ready, x1_ready = (
            sem(n) for n in ("tab_ready", "xin_done", "xin_copied", "xs_done", "z_ready", "zs_done", "x_ready", "x1_ready"))
        y_done, y_gelu, y_turned, y_copied, last_turned, last_copied, last_out = (
            sem(n) for n in ("y_done", "y_gelu", "y_turned", "y_copied", "last_turned", "last_copied", "last_out"))
        dv = sem("dve_step")
        block = ctx.enter_context(nc.Block())

        @block.sync
        def _(sp):
            for q, src in enumerate((g.lam_re, g.lam_im)):
                for half in range(2):
                    sp.dma_start(lam_st[:, q, half, :], src).then_inc(par_in, 16)
            sp.dma_start(dt[:, :], g.log_dt.partition_broadcast(P)).then_inc(par_in, 16)
            sp.dma_start(sgn[:, :], g.c_sign).then_inc(par_in, 16)
            sp.dma_start(swap[:, :], g.c_swap).then_inc(par_in, 16)
            sp.dma_start(dsk[:, :], g.d_skip.rearrange("(g c) -> c g", c=GC),
                         allow_slow_non_contiguous=True).then_inc(par_in, 16)
            for dst, lo_, hi_ in ((b_x, g.b_re, g.b_im), (b_s, g.b_im, g.b_re)):
                sp.dma_start(dst[0:ST, :, :], lo_.rearrange("g p c -> p g c")).then_inc(bc_in, 16)
                sp.dma_start(dst[ST:P, :, :], hi_.rearrange("g p c -> p g c")).then_inc(bc_in, 16)
            for q, (lo_, hi_) in enumerate(((g.c_re, g.c_im), (g.c_im, g.c_re))):
                for half, src in enumerate((lo_, hi_)):
                    sp.dma_start(c_st[:, q, :, half * ST:(half + 1) * ST],
                                 src.rearrange("(a g) c p -> (g c) a p", a=4)).then_inc(bc_in, 16)
            uv = g.d_u.rearrange("(k l) c -> k l c", l=L)
            for b in range(NBATCH):
                if b:
                    sp.wait_ge(u_grouped, b)
                    sp.wait_ge(st_turned, b)
                else:
                    sp.wait_ge(zeroed, 2)
                cs = slice(b * P, (b + 1) * P)
                sp.dma_start(u_tok[:, :, :], uv[:, :, cs]).then_inc(u_in, 16)
                sp.dma_start(us_tok[:, L - 1, :], g.d_us[:, cs]).then_inc(us_in, 16)
                for q, (lo_, hi_) in enumerate(((g.state_re, g.state_im), (g.state_im, g.state_re))):
                    for half, src in enumerate((lo_, hi_)):
                        for smp in range(NS):
                            sp.dma_start(st_x[smp * GB:(smp + 1) * GB, q, half * ST:(half + 1) * ST],
                                         src[smp, b * GB:(b + 1) * GB, :]).then_inc(st_in, 16)
                sp.wait_ge(kt_ready, b + 1)
                if b:
                    sp.wait_ge(y_done, b)
                for l in range(L):
                    sp.dma_start(mi[l * GC:(l + 1) * GC, :, l * GC:P],
                                 kt[:, :, 0:L - l, :].rearrange("c g l d -> c g (l d)")).then_inc(mi_in, 16)
                sp.wait_ge(last_copied, b + 1)
                for half, (pd, sd) in enumerate(((g.ssm_re_prompt, g.ssm_re_sample), (g.ssm_im_prompt, g.ssm_im_sample))):
                    sp.dma_start(pd[b * GB:(b + 1) * GB, :], xlt[:, half * ST:(half + 1) * ST]).then_inc(last_out, 16)
                    for smp in range(NS):
                        sp.dma_start(sd[smp, b * GB:(b + 1) * GB, :],
                                     x1t[smp * GB:(smp + 1) * GB, half * ST:(half + 1) * ST]).then_inc(last_out, 16)
            sp.wait_ge(last_out, 16 * 18 * NBATCH)

        @block.gpsimd
        def _(pool):
            pool.memset(mi[:, :, :], 0.0).then_inc(zeroed, 1)
            pool.memset(us_tok[:, :, :], 0.0).then_inc(zeroed, 1)
            for b in range(NBATCH):
                pool.wait_ge(u_in, 16 * (b + 1))
                pool.wait_ge(us_in, 16 * (b + 1))
                if b == 0:
                    pool.wait_ge(zeroed, 2)
                else:
                    pool.wait_ge(u_turned, b)
                pool.tensor_copy(u_grp[:, :, :, :], u_tok[:, :, :].rearrange("p l (g c) -> p g l c", c=GC))
                pool.tensor_copy(us_grp[:, :, :, :],
                                 us_tok[:, :, :].rearrange("p l (g c) -> p g l c", c=GC)).then_inc(u_grouped, 1)

        R = lambda n: v[:, n, :]

        @block.scalar
        def _(act):
            act.wait_ge(dve_par, 1)
            act.activation(R(8), R(6), ACT.Sin).then_inc(act_par, 1)
            act.activation(R(9), R(6), ACT.Sin, scale=0.5).then_inc(act_par, 1)
            for b in range(NBATCH):
                last = b == 0

                def copy(out, in_, need, count, done, func=ACT.Copy):
                    act.wait_ge(need, count)
                    return act.activation(out, in_, func).then_inc(done, 1)

                act.wait_ge(u_turned, b + 1)
                if b:
                    act.wait_ge(y_done, b)
                for h in range(2):
                    act.activation(u[:, 4 * h:4 * h + 4, 0:P], ps[:, h, :].rearrange("p (g k) -> p g k", g=4), ACT.Copy)
                act.activation(u[:, :, P:P + NS], ps[:, 2, 0:GB * NS].rearrange("p (g k) -> p g k", g=GB),
                               ACT.Copy).then_inc(u_copied, 1)
                act.wait_ge(st_turned, b + 1)
                if b:
                    act.wait_ge(x1_ready, b)
                for q, dst in enumerate((x0, x0s)):
                    o = 3 * BANK + q * GB * NS
                    ins = act.activation(dst[:, :, :], psf[:, o:o + GB * NS].rearrange("p (b g) -> p b g", g=GB), ACT.Copy)
                ins.then_inc(st_copied, 1)
                act.wait_ge(b_turned, b + 1)
                act.activation(bst[:, :, :].rearrange("p g k -> p (g k)"), psf[:, 4 * BANK:6 * BANK],
                               ACT.Copy).then_inc(b_copied, 1)
                act.wait_ge(kt_done, b + 1)
                if b:
                    act.wait_ge(mi_in, 16 * L * b)
                act.activation(kt[:, :, :, :].rearrange("c g l d -> c (g l d)"), psf[0:GC, 6 * BANK:8 * BANK],
                               ACT.Copy).then_inc(kt_copied, 1)
                act.wait_ge(xin_done, b + 1)
                if b:
                    act.wait_ge(x1_ready, b)
                for h in range(2):
                    act.activation(xin[:, 4 * h:4 * h + 4, 0:P], ps[:, h, :].rearrange("p (g k) -> p g k", g=4), ACT.Copy)
                act.activation(xin[:, :, P:P + NS], ps[:, 2, 0:GB * NS].rearrange("p (g k) -> p g k", g=GB),
                               ACT.Copy).then_inc(xin_copied, 1)
                act.wait_ge(y_done, b + 1)
                if b:
                    act.wait_ge(y_turned, b)
                for h in range(2):
                    act.activation(y[:, :, h * 64:(h + 1) * 64].rearrange("p l (g c) -> p g l c", c=GC),
                                   ps[:, 4 + h, :].rearrange("p (g l c) -> p g l c", g=4, l=L), ACT.Gelu_apprx_tanh)
                act.activation(ys[:, :], ps[0:NS, 6, 0:P], ACT.Gelu_apprx_tanh).then_inc(y_gelu, 1)
                act.wait_ge(last_turned, b + 1)
                if b:
                    act.wait_ge(last_out, 16 * 18 * b)
                act.activation(xlt[:, :], ps[0:GB, 7, 0:P], ACT.Copy)
                act.activation(x1t[:, :], ps[0:GB * NS, 7, P:2 * P], ACT.Copy).then_inc(last_copied, 1)
                act.wait_ge(y_turned, b + 1)
                act.activation(g.gT[:, b, 0:NP].rearrange("p (k l) -> p l k", l=L),
                               psf[:, 0:2 * BANK].rearrange("p (l k) -> p l k", l=L), ACT.Copy)
                act.activation(g.gT[:, b, NP:T], ps[:, 2, 0:NS], ACT.Copy).then_inc(y_copied, 1)

        @block.vector
        def _(dve):
            steps = [0]

            def step(ins):
                ins.then_inc(dv, 1)
                steps[0] += 1
                dve.wait_ge(dv, steps[0])

            def tt(out, a, b, op=ALU.mult):
                step(dve.tensor_tensor(out, a, b, op))

            def tsc(out, a, s1, s2, op0, op1=ALU.bypass):
                step(dve.tensor_scalar(out, a, s1, s2, op0, op1))

            def stt(out, a, s, b, op0, op1):
                step(dve.scalar_tensor_tensor(out=out, in0=a, scalar=s, in1=b, op0=op0, op1=op1))

            def rounded(out, x, per):
                tsc(out, x, 1.0 / per, 12582912.0, ALU.mult, ALU.add)
                tsc(out, out, -12582912.0, None, ALU.add)

            def exp_parts(x, em, two_k, n, tmp):
                rounded(n, x, math.log(2.0))
                tsc(n, n, 126.0, -126.0, ALU.min, ALU.max)
                stt(tmp, n, -0.693359375, x, ALU.mult, ALU.add)
                stt(tmp, n, 2.12194440e-4, tmp, ALU.mult, ALU.add)
                tsc(tmp, tmp, 40.0, -40.0, ALU.min, ALU.max)
                tsc(em, tmp, 1 / 5040.0, 1 / 720.0, ALU.mult, ALU.add)
                for c in (1 / 120.0, 1 / 24.0, 1 / 6.0, 0.5, 1.0):
                    tt(em, em, tmp)
                    tsc(em, em, c, None, ALU.add)
                tt(em, em, tmp)
                tsc(ki[:, :], n, 127.0, None, ALU.add)
                step(dve.tensor_scalar(two_k.bitcast(I32), ki[:, :], 23, None, ALU.logical_shift_left))

            dve.wait_ge(lam_turned, 1)
            step(dve.tensor_copy(lr[:, :], ps[:, 0, 0:NG]))
            step(dve.tensor_copy(li[:, :], ps[:, 0, NG:2 * NG]))
            dve.wait_ge(par_in, 16 * 8)
            exp_parts(dt[:, :], R(0), R(1), R(2), R(3))
            stt(dt[:, :], R(0), 1.0, R(1), ALU.add, ALU.mult)
            tt(R(4), lr[:, :], dt[:, :])
            tt(R(5), li[:, :], dt[:, :])
            rounded(R(7), R(5), 2 * math.pi)
            stt(R(6), R(7), -6.28125, R(5), ALU.mult, ALU.add)
            stt(R(6), R(7), -0.0019350051879882812, R(6), ALU.mult, ALU.add)
            stt(R(6), R(7), -3.019916e-07, R(6), ALU.mult, ALU.add)
            dve.tensor_scalar(R(6), R(6), 3.141592, -3.141592, ALU.min, ALU.max).then_inc(dve_par, 1)
            exp_parts(R(4), R(0), R(1), R(2), R(3))
            dve.wait_ge(act_par, 2)
            tt(R(9), R(9), R(9))
            tsc(R(9), R(9), -2.0, None, ALU.mult)
            tsc(R(10), R(9), 1.0, None, ALU.add)
            tsc(R(11), R(1), -1.0, None, ALU.add)
            tt(R(12), R(0), R(1))
            tt(R(12), R(12), R(11), ALU.add)
            tsc(R(13), R(12), 1.0, None, ALU.add)
            tt(R(14), R(12), R(10))
            tt(R(14), R(14), R(9), ALU.add)
            tt(R(15), R(13), R(8))
            tt(R(0), lr[:, :], lr[:, :])
            tt(R(1), li[:, :], li[:, :])
            tt(R(0), R(0), R(1), ALU.add)
            step(dve.reciprocal(R(1), R(0)))
            tt(R(2), R(14), lr[:, :])
            tt(R(3), R(15), li[:, :])
            tt(R(2), R(2), R(3), ALU.add)
            tt(R(2), R(2), R(1))
            tt(R(3), R(15), lr[:, :])
            tt(R(4), R(14), li[:, :])
            tt(R(3), R(3), R(4), ALU.subtract)
            tt(R(3), R(3), R(1))
            tsc(R(3), R(3), sgn[:, 0:1], None, ALU.mult)
            dve.wait_ge(bc_in, 16 * 8)
            cr, ci = over(R(2), GC), over(R(3), GC)
            tt(bb_x[:, :, :], b_x[:, :, :], cr)
            tt(bt[:, :, :], b_s[:, :, :], ci)
            tt(bb_x[:, :, :], bb_x[:, :, :], bt[:, :, :], ALU.add)
            tt(bb_s[:, :, :], b_s[:, :, :], cr)
            tt(bt[:, :, :], b_x[:, :, :], ci)
            tt(bb_s[:, :, :], bb_s[:, :, :], bt[:, :, :], ALU.subtract)
            dve.wait_ge(c_turned, 1)
            for dst, bank in ((c_x, 1), (c_s, 2)):
                tsc(dst[:, :, :].rearrange("p g c -> p (g c)"), ps[:, bank, :], sgn[:, 0:1], -1.0, ALU.mult, ALU.mult)
            step(dve.memset(pr[:, :, 0:1], 1.0))
            step(dve.memset(pi[:, :, 0:1], 0.0))
            tsc(pr[:, :, 1:2], R(14).unsqueeze(2), 1.0, None, ALU.add)
            tsc(pi[:, :, 1:2], R(15).unsqueeze(2), sgn[:, 0:1], None, ALU.mult)

            def double(re, im, n, fr, fi, a, b):
                tt(a, re[:, :, 1:n + 1], fr)
                tt(b, im[:, :, 1:n + 1], fi)
                tt(re[:, :, n + 1:2 * n + 1], a, b, ALU.subtract)
                tt(a, im[:, :, 1:n + 1], fr)
                tt(b, re[:, :, 1:n + 1], fi)
                tt(im[:, :, n + 1:2 * n + 1], a, b, ALU.add)

            for n in (1, 2, 4):
                double(pr, pi, n, pr[:, :, n:n + 1].broadcast_to([P, NG, n]), pi[:, :, n:n + 1].broadcast_to([P, NG, n]),
                       t1[:, :, 0:n], t2[:, :, 0:n])
            for l in range(L):
                step(dve.tensor_copy(qr[:, :, l:l + 1], pr[:, :, L - 1 - l:L - l]))
                step(dve.tensor_copy(qi[:, :, l:l + 1], pi[:, :, L - 1 - l:L - l]))
            step(dve.tensor_copy(wr[:, :], R(10)))
            tsc(wi[:, :], R(8), sgn[:, 0:1], None, ALU.mult)
            step(dve.tensor_copy(rad[:, :], R(13)))
            for _ in range(3):
                tt(R(0), wr[:, :], wr[:, :])
                tt(R(1), wi[:, :], wi[:, :])
                tt(R(2), wr[:, :], wi[:, :])
                tt(wr[:, :], R(0), R(1), ALU.subtract)
                tsc(wi[:, :], R(2), 2.0, None, ALU.mult)
                tt(rad[:, :], rad[:, :], rad[:, :])
            for b in range(NBATCH):
                gs = slice(b * GB, (b + 1) * GB)
                if b:
                    dve.wait_ge(b_turned, b)
                    dve.wait_ge(y_done, b)
                tal = ta[:, :, 0:L, :]
                tt(bl[:, :, :, :], over(qr[:, gs, :], GC), mid(bb_x[:, gs, :], L))
                tt(tal, over(qi[:, gs, :], GC), mid(bb_s[:, gs, :], L))
                dve.tensor_tensor(bl[:, :, :, :], bl[:, :, :, :], tal, ALU.add).then_inc(bl_ready, 1)
                dve.wait_ge(bl_ready, b + 1)
                tt(cl[:, :, :, :], over(pr[:, gs, :], GC), mid(c_x[:, gs, :], L + 1))
                tt(ta[:, :, :, :], over(pi[:, gs, :], GC), mid(c_s[:, gs, :], L + 1))
                dve.tensor_tensor(cl[:, :, :, :], cl[:, :, :, :], ta[:, :, :, :], ALU.add).then_inc(cl_ready, 1)
                step(dve.memset(tc[:, :, 0:1], 1.0))
                step(dve.memset(ts[:, :, 0:1], 0.0))
                step(dve.tensor_copy(tc[:, :, 1:2], wr[:, gs].unsqueeze(2)))
                step(dve.tensor_copy(ts[:, :, 1:2], wi[:, gs].unsqueeze(2)))
                n = 1
                while n < NC - 1:
                    m = min(n, NC - 1 - n)
                    fr, fi = (a[:, :, n:n + 1].broadcast_to([P, GB, m]) for a in (tc, ts))
                    tt(z[:, :, 0:m], tc[:, :, 1:m + 1], fr)
                    tt(tb[:, :, 0:m], ts[:, :, 1:m + 1], fi)
                    tt(tc[:, :, n + 1:n + m + 1], z[:, :, 0:m], tb[:, :, 0:m], ALU.subtract)
                    tt(z[:, :, 0:m], ts[:, :, 1:m + 1], fr)
                    tt(tb[:, :, 0:m], tc[:, :, 1:m + 1], fi)
                    tt(ts[:, :, n + 1:n + m + 1], z[:, :, 0:m], tb[:, :, 0:m], ALU.add)
                    n += m
                dve.wait_ge(kt_copied, b + 1)
                tt(tb[0:GC, :, 0:GC], g.ident[0:GC, 0:GC].unsqueeze(1).broadcast_to([GC, GB, GC]), over(dsk[:, gs], GC))
                dve.tensor_tensor(kt[:, :, 0, :], kt[:, :, 0, :], tb[0:GC, :, 0:GC], ALU.add).then_inc(kt_ready, 1)
                dve.wait_ge(xin_copied, b + 1)
                tt(z[:, :, :], xin[:, :, 0:P], tc[:, :, :])
                dve.wait_ge(xs_done, b + 1)
                psx = psf[:, 2 * BANK:4 * BANK].rearrange("p (g k) -> p g k", g=GB)
                tt(tb[:, :, :], psx, ts[:, :, :])
                tt(z[:, :, :], z[:, :, :], tb[:, :, :], ALU.subtract)
                for q in range(GB):
                    r = rad[:, b * GB + q:b * GB + q + 1].broadcast_to([P, NC])
                    ins = dve.tensor_tensor_scan(z[:, q, :], r, z[:, q, :], 0.0, ALU.mult, ALU.add)
                ins.then_inc(z_ready, 1)
                dve.wait_ge(z_ready, b + 1)
                if b:
                    dve.wait_ge(last_turned, b)
                step(dve.memset(xall[:, :, 0:1], 0.0))
                tt(xall[:, :, 1:NC + 1], z[:, :, :], tc[:, :, :])
                dve.wait_ge(zs_done, b + 1)
                psz = psf[:, 0:2 * BANK].rearrange("p (g k) -> p g k", g=GB)
                tt(tb[:, :, :], psz, ts[:, :, :])
                dve.tensor_tensor(xall[:, :, 1:NC + 1], xall[:, :, 1:NC + 1], tb[:, :, :], ALU.add).then_inc(x_ready, 1)
                dve.wait_ge(st_copied, b + 1)
                tbs = tb[:, 0, 0:NS * GB].rearrange("p (b g) -> p b g", g=GB)
                tt(x1[:, :, :], x0[:, :, :], pr[:, gs, 1].unsqueeze(1).broadcast_to([P, NS, GB]))
                tt(tbs, x0s[:, :, :], pi[:, gs, 1].unsqueeze(1).broadcast_to([P, NS, GB]))
                tt(x1[:, :, :], x1[:, :, :], tbs, ALU.add)
                dve.tensor_tensor(x1[:, :, :], x1[:, :, :], xin[:, :, P:P + NS].rearrange("p g b -> p b g"),
                                  ALU.add).then_inc(x1_ready, 1)
                dve.wait_ge(x1_ready, b + 1)

        @block.tensor
        def _(pe):
            pe.wait_ge(par_in, 16 * 8)
            for q in range(2):
                mm = pe.transpose(ps[:, 0, q * NG:(q + 1) * NG], lam_st[:, q, :, :].rearrange("g a p -> g (a p)"),
                                  g.ident[0:NG, 0:NG])
            mm.then_inc(lam_turned, 1)
            pe.wait_ge(bc_in, 16 * 8)
            for q in range(2):
                for a in range(4):
                    mm = pe.transpose(ps[:, 1 + q, a * P:(a + 1) * P], c_st[:, q, a, :], g.ident[:, :])
            mm.then_inc(c_turned, 1)
            for b in range(NBATCH):
                pe.wait_ge(u_grouped, b + 1)
                if b == 0:
                    pe.wait_ge(zeroed, 2)
                    pe.wait_ge(bl_ready, 1)
                else:
                    pe.wait_ge(y_copied, b)
                for q in range(GB):
                    pe.transpose(psf[:, q * P:(q + 1) * P], u_grp[:, q, :, :].rearrange("p l c -> p (l c)"),
                                 g.ident[:, :])
                for q in range(GB):
                    mm = pe.transpose(ps[:, 2, q * NS:(q + 1) * NS],
                                      us_grp[:, q, :, :].rearrange("p l c -> p (l c)"), g.ident[0:NS, 0:NS])
                mm.then_inc(u_turned, 1)
                pe.wait_ge(st_in, 16 * 32 * (b + 1))
                if b:
                    pe.wait_ge(z_ready, b)
                for q in range(2):
                    o = 3 * BANK + q * GB * NS
                    mm = pe.transpose(psf[:, o:o + GB * NS], st_x[:, q, :], g.ident[0:GB * NS, 0:GB * NS])
                mm.then_inc(st_turned, 1)
                pe.wait_ge(bl_ready, b + 1)
                if b:
                    pe.wait_ge(y_gelu, b)
                for q in range(GB):
                    o = 4 * BANK + q * P
                    mm = pe.transpose(psf[:, o:o + P], bl[:, q, :, :].rearrange("p l c -> p (l c)"), g.ident[:, :])
                mm.then_inc(b_turned, 1)
                pe.wait_ge(cl_ready, b + 1)
                if b:
                    pe.wait_ge(last_copied, b)
                for q in range(GB):
                    o = 6 * BANK + q * P
                    mm = pe.matmul(psf[0:GC, o:o + P], bb_x[:, b * GB + q, :],
                                   cl[:, q, 0:L, :].rearrange("p l c -> p (l c)"), start=True, stop=True)
                mm.then_inc(kt_done, 1)
                pe.wait_ge(b_copied, b + 1)
                pe.wait_ge(u_copied, b + 1)
                for q in range(GB):
                    pe.matmul(psf[:, q * P:(q + 1) * P], bst[:, q, :], u[:, q, 0:P], start=True, stop=True)
                for q in range(GB):
                    mm = pe.matmul(ps[:, 2, q * NS:(q + 1) * NS], bst[:, q, :], u[:, q, P:P + NS], start=True, stop=True)
                mm.then_inc(xin_done, 1)
                pe.wait_ge(xin_copied, b + 1)
                pe.wait_ge(st_copied, b + 1)
                for h in range(2):
                    mm = pe.matmul(ps[:, 2 + h, :], swap[:, :], xin[:, 4 * h:4 * h + 4, 0:P], start=True, stop=True)
                mm.then_inc(xs_done, 1)
                pe.wait_ge(z_ready, b + 1)
                for h in range(2):
                    mm = pe.matmul(ps[:, h, :], swap[:, :], z[:, 4 * h:4 * h + 4, :], start=True, stop=True)
                mm.then_inc(zs_done, 1)
                pe.wait_ge(x_ready, b + 1)
                pe.wait_ge(mi_in, 16 * L * (b + 1))
                pe.wait_ge(kt_copied, b + 1)
                for q in range(GB):
                    o = 4 * BANK + q * P
                    pe.matmul(psf[:, o:o + P], u[:, q, 0:P], mi[:, q, :], start=True, stop=False)
                    pe.matmul(psf[:, o:o + P], xall[:, q, 0:NC], cl[:, q, 1:L + 1, :].rearrange("p l c -> p (l c)"),
                              start=False, stop=True)
                for q in range(GB):
                    cs = slice(q * GC, (q + 1) * GC)
                    pe.matmul(ps[0:NS, 6, cs], u[:, q, P:P + NS], mi[:, q, P - GC:P], start=True, stop=False)
                    mm = pe.matmul(ps[0:NS, 6, cs], x0[:, :, q], cl[:, q, 1, :], start=False, stop=True)
                mm.then_inc(y_done, 1)
                pe.wait_ge(x1_ready, b + 1)
                pe.transpose(ps[0:GB, 7, 0:P], xall[:, :, NC], g.ident[:, :])
                pe.transpose(ps[0:GB * NS, 7, P:2 * P], x1[:, :, :].rearrange("p b g -> p (b g)"),
                             g.ident[:, :]).then_inc(last_turned, 1)
                pe.wait_ge(y_gelu, b + 1)
                for l in range(L):
                    pe.transpose(psf[:, l * P:(l + 1) * P], y[:, l, :], g.ident[:, :])
                pe.transpose(ps[:, 2, 0:NS], ys[:, :], g.ident[0:NS, 0:NS]).then_inc(y_turned, 1)


DIST = 383


def bucket_of_distance():
    exact = NB // 2

    def bucket(n):
        return n if n < exact else min(NB - 1, exact + int(math.log(n / exact) / math.log(128 / exact) * (NB - exact)))
    return [bucket(max(n, 0)) for n in range(1024)]


def phase_glu(nc, g):
    with ExitStack() as ctx:
        sb = lambda n, s, d=F32: ctx.enter_context(nc.sbuf_tensor("l_" + n, s, d))
        ps, sem = g.ps, lambda n: g.sem("l_" + n)
        wst = sb("wst", [P, 4, SW])
        wh, wl = sb("wh", [P, 4, SW], F32R), sb("wl", [P, 4, SW], F32R)
        xh, xl = sb("xh", [P, 4, T], F32R), sb("xl", [P, 4, T], F32R)
        bias = sb("bias", [P, 4])
        sg = sb("sg", [P, 2, T])
        w_in, b_in, w_hi, w_lo, x_hi, x_lo, done, sig, prod, y_hi, y_lo = (
            sem(n) for n in ("w_in", "b_in", "w_hi", "w_lo", "x_hi", "x_lo", "done", "sig", "prod", "y_hi", "y_lo"))
        block = ctx.enter_context(nc.Block())

        @block.sync
        def _(sp):
            sp.dma_start(wst[:, :, :], g.w_glu.rearrange("(k p) n -> p k n", p=P)).then_inc(w_in, 16)
            sp.dma_start(bias[:, :], g.b_glu.rearrange("(m p) -> p m", p=P), allow_slow_non_contiguous=True).then_inc(b_in, 16)

        @block.scalar
        def _(act):
            act.activation(xh[:, :, :], g.gT[:, :, :], ACT.Copy).then_inc(x_hi, 1)
            act.wait_ge(w_in, 16)
            act.activation(wh[:, :, :], wst[:, :, :], ACT.Copy).then_inc(w_hi, 1)
            act.wait_ge(b_in, 16)
            for m in range(4):
                act.wait_ge(done, m + 1)
                if m >= 2:
                    act.wait_ge(prod, m - 1)
                act.activation(as_thirds(sg[:, m % 2, :]), thirds(ps, m % 2), ACT.Sigmoid, bias=bias[:, m:m + 1]).then_inc(sig, 1)
                act.wait_ge(prod, m + 1)
                act.activation(g.ys_h[:, m, :], sg[:, m % 2, :], ACT.Copy).then_inc(y_hi, 1)

        @block.vector
        def _(dve):
            dve.wait_ge(x_hi, 1)
            dve.tensor_tensor(xl[:, :, :], g.gT[:, :, :], xh[:, :, :].bitcast(F32), ALU.subtract).then_inc(x_lo, 1)
            dve.wait_ge(w_hi, 1)
            dve.tensor_tensor(wl[:, :, :], wst[:, :, :], wh[:, :, :].bitcast(F32), ALU.subtract).then_inc(w_lo, 1)
            for m in range(4):
                dve.wait_ge(sig, m + 1)
                dve.tensor_tensor(sg[:, m % 2, :], sg[:, m % 2, :], g.gT[:, m, :], ALU.mult).then_inc(prod, 1)
                dve.wait_ge(y_hi, m + 1)
                dve.tensor_tensor(g.ys_l[:, m, :], sg[:, m % 2, :], g.ys_h[:, m, :].bitcast(F32), ALU.subtract).then_inc(y_lo, 1)

        @block.tensor
        def _(pe):
            pe.wait_ge(w_lo, 1)
            pe.wait_ge(x_lo, 1)
            for m in range(4):
                if m >= 2:
                    pe.wait_ge(sig, m - 1)
                cs = slice(m * P, (m + 1) * P)
                project(pe, ps, m % 2, wh[:, :, cs], wl[:, :, cs], xh, xl, 4).then_inc(done, 1)


def phase_attention(nc, g):
    with ExitStack() as ctx:
        sb = lambda n, s, d=F32: ctx.enter_context(nc.sbuf_tensor("t_" + n, s, d))
        ps, sem = g.ps, lambda n: g.sem("t_" + n)
        psf = ps[:, :, :].rearrange("p b c -> p (b c)")
        NLG = 4
        vv = sb("v", [P, NT, AW])
        nci = sb("nci", [P, P])
        mask01 = sb("mask01", [P, P + 2 * P])
        rel_t = sb("rel", [NB, H])
        rel_rep = sb("rel_rep", [NB, H, P])
        onehot = sb("onehot", [NB, DIST])
        b31 = sb("b31", [P, H])
        drow = sb("drow", [P, 2, DIST])
        t8h, t8l = sb("t8h", [P, H, 2 * P], F32R), sb("t8l", [P, H, 2 * P], F32R)
        lg = sb("lg", [P, NLG, NP])
        t8 = lg[:, 0:2, :].rearrange("p s (h c) -> p (s h) c", c=2 * P)
        pt = sb("pt", [P, 2, NP])
        ident_r = sb("ident_r", [P, P], F32R)
        m8 = sb("m8", [P, 8])
        mx, nmx, den, rden = (sb(n, [P, NT * H]) for n in ("mx", "nmx", "den", "rden"))

        v_in, c_in, rel_ready, d_done, d_copied, d_out, t_in, t_ready, m_ready = (
            sem(n) for n in ("v_in", "c_in", "rel_ready", "d_done", "d_copied", "d_out", "t_in", "t_ready", "m_ready"))
        s_done, l_done, nmx_done, e_done, r_done, p_done, turned, pt_done, y_done, yh_done, yl_done = (
            sem(n) for n in ("s_done", "l_done", "nmx_done", "e_done", "r_done", "p_done", "turned", "pt_done", "y_done",
                             "yh_done", "yl_done"))
        th_done, tl_done, late, tab_in, kx_in = (sem(n) for n in ("th_done", "tl_done", "late", "tab_in", "kx_in"))
        block = ctx.enter_context(nc.Block())
        steps = [(i, h) for i in range(NT) for h in range(H)]
        NSTEP = len(steps)
        masks = [mask01[:, 0:P], mask01[:, P:3 * P]] + list(g.mask)

        @block.sync
        def _(sp):
            sp.dma_start(g.table[:, :], g.page_table.rearrange("b n -> (b n)").unsqueeze(0)).then_inc(tab_in, 16)
            sp.dma_start(nci[:, :], g.c_not_causal).then_inc(c_in, 16)
            sp.dma_start(rel_t[:, :], g.rel_bias).then_inc(c_in, 16)
            sp.dma_start(onehot[:, :], g.c_onehot).then_inc(c_in, 16)
            sp.dma_start(b31[:, :], g.rel_bias[NB - 1, :].partition_broadcast(P)).then_inc(c_in, 16)
            sp.dma_start(vv[:, :, :], g.v_prompt.rearrange("(i p) c -> p i c", p=P)).then_inc(v_in, 16)
            for h in range(H):
                sp.wait_ge(d_copied, h + 1)
                sp.dma_start(g.d_bias[h, :].rearrange("(p m) -> p m", m=DIST), drow[:, h % 2, :]).then_inc(d_out, 16)
                sp.wait_ge(d_out, 16 * (h + 1))
                src = g.d_bias[h, P - 1:P - 1 + P * (DIST - 1)].rearrange("(p m) -> p m", m=DIST - 1)[:, 0:2 * P]
                sp.dma_start(t8[:, h, :], src).then_inc(t_in, 16)
            sp.wait_ge(tab_in, 16)
            for b in range(NS):
                for q in range(2):
                    page = sp.value_load(g.table[0:1, 2 * b + q:2 * b + q + 1], min_val=0, max_val=g.cache_k.shape[0] - 1)
                    sp.dma_start(g.kx[:, b, q, :], g.cache_kidx[bass.ds(page, 1), :, :].rearrange(
                        "a p c -> p (a c)")).then_inc(kx_in, 16)
            sp.wait_ge(kx_in, 16 * 2 * NS)

        @block.scalar
        def _(act):
            for h in range(H):
                act.wait_ge(d_done, h + 1)
                if h >= 2:
                    act.wait_ge(d_out, 16 * (h - 1))
                act.activation(drow[:, h % 2, :], ps[:, h % 2, 0:DIST], ACT.Copy, scale=8.0).then_inc(d_copied, 1)
            act.activation(ident_r[:, :], g.ident[:, :], ACT.Copy)
            act.wait_ge(t_ready, 1)
            act.activation(t8h[:, :, :], t8[:, :, :], ACT.Copy).then_inc(th_done, 1)

            def probs(n):
                i = steps[n][0]
                act.wait_ge(nmx_done, n + 1)
                act.activation(lg[:, n % NLG, 0:(i + 1) * P], lg[:, n % NLG, 0:(i + 1) * P], ACT.Exp,
                               bias=nmx[:, n:n + 1], accum_out=den[:, n:n + 1]).then_inc(e_done, 1)

            def pt_copy(n):
                w = (steps[n][0] + 1) * P
                act.wait_ge(turned, n + 1)
                if n >= 2:
                    act.wait_ge(y_done, n - 1)
                act.activation(pt[:, n % 2, 0:w], psf[:, 4 * BANK:4 * BANK + w], ACT.Copy).then_inc(pt_done, 1)

            def y_high(n):
                i, h = steps[n]
                act.wait_ge(y_done, n + 1)
                act.activation(g.ya_h[:, h // 2, i * P:(i + 1) * P], ps[:, 6 + (n // 2) % 2, 0:P], ACT.Copy).then_inc(yh_done, 1)

            for n in range(NSTEP + 3):
                if n < NSTEP:
                    probs(n)
                if 2 <= n < NSTEP + 2:
                    pt_copy(n - 2)
                if n >= 3 and n % 2 == 0:
                    y_high(n - 3)
            assert (NSTEP + 2) % 2 == 0

        @block.vector
        def _(dve):
            dve.wait_ge(c_in, 64)
            dve.tensor_copy(rel_rep[:, :, :], over(rel_t[:, :], P)).then_inc(rel_ready, 1)
            dve.memset(mask01[:, P:2 * P], 0.0)
            dve.tensor_scalar(mask01[:, 0:P], nci[:, :], HIDE, None, ALU.mult)
            dve.tensor_scalar(mask01[:, 2 * P:3 * P], nci[:, :], HIDE, None, ALU.mult).then_inc(m_ready, 1)
            dve.tensor_scalar(b31[:, :], b31[:, :], 8.0, None, ALU.mult).then_inc(m_ready, 1)
            dve.wait_ge(m_ready, 2)
            dve.wait_ge(t_in, 16 * H)
            dve.tensor_tensor(t8[:, :, :], t8[:, :, :], over(b31[:, :], 2 * P), ALU.subtract).then_inc(t_ready, 1)
            dve.wait_ge(th_done, 1)
            dve.tensor_tensor(t8l[:, :, :], t8[:, :, :], t8h[:, :, :].bitcast(F32), ALU.subtract).then_inc(tl_done, 1)

            def logits(n):
                i = steps[n][0]
                w = (i + 1) * P
                dve.wait_ge(s_done, n + 1)
                if n >= NLG:
                    dve.wait_ge(turned, n - NLG + 1)
                dve.tensor_tensor_reduce(out=lg[:, n % NLG, 0:w], in0=psf[:, (n % 2) * 1024:(n % 2) * 1024 + w],
                                         in1=masks[i], scale=0.125, scalar=-3.0e38, op0=ALU.add, op1=ALU.max,
                                         accum_out=mx[:, n:n + 1]).then_inc(l_done, 1)
                dve.wait_ge(l_done, n + 1)
                dve.tensor_scalar(nmx[:, n:n + 1], mx[:, n:n + 1], -1.0, None, ALU.mult).then_inc(nmx_done, 1)

            def scale(n):
                w = (steps[n][0] + 1) * P
                dve.wait_ge(e_done, n + 1)
                dve.reciprocal(rden[:, n:n + 1], den[:, n:n + 1]).then_inc(r_done, 1)
                dve.wait_ge(r_done, n + 1)
                dve.tensor_scalar(lg[:, n % NLG, 0:w], lg[:, n % NLG, 0:w], rden[:, n:n + 1], None,
                                  ALU.mult).then_inc(p_done, 1)

            def y_low(n):
                i, h = steps[n]
                dve.wait_ge(yh_done, n // 2 + 1)
                o = g.ya_h[:, h // 2, i * P:(i + 1) * P]
                dve.tensor_tensor(g.ya_l[:, h // 2, i * P:(i + 1) * P], ps[:, 6 + (n // 2) % 2, 0:P], o.bitcast(F32),
                                  ALU.subtract).then_inc(yl_done, 1)

            def late_round(k):
                sc = g.mask[NT - 3]
                dve.max(m8[:, :], sc).then_inc(late, 1)
                dve.wait_ge(late, 2 * k + 1)
                dve.match_replace(out=sc, in_to_replace=m8[:, :], in_values=sc, imm_value=TAKEN).then_inc(late, 1)
                dve.wait_ge(late, 2 * k + 2)
                if k == LATE_ROUNDS - 1:
                    dve.tensor_scalar(sc, sc, -3.2e38, HIDE, ALU.is_gt, ALU.mult).then_inc(late, 1)
                    dve.wait_ge(late, 2 * k + 3)

            for n in range(NSTEP + 4):
                if n < NSTEP:
                    logits(n)
                if 1 <= n <= NSTEP:
                    scale(n - 1)
                if n >= 4 and n % 2 == 1:
                    y_low(n - 4)
                k = n - (NSTEP - H - 2 * LATE_ROUNDS)
                if k >= 0 and k % 2 == 0 and k // 2 < LATE_ROUNDS:
                    late_round(k // 2)

        @block.tensor
        def _(pe):
            pe.wait_ge(rel_ready, 1)
            for h in range(H):
                if h >= 2:
                    pe.wait_ge(d_copied, h - 1)
                pe.matmul(ps[:, h % 2, 0:DIST], rel_rep[:, h, :], onehot[:, :], start=True, stop=True).then_inc(d_done, 1)
            pe.wait_ge(d_copied, H)
            pe.wait_ge(th_done, 1)
            pe.wait_ge(tl_done, 1)
            pe.wait_ge(m_ready, 2)
            pe.wait_ge(v_in, 16)

            def scores(n):
                i, h = steps[n]
                w, r, o = (i + 1) * P, (h % 2) * HD, (n % 2) * 1024
                if n >= 2:
                    pe.wait_ge(l_done, n - 1)
                for c in range(0, w, BANK):
                    m = min(BANK, w - c)
                    pe.matmul(psf[:, o + c:o + c + m], g.qT[r:r + HD, h // 2, i * P:(i + 1) * P],
                              g.kT[r:r + HD, h // 2, c:c + m], start=True, stop=False, skip_group_check=True)
                cuts = [(0, 1)] if i == 0 else [(i - 1, i), (i, i + 1)] if i * P % BANK == 0 else [(i - 1, i + 1)]
                for a, b in cuts:
                    ts = slice((a - i + 1) * P, (b - i + 1) * P)
                    for t in (t8h, t8l):
                        mm = pe.matmul(psf[:, o + a * P:o + b * P], ident_r[:, :], t[:, h, ts],
                                       start=False, stop=t is t8l, skip_group_check=True)
                mm.then_inc(s_done, 1)

            def turn(n):
                i = steps[n][0]
                pe.wait_ge(p_done, n + 1)
                if n:
                    pe.wait_ge(pt_done, n)
                for j in range(i + 1):
                    mm = pe.transpose(psf[:, 4 * BANK + j * P:4 * BANK + (j + 1) * P], lg[:, n % NLG, j * P:(j + 1) * P],
                                      g.ident[:, :])
                mm.then_inc(turned, 1)

            def weigh(n):
                i, h = steps[n]
                pe.wait_ge(pt_done, n + 1)
                if n >= 4 and h % 2 == 0:
                    pe.wait_ge(yl_done, n // 2 - 1)
                r = (h % 2) * HD
                for j in range(i + 1):
                    mm = pe.matmul(ps[r:r + HD, 6 + (n // 2) % 2, 0:P], vv[:, j, h * HD:(h + 1) * HD],
                                   pt[:, n % 2, j * P:(j + 1) * P], start=(j == 0), stop=(j == i), skip_group_check=True)
                mm.then_inc(y_done, 1)

            for n in range(NSTEP + 3):
                if n < NSTEP:
                    scores(n)
                if 2 <= n < NSTEP + 2:
                    turn(n - 2)
                if n >= 3:
                    weigh(n - 3)


def phase_sample(nc, g):
    BH = NS * H
    with ExitStack() as ctx:
        sb = lambda n, s, d=F32: ctx.enter_context(nc.sbuf_tensor("a_" + n, s, d))
        ps, sem = g.ps, lambda n: g.sem("a_" + n)
        psf = ps[:, :, :].rearrange("p b c -> p (b c)")
        kk, vv = sb("k", [P, 2, 2, AW]), sb("v", [P, NS, 2, AW])
        vs = sb("vs", [NS, AW])
        own = sb("own", [NS, NS * JH + BH])
        ownT32, ownT64 = sb("ownT32", [NS * JH, NS]), sb("ownT64", [BH, NS])
        jsel = sb("jsel", [P, NS * JH])
        rel_t, onehot = sb("rel", [NB, H]), sb("onehot", [NB, SK])
        rel_rep = sb("rel_rep", [NB, NS, H])
        bias = sb("bias", [BH, SK])
        wcol, wtmp = sb("wcol", [NS * JH, 1]), sb("wtmp", [NS * JH, NS])
        qm = sb("qm", [ID, NS, NS * JH])
        kxT = sb("kxT", [ID, 2, SK])
        sc32 = sb("sc32", [NS * JH, SK])
        sc = sb("sc", [NS, SK])
        m8 = sb("m8", [NS, 8])
        qb = sb("qb", [P, 4, NS, BH])
        kTb = sb("kT", [P, 2, 4, SK])
        lg, dmsk = sb("lg", [BH, SK]), sb("dmsk", [BH, SK])
        mx, nmx, den, rden = (sb(n, [BH, 1]) for n in ("mx", "nmx", "den", "rden"))
        pself = sb("pself", [BH, NS])
        hsel = sb("hsel", [BH, H])
        pT = sb("pT", [P, 2, NS, BH])
        psT = sb("psT", [NS, BH])
        yb = sb("yb", [BH, AW])
        yf = sb("yf", [P, 4, NS])

        c_in, vs_in = (sem(n) for n in ("c_in", "vs_in"))
        v_in = [sem(f"v_in{b}") for b in range(NS)]
        k_in = [sem(f"k_in{i}") for i in range(2)]
        zero, setup, w_done, w_ready, kx_turned, kx_copied, sc_done, sc_ready, sum_done, sel = (
            sem(n) for n in ("zero", "setup", "w_done", "w_ready", "kx_turned", "kx_copied", "sc_done", "sc_ready",
                             "sum_done", "sel"))
        k_turned, k_copied, lg_done, msk_done, msk_ready, bias_done, bias_ready, exp_done, p_ready, p_turned, p_copied, y_done, y_own, y_summed = (
            sem(n) for n in ("k_turned", "k_copied", "lg_done", "msk_done", "msk_ready", "bias_done", "bias_ready",
                             "exp_done", "p_ready", "p_turned", "p_copied", "y_done", "y_own", "y_summed"))
        dv, nmx_done, kc = sem("dve_step"), sem("nmx_done"), sem("kcol")
        block = ctx.enter_context(nc.Block())

        @block.sync
        def _(sp):
            for n, (dst, src) in enumerate(((own[:, :], g.c_own), (ownT32[:, :], g.c_own32), (ownT64[:, :], g.c_own64),
                                            (jsel[ID:ID + JH, :], g.c_jsel), (rel_t[:, :], g.rel_bias),
                                            (onehot[:, :], g.c_onehot_s), (hsel[:, :], g.c_headsel))):
                sp.dma_start(dst, src).then_inc(c_in, 16)
            sp.dma_start(vs[:, :], g.v_sample).then_inc(vs_in, 16)
            pages = [sp.value_load(g.table[0:1, n:n + 1], min_val=0, max_val=g.cache_k.shape[0] - 1) for n in range(2 * NS)]
            for b in range(NS):
                if b >= 2:
                    sp.wait_ge(k_turned, 2 * (b - 1))
                for q in range(2):
                    pg = bass.ds(pages[2 * b + q], 1)
                    sp.dma_start(kk[:, b % 2, q, :], g.cache_k[pg, :, :].rearrange("a p c -> p (a c)")).then_inc(k_in[b % 2], 16)

        @block.gpsimd
        def _(pool):
            pool.memset(qm[:, :, :], 0.0).then_inc(zero, 1)
            pool.memset(qb[:, :, :, :], 0.0).then_inc(zero, 1)
            pool.memset(pT[:, :, :, :], 0.0).then_inc(zero, 1)
            pages = [pool.value_load(g.table[0:1, n:n + 1], min_val=0, max_val=g.cache_v.shape[0] - 1) for n in range(2 * NS)]
            for b in range(NS):
                for q in range(2):
                    pool.dma_start(vv[:, b, q, :], g.cache_v[bass.ds(pages[2 * b + q], 1), :, :].rearrange(
                        "a p c -> p (a c)")).then_inc(v_in[b], 16)

        @block.scalar
        def _(act):
            for b in range(NS):
                act.wait_ge(kx_turned, b + 1)
                if b >= 2:
                    act.wait_ge(sc_done, b - 1)
                act.activation(kxT[:, b % 2, 0:PAST], ps[0:ID, b % 2, 0:PAST], ACT.Copy)
                act.activation(kxT[:, b % 2, PAST:SK], g.kwT[0:ID, NP + b:NP + b + 1], ACT.Copy).then_inc(kx_copied, 1)
            for b in range(NS):
                act.wait_ge(k_turned, 2 * (b + 1))
                if b >= 2:
                    act.wait_ge(lg_done, b - 1)
                o = (2 + 2 * (b % 2)) * BANK
                act.activation(kTb[:, b % 2, :, 0:PAST], psf[:, o:o + 4 * PAST].rearrange("p (m s) -> p m s", m=4), ACT.Copy)
                act.activation(kTb[:, b % 2, :, PAST:SK], g.kT[:, :, NP + b:NP + b + 1], ACT.Copy).then_inc(k_copied, 1)
            act.wait_ge(nmx_done, 1)
            act.activation(lg[:, :], lg[:, :], ACT.Exp, bias=nmx[:, 0:1], accum_out=den[:, 0:1]).then_inc(exp_done, 1)
            act.wait_ge(p_turned, 1)
            act.wait_ge(zero, 3)
            for q in range(2):
                for b in range(NS):
                    hs = slice(b * H, (b + 1) * H)
                    act.activation(pT[:, q, b, hs], ps[:, 0, q * BH + b * H:q * BH + (b + 1) * H], ACT.Copy)
            act.activation(psT[:, :], ps[0:NS, 0, 2 * BH:3 * BH], ACT.Copy).then_inc(p_copied, 1)

        @block.vector
        def _(dve):
            steps = [0]

            def step(ins):
                ins.then_inc(dv, 1)
                steps[0] += 1
                dve.wait_ge(dv, steps[0])

            dve.wait_ge(zero, 2)
            qmf = qm[:, :, :].rearrange("p b n -> p (b n)")
            for j in range(JH):
                r = (j % 2) * ID
                dve.tensor_copy(qmf[:, j:j + (NS * JH + JH) * (NS - 1) + 1:NS * JH + JH], g.qiT[r:r + ID, j // 2, NP:T])
            for h in range(H):
                r = (h % 2) * HD
                q = qb[r:r + HD, h // 2, :, :].rearrange("p b n -> p (b n)")
                ins = dve.tensor_copy(q[:, h:h + (BH + H) * (NS - 1) + 1:BH + H], g.qT[r:r + HD, h // 2, NP:T])
            dve.wait_ge(c_in, 16 * 7)
            dve.tensor_copy(rel_rep[:, :, :], rel_t[:, :].unsqueeze(1).broadcast_to([NB, NS, H])).then_inc(setup, 1)
            dve.wait_ge(w_done, 1)
            step(dve.tensor_tensor(wtmp[:, :], ps[0:NS * JH, 7, 0:NS], ownT32[:, :], ALU.mult))
            step(dve.tensor_reduce(wcol[:, :], wtmp[:, :], AX.X, ALU.add))
            dve.wait_ge(bias_done, 1)
            dve.tensor_copy(bias[:, :], ps[0:BH, 6, 0:SK]).then_inc(bias_ready, 1)
            dve.wait_ge(sc_done, NS)
            dve.tensor_scalar(sc32[:, :], ps[0:NS * JH, 7, 0:SK], 0.0, wcol[:, 0:1], ALU.max, ALU.mult).then_inc(sc_ready, 1)
            dve.wait_ge(sum_done, 1)
            step(dve.tensor_copy(sc[:, :], ps[0:NS, 6, 0:SK]))
            for _ in range(STOPK // 8):
                step(dve.max(m8[:, :], sc[:, :]))
                step(dve.match_replace(out=sc[:, :], in_to_replace=m8[:, :], in_values=sc[:, :], imm_value=TAKEN))
            dve.tensor_scalar(sc[:, :], sc[:, :], -3.2e38, HIDE, ALU.is_gt, ALU.mult).then_inc(sel, 1)
            dve.wait_ge(msk_done, 1)
            step(dve.tensor_tensor(dmsk[:, :], ps[0:BH, 6, 0:SK], bias[:, :], ALU.add))
            dve.wait_ge(lg_done, NS)
            step(dve.scalar_tensor_tensor(out=lg[:, :], in0=ps[0:BH, 7, 0:SK], scalar=0.125, in1=dmsk[:, :],
                                          op0=ALU.mult, op1=ALU.add))
            step(dve.tensor_reduce(mx[:, :], lg[:, :], AX.X, ALU.max))
            dve.tensor_scalar(nmx[:, :], mx[:, :], -1.0, None, ALU.mult).then_inc(nmx_done, 1)
            dve.wait_ge(exp_done, 1)
            step(dve.reciprocal(rden[:, :], den[:, :]))
            step(dve.tensor_scalar(lg[:, :], lg[:, :], rden[:, 0:1], None, ALU.mult))
            dve.tensor_scalar(pself[:, :], ownT64[:, :], lg[:, PAST:SK], None, ALU.mult).then_inc(p_ready, 1)
            dve.wait_ge(y_done, 1)
            dve.tensor_tensor(yb[:, :].rearrange("p (h c) -> p h c", h=H), ps[0:BH, 1, :].rearrange("p (h c) -> p h c", h=H),
                              over(hsel[:, :], HD), ALU.mult).then_inc(y_own, 1)
            dve.wait_ge(y_summed, 1)
            step(dve.tensor_copy(yf[:, :, :], ps[:, 0, 0:4 * NS].rearrange("p (m b) -> p m b", m=4)))
            step(dve.tensor_copy(g.ya_h[:, :, NP:T], yf[:, :, :]))
            step(dve.tensor_tensor(g.ya_l[:, :, NP:T], yf[:, :, :], g.ya_h[:, :, NP:T].bitcast(F32), ALU.subtract))

        @block.tensor
        def _(pe):
            pe.wait_ge(setup, 1)
            pe.wait_ge(c_in, 16 * 7)
            pe.matmul(ps[0:NS * JH, 7, 0:NS], jsel[ID:ID + JH, :], g.kwT[ID:ID + JH, NP:T], start=True, stop=True).then_inc(w_done, 1)
            pe.matmul(ps[0:BH, 6, 0:SK], rel_rep[:, :, :].rearrange("p b h -> p (b h)"), onehot[:, :],
                      start=True, stop=True).then_inc(bias_done, 1)

            def index_turn(b):
                if b >= 2:
                    pe.wait_ge(kx_copied, b - 1)
                for q in range(2):
                    mm = pe.transpose(ps[0:ID, b % 2, q * P:(q + 1) * P], g.kx[:, b, q, :], g.ident[:, :])
                mm.then_inc(kx_turned, 1)

            index_turn(0)
            for b in range(NS):
                if b + 1 < NS:
                    index_turn(b + 1)
                pe.wait_ge(kx_copied, b + 1)
                if b == 0:
                    pe.wait_ge(dv, 2)
                pe.matmul(ps[0:NS * JH, 7, 0:SK], qm[:, b, :], kxT[:, b % 2, :], start=(b == 0), stop=(b == NS - 1)).then_inc(sc_done, 1)
            pe.wait_ge(sc_ready, 1)
            pe.wait_ge(bias_ready, 1)
            pe.matmul(ps[0:NS, 6, 0:SK], ownT32[:, :], sc32[:, :], start=True, stop=True).then_inc(sum_done, 1)

            def key_turn(b):
                for q in range(2):
                    if q == 0:
                        pe.wait_ge(k_in[b % 2], 32 * (b // 2 + 1))
                        if b >= 2:
                            pe.wait_ge(k_copied, b - 1)
                    for m in range(4):
                        o = (2 + 2 * (b % 2)) * BANK + m * PAST + q * P
                        mm = pe.transpose(psf[:, o:o + P], kk[:, b % 2, q, m * P:(m + 1) * P], g.ident[:, :])
                    mm.then_inc(k_turned, 1)

            key_turn(0)
            for b in range(NS):
                if b + 1 < NS:
                    key_turn(b + 1)
                pe.wait_ge(k_copied, b + 1)
                for m in range(4):
                    mm = pe.matmul(ps[0:BH, 7, 0:SK], qb[:, m, b, :], kTb[:, b % 2, m, :],
                                   start=(b == 0 and m == 0), stop=(b == NS - 1 and m == 3))
                mm.then_inc(lg_done, 1)
            pe.wait_ge(sel, 1)
            pe.matmul(ps[0:BH, 6, 0:SK], own[:, NS * JH:], sc[:, :], start=True, stop=True).then_inc(msk_done, 1)
            pe.wait_ge(p_ready, 1)
            for q in range(2):
                pe.transpose(ps[:, 0, q * BH:(q + 1) * BH], lg[:, q * P:(q + 1) * P], g.ident[0:BH, 0:BH])
            pe.transpose(ps[0:NS, 0, 2 * BH:3 * BH], pself[:, :], g.ident[0:BH, 0:BH]).then_inc(p_turned, 1)
            pe.wait_ge(p_copied, 1)
            pe.wait_ge(vs_in, 16)
            pe.matmul(ps[0:BH, 1, :], psT[:, :], vs[:, :], start=True, stop=False)
            for b in range(NS):
                pe.wait_ge(v_in[b], 32)
                for q in range(2):
                    mm = pe.matmul(ps[0:BH, 1, :], pT[:, q, b, :], vv[:, b, q, :], start=False, stop=(b == NS - 1 and q == 1))
            mm.then_inc(y_done, 1)
            pe.wait_ge(y_own, 1)
            for m in range(4):
                mm = pe.matmul(ps[:, 0, m * NS:(m + 1) * NS], yb[:, m * P:(m + 1) * P], ownT64[:, :], start=True, stop=True)
            mm.then_inc(y_summed, 1)


FT = 2 * FF // P
NG2 = FF // P // 2


def phase_merge(nc, g):
    with ExitStack() as ctx:
        sb = lambda n, s, d=F32: ctx.enter_context(nc.sbuf_tensor("m_" + n, s, d))
        ps, sem = g.ps, lambda n: g.sem("m_" + n)
        wst = sb("wst", [P, 2, 8, P])
        wh, wl = sb("wh", [P, 2, 8, P], F32R), sb("wl", [P, 2, 8, P], F32R)
        gt = sb("gt", [P, 2, 2, T])
        ma, mb = sb("ma", [P, T]), sb("mb", [P, T])
        w_in = [sem(f"w_in{i}") for i in range(2)]
        g_in = [sem(f"g_in{i}") for i in range(2)]
        w_hi, w_lo, done, prod, merged, m_hi, m_lo = (
            sem(n) for n in ("w_hi", "w_lo", "done", "prod", "merged", "m_hi", "m_lo"))
        block = ctx.enter_context(nc.Block())

        @block.sync
        def _(sp):
            wa = g.w_att_out.rearrange("(k p) n -> p k n", p=P)
            wb = g.w_ssm_out.rearrange("(k p) n -> p k n", p=P)
            for m in range(8):
                s, cs = m % 2, slice(m * P, (m + 1) * P)
                if m >= 2:
                    sp.wait_ge(w_lo, m - 1)
                sp.dma_start(wst[:, s, 0:4, :], wa[:, :, cs]).then_inc(w_in[s], 16)
                sp.dma_start(wst[:, s, 4:8, :], wb[:, :, cs]).then_inc(w_in[s], 16)
                if m >= 2:
                    sp.wait_ge(merged, m - 1)
                sp.dma_start(gt[:, s, 0, :], g.d_gates[:, m, :]).then_inc(g_in[s], 16)
                sp.dma_start(gt[:, s, 1, :], g.d_gates[:, 8 + m, :]).then_inc(g_in[s], 16)

        @block.gpsimd
        def _(pool):
            for m in range(8):
                s = m % 2
                pool.wait_ge(w_hi, m + 1)
                pool.tensor_tensor(wl[:, s, :, :], wst[:, s, :, :], wh[:, s, :, :].bitcast(F32), ALU.subtract).then_inc(w_lo, 1)

        @block.scalar
        def _(act):
            for m in range(9):
                if m < 8:
                    act.wait_ge(w_in[m % 2], 32 * (m // 2 + 1))
                    if m >= 2:
                        act.wait_ge(done, 2 * (m - 1))
                    act.activation(wh[:, m % 2, :, :], wst[:, m % 2, :, :], ACT.Copy).then_inc(w_hi, 1)
                if m:
                    act.wait_ge(merged, m)
                    act.activation(g.xT_h[:, m - 1, :], ma[:, :], ACT.Copy).then_inc(m_hi, 1)

        @block.vector
        def _(dve):
            for m in range(8):
                s = m % 2
                dve.wait_ge(g_in[s], 32 * (m // 2 + 1))
                dve.wait_ge(done, 2 * m + 1)
                if m:
                    dve.wait_ge(m_lo, m)
                dve.tensor_tensor(as_thirds(ma[:, :]), thirds(ps, 0), as_thirds(gt[:, s, 0, :]), ALU.mult).then_inc(prod, 1)
                dve.wait_ge(done, 2 * m + 2)
                dve.tensor_tensor(as_thirds(mb[:, :]), thirds(ps, 1), as_thirds(gt[:, s, 1, :]), ALU.mult).then_inc(prod, 1)
                dve.wait_ge(prod, 2 * m + 2)
                dve.tensor_tensor(ma[:, :], ma[:, :], mb[:, :], ALU.add).then_inc(merged, 1)
                dve.wait_ge(m_hi, m + 1)
                dve.tensor_tensor(g.xT_l[:, m, :], ma[:, :], g.xT_h[:, m, :].bitcast(F32), ALU.subtract).then_inc(m_lo, 1)

        @block.tensor
        def _(pe):
            for m in range(8):
                s = m % 2
                pe.wait_ge(w_lo, m + 1)
                for q, (xh, xl) in enumerate(((g.ya_h, g.ya_l), (g.ys_h, g.ys_l))):
                    if m:
                        pe.wait_ge(prod, 2 * m - 1 + q)
                    project(pe, ps, q, wh[:, s, 4 * q:4 * q + 4, :], wl[:, s, 4 * q:4 * q + 4, :], xh, xl, 4).then_inc(done, 1)


def phase_out(nc, g):
    with ExitStack() as ctx:
        sb = lambda n, s, d=F32: ctx.enter_context(nc.sbuf_tensor("o_" + n, s, d))
        ps, sem = g.ps, lambda n: g.sem("o_" + n)
        psf = ps[:, :, :].rearrange("p b c -> p (b c)")
        wst = sb("wst", [P, 2, D])
        wh, wl = sb("wh", [P, KD, D], F32R), sb("wl", [P, KD, D], F32R)
        gpost, gffn = sb("gpost", [P, D]), sb("gffn", [P, D])
        x = sb("x", [P, 2, D])
        z = sb("z", [P, 2, D])
        xn = sb("xn", [P, D])
        junk = sb("junk", [P, D])
        st = sb("st", [P, 2, 4, 9])
        w_in = [sem(f"w_in{i}") for i in range(2)]
        x_in = [sem(f"x_in{i}") for i in range(2)]
        w_hi, w_lo, g_in, done, z_done, ss_done, var_done, std_done, r_done, x2_done, xn_done, turned, hi_done, lo_done = (
            sem(n) for n in ("w_hi", "w_lo", "g_in", "done", "z_done", "ss_done", "var_done", "std_done", "r_done",
                             "x2_done", "xn_done", "turned", "hi_done", "lo_done"))
        x2_out = [sem(f"x2_out{i}") for i in range(2)]
        zs_done = sem("zs_done")
        block = ctx.enter_context(nc.Block())

        def rows(i):
            return TILES[i][1]

        @block.sync
        def _(sp):
            wv = g.w_o.rearrange("(k p) n -> p k n", p=P)
            for k in range(KD):
                if k >= 2:
                    sp.wait_ge(w_lo, k - 1)
                sp.dma_start(wst[:, k % 2, :], wv[:, k, :]).then_inc(w_in[k % 2], 16)
                if k == 1:
                    sp.dma_start(gpost[:, :], g.g_post_mix.partition_broadcast(P)).then_inc(g_in, 16)
                    sp.dma_start(gffn[:, :], g.g_pre_ffn.partition_broadcast(P)).then_inc(g_in, 16)

            def store(i):
                t0, n = TILES[i]
                sp.wait_ge(x2_done, i + 1)
                sp.dma_start(g.d_x2[t0:t0 + n, :], z[0:n, i % 2, :]).then_inc(x2_out[i % 2], 16)

            for i, (t0, n) in enumerate(TILES):
                if i >= 2:
                    store(i - 2)
                src = g.x_prompt.rearrange("b t d -> (b t) d")[t0:t0 + n, :] if i < NT else \
                    g.x_sample.rearrange("b t d -> (b t) d")
                sp.dma_start(x[0:n, i % 2, :], src).then_inc(x_in[i % 2], 16)
            store(7)
            store(8)
            sp.wait_ge(x2_out[0], 16 * 5)
            sp.wait_ge(x2_out[1], 16 * 4)

        @block.gpsimd
        def _(pool):
            for k in range(KD):
                pool.wait_ge(w_hi, k + 1)
                pool.tensor_tensor(wl[:, k, :], wst[:, k % 2, :], wh[:, k, :].bitcast(F32), ALU.subtract).then_inc(w_lo, 1)

        @block.scalar
        def _(act):
            for k in range(KD):
                act.wait_ge(w_in[k % 2], 16 * (k // 2 + 1))
                act.activation(wh[:, k, :], wst[:, k % 2, :], ACT.Copy).then_inc(w_hi, 1)

            def square(i, q):
                n = rows(i)
                c = 2 * i + q
                if c:
                    act.wait_ge(ss_done, c)
                act.activation(junk[0:n, :], z[0:n, i % 2, :], ACT.Square, accum_out=st[0:n, q, 0, i:i + 1]).then_inc(ss_done, 1)
                act.wait_ge(var_done, c + 1)
                act.activation(st[0:n, q, 2, i:i + 1], st[0:n, q, 1, i:i + 1], ACT.Sqrt).then_inc(std_done, 1)

            def high(i):
                t0, n = TILES[i]
                act.wait_ge(turned, i + 1)
                act.activation(g.xT_h[:, :, t0:t0 + n], psf[:, 4 * BANK:6 * BANK].rearrange(
                    "p (k t) -> p k t", k=KD)[:, :, 0:n], ACT.Copy).then_inc(hi_done, 1)

            for i in range(9):
                n = rows(i)
                act.wait_ge(done, i + 1)
                if i >= 2:
                    act.wait_ge(x2_out[i % 2], 16 * (i // 2))
                    act.wait_ge(xn_done, i - 1)
                act.activation(z[0:n, i % 2, :], psf[0:n, (i % 2) * 1024:(i % 2) * 1024 + D], ACT.Copy).then_inc(z_done, 1)
                act.wait_ge(z_done, i + 1)
                square(i, 0)
                act.wait_ge(x2_done, i + 1)
                square(i, 1)
                if i:
                    high(i - 1)
            high(8)

        @block.vector
        def _(dve):
            rc = [0]

            def norm(i, q):
                n = rows(i)
                c = 2 * i + q
                dve.wait_ge(ss_done, c + 1)
                dve.tensor_scalar(st[0:n, q, 1, i:i + 1], st[0:n, q, 0, i:i + 1], 1.0 / D, EPS, ALU.mult, ALU.add).then_inc(var_done, 1)
                dve.wait_ge(std_done, c + 1)
                newton_rstd(dve, st[0:n, q, 3, i:i + 1], st[0:n, q, 2, i:i + 1], st[0:n, q, 1, i:i + 1], r_done, rc[0])
                rc[0] += 5

            def low(i):
                t0, n = TILES[i]
                dve.wait_ge(hi_done, i + 1)
                dve.tensor_tensor(g.xT_l[:, :, t0:t0 + n], psf[:, 4 * BANK:6 * BANK].rearrange(
                    "p (k t) -> p k t", k=KD)[:, :, 0:n], g.xT_h[:, :, t0:t0 + n].bitcast(F32), ALU.subtract).then_inc(lo_done, 1)

            dve.wait_ge(g_in, 32)
            for i in range(9):
                n = rows(i)
                zi = z[0:n, i % 2, :]
                norm(i, 0)
                dve.scalar_tensor_tensor(out=zi, in0=zi, scalar=st[0:n, 0, 3, i:i + 1], in1=gpost[0:n, :],
                                         op0=ALU.mult, op1=ALU.mult).then_inc(zs_done, 1)
                dve.wait_ge(zs_done, i + 1)
                dve.wait_ge(x_in[i % 2], 16 * (i // 2 + 1))
                dve.tensor_tensor(zi, zi, x[0:n, i % 2, :], ALU.add).then_inc(x2_done, 1)
                dve.wait_ge(x2_done, i + 1)
                norm(i, 1)
                if i:
                    dve.wait_ge(turned, i)
                dve.scalar_tensor_tensor(out=xn[0:n, :], in0=zi, scalar=st[0:n, 1, 3, i:i + 1], in1=gffn[0:n, :],
                                         op0=ALU.mult, op1=ALU.mult).then_inc(xn_done, 1)
                if i:
                    low(i - 1)
            low(8)

        @block.tensor
        def _(pe):
            def turn(i):
                n = rows(i)
                pe.wait_ge(xn_done, i + 1)
                if i:
                    pe.wait_ge(lo_done, i)
                for k in range(KD):
                    o = 4 * BANK + k * P
                    mm = pe.transpose(psf[:, o:o + n], xn[0:n, k * P:(k + 1) * P], g.ident[0:n, 0:n])
                mm.then_inc(turned, 1)

            for i, (t0, n) in enumerate(TILES):
                if i >= 2:
                    pe.wait_ge(z_done, i - 1)
                for k in range(KD):
                    if i == 0:
                        pe.wait_ge(w_lo, k + 1)
                    for q, (x_, w) in enumerate(((g.xT_h, wh), (g.xT_h, wl), (g.xT_l, wh))):
                        for c in range(2):
                            mm = pe.matmul(ps[0:n, (i % 2) * 2 + c, :], x_[:, k, t0:t0 + n], w[:, k, c * BANK:(c + 1) * BANK],
                                           start=(k == 0 and q == 0), stop=(k == KD - 1 and q == 2))
                mm.then_inc(done, 1)
                if i:
                    turn(i - 1)
            turn(8)


def phase_ffn_setup(nc, g):
    with ExitStack() as ctx:
        sb = lambda n, s, d=F32: ctx.enter_context(nc.sbuf_tensor("q_" + n, s, d))
        ps, sem = g.ps, lambda n: g.sem("q_" + n)
        psf = ps[:, :, :].rearrange("p b c -> p (b c)")
        cst = sb("cst", [FT, 4, P])
        sst = sb("sst", [FT, 2 * NS, P])
        sc = sb("sc", [P, NS, 2, FT])
        tmp = sb("tmp", [P, NS, FT])
        c_in, turned, copied, dv, row_out = (sem(n) for n in ("c_in", "turned", "copied", "dv", "row_out"))
        block = ctx.enter_context(nc.Block())

        @block.sync
        def _(sp):
            for j in range(3):
                sp.dma_start(cst[:, j, :], g.conv_w[j, :].rearrange("(t p) -> t p", p=P)).then_inc(c_in, 16)
            sp.dma_start(cst[:, 3, :], g.conv_b.rearrange("(t p) -> t p", p=P)).then_inc(c_in, 16)
            sp.dma_start(sst[:, :, :], g.state_conv.rearrange("b i (t p) -> t (b i) p", p=P)).then_inc(c_in, 16)
            sp.dma_start(g.conv_sample[:, 0, :], g.state_conv[:, 1, :]).then_inc(row_out, 16)
            sp.wait_ge(row_out, 16)

        @block.scalar
        def _(act):
            act.wait_ge(turned, 1)
            act.activation(g.cw[:, :, :].rearrange("p j t -> p (j t)"), ps[:, 0, 0:4 * FT], ACT.Copy)
            act.activation(sc[:, :, :, :].rearrange("p b i t -> p (b i t)"), psf[:, BANK:BANK + 2 * NS * FT],
                           ACT.Copy).then_inc(copied, 1)

        @block.vector
        def _(dve):
            n = [0]

            def step(ins):
                ins.then_inc(dv, 1)
                n[0] += 1
                dve.wait_ge(dv, n[0])

            def w(j):
                return g.cw[:, j, :].unsqueeze(1).broadcast_to([P, NS, FT])

            dve.wait_ge(copied, 1)
            step(dve.tensor_tensor(tmp[:, :, :], sc[:, :, 0, :], w(0), ALU.mult))
            step(dve.tensor_tensor(sc[:, :, 1, :], sc[:, :, 1, :], w(1), ALU.mult))
            step(dve.tensor_tensor(tmp[:, :, :], tmp[:, :, :], sc[:, :, 1, :], ALU.add))
            step(dve.tensor_tensor(g.conv0[:, :, :].rearrange("p t b -> p b t"), tmp[:, :, :], w(3), ALU.add))

        @block.tensor
        def _(pe):
            pe.wait_ge(c_in, 16 * 5)
            for j in range(4):
                pe.transpose(ps[:, 0, j * FT:(j + 1) * FT], cst[:, j, :], g.ident[0:FT, 0:FT])
            for r in range(2 * NS):
                mm = pe.transpose(psf[:, BANK + r * FT:BANK + (r + 1) * FT], sst[:, r, :], g.ident[0:FT, 0:FT])
            mm.then_inc(turned, 1)


def phase_ffn(nc, g):
    with ExitStack() as ctx:
        sb = lambda n, s, d=F32: ctx.enter_context(nc.sbuf_tensor("f_" + n, s, d))
        ps, sem = g.ps, lambda n: g.sem("f_" + n)
        wst = sb("wst", [P, 2, 8 * P])
        wh, wl = sb("wh", [P, 2, 8 * P], F32R), sb("wl", [P, 2, 8 * P], F32R)
        up = sb("up", [P, 2, 2 + T])
        acc = sb("acc", [P, 2, T])
        gh, gl = sb("gh", [P, 2, 2, T], F32R), sb("gl", [P, 2, 2, T], F32R)
        keep = sb("keep", [P, 10, FT])
        kept = sb("kept", [FT, 10, P])

        w_in = [sem(f"w_in{i}") for i in range(2)]
        w_hi, w_lo = sem("w_hi"), sem("w_lo")
        up_done, up_evac, down_done, down_evac = (sem(n) for n in ("up_done", "up_evac", "down_done", "down_evac"))
        tap0, tap0s, tap1, conv, gelu, prod, g_hi, g_lo, kept_cols, zero = (
            sem(n) for n in ("tap0", "tap0s", "tap1", "conv", "gelu", "prod", "g_hi", "g_lo", "kept_cols", "zero"))
        k_turned, k_copied, k_out = sem("k_turned"), sem("k_copied"), sem("k_out")
        block = ctx.enter_context(nc.Block())

        def job(it, q):
            return it * 6 + (q - 2)

        NJOB = 4 + 6 * (NG2 - 1) + 2
        up_v = g.w_up.rearrange("(k p) n -> p k n", p=P)
        down_v = g.w_down.rearrange("(k p) n -> p k n", p=P)

        def up_cols(it, q):
            return it * (2 * P) + ((q % 2) * FF + (q // 2) * P)

        @block.sync
        def _(sp):
            def load(j, s, it, q):
                if not isinstance(j, int) or j >= 2:
                    sp.wait_ge(w_lo, j - 1)
                if q < 4:
                    src = up_v[:, :, bass.ds(up_cols(it, q), P)]
                    dst = wst[:, s, :].rearrange("p (k n) -> p k n", k=KD)
                else:
                    src = down_v[:, bass.ds((it - 1) * 2, 2), (q - 4) * BANK:(q - 3) * BANK]
                    dst = wst[:, s, :].rearrange("p (k n) -> p k n", k=2)
                sp.dma_start(dst, src).then_inc(w_in[s], 16)

            for q in range(4):
                load(q, q % 2, 0, q)
            for q in range(6):
                load(job(1, q), q % 2, 1, q)
            with sp.Fori(0, (NG2 - 2) // 2) as j:
                for e in range(2):
                    for q in range(6):
                        load(j * 12 + job(2 + e, q), q % 2, j * 2 + (2 + e), q)
            for q in (4, 5):
                load(job(NG2, q - 4), q % 2, NG2, q)
            sp.wait_ge(k_copied, 1)
            sp.dma_start(g.conv_prompt.rearrange("i (t p) -> t i p", p=P), kept[:, 0:2, :]).then_inc(k_out, 16)
            sp.dma_start(g.conv_sample[:, 1, :].rearrange("b (t p) -> t b p", p=P), kept[:, 2:10, :]).then_inc(k_out, 16)
            sp.wait_ge(k_out, 32)

        @block.gpsimd
        def _(pool):
            def low(j, s):
                pool.wait_ge(w_hi, j + 1)
                pool.tensor_tensor(wl[:, s, :], wst[:, s, :], wh[:, s, :].bitcast(F32), ALU.subtract).then_inc(w_lo, 1)

            def keep_cols(it, q):
                u = it * 4 + q
                pool.wait_ge(up_evac, u + 1)
                tile = bass.ds(it * 2 + (q // 2 + (q % 2) * (FT // 2)), 1)
                pool.tensor_copy(keep[:, :, tile], up[:, q % 2, NP:NP + 10].unsqueeze(2)).then_inc(kept_cols, 1)

            pool.memset(g.fT[:, :, :], 0.0).then_inc(zero, 1)
            pool.memset(up[:, :, 0:2], 0.0).then_inc(zero, 1)
            low(0, 0)
            for q in range(4):
                low(q + 1, (q + 1) % 2)
                keep_cols(0, q)

            def iteration(it, j0):
                for q in range(6):
                    low(j0 + (q + 1), (q + 1) % 2)
                    if q < 4:
                        keep_cols(it, q)

            iteration(1, job(1, 0))
            with pool.Fori(0, (NG2 - 2) // 2) as j:
                for e in range(2):
                    iteration(j * 2 + (2 + e), j * 12 + job(2 + e, 0))
            low(NJOB - 1, 1)

        @block.scalar
        def _(act):
            def high(it, q):
                if isinstance(it, int) and it in (0, NG2):
                    s, uses = (q % 2, 16 * (q // 2 + 1)) if it == 0 else (q % 2, 16 * (NJOB // 2))
                else:
                    s, uses = q % 2, it * 48 + 16 * ((q - 2) // 2 + 1)
                act.wait_ge(w_in[s], uses)
                if isinstance(it, int) and it == NG2:
                    act.wait_ge(down_done, (NG2 - 2) * 8 + 4 * (q - 3))
                elif q >= 2:
                    act.wait_ge(up_done, it * 4 + (q - 1))
                elif isinstance(it, int) and it == 1:
                    act.wait_ge(up_done, q + 3)
                elif not isinstance(it, int) or it > 1:
                    act.wait_ge(down_done, it * 8 + (4 * q - 12))
                act.activation(wh[:, s, :], wst[:, s, :], ACT.Copy).then_inc(w_hi, 1)

            def evacuate(it, q):
                u, r = it * 4 + q, q % 2
                tile = bass.ds(it * 2 + (q // 2 + r * (FT // 2)), 1)
                act.wait_ge(up_done, u + 1)
                if not isinstance(it, int) or it or q >= 2:
                    act.wait_ge(conv, u - 1)
                    act.wait_ge(kept_cols, u - 1)
                act.activation(as_thirds(up[:, r, 2:2 + T]), thirds(ps, r), ACT.Copy).then_inc(up_evac, 1)
                act.wait_ge(up_evac, u + 1)
                if not isinstance(it, int) or it or q >= 2:
                    act.wait_ge(g_lo, it * 2 + q // 2)
                act.activation(acc[:, r, 0:NP], up[:, r, 0:NP], ACT.Identity, scale=g.cw[:, 0, tile],
                               bias=g.cw[:, 3, tile]).then_inc(tap0, 1)

            def gate(it, r, par):
                m = it * 2 + r
                act.wait_ge(conv, m * 2 + 1)
                act.activation(acc[:, 0, :], acc[:, 0, :], ACT.Gelu_apprx_tanh).then_inc(gelu, 1)

            def part(it, r, par):
                m = it * 2 + r
                act.wait_ge(prod, m + 1)
                if not isinstance(it, int) or it >= 2:
                    act.wait_ge(down_done, (it - 1) * 8)
                act.activation(gh[:, par, r, :], acc[:, 0, :], ACT.Copy).then_inc(g_hi, 1)

            def iteration(it, n, par, last=False):
                high(it, 1)
                for q in range(4):
                    evacuate(it, q)
                    if q + 2 < n:
                        high(it, q + 2)
                    elif q + 2 == n:
                        high(it + 1, 0)
                    if q % 2 == 1:
                        gate(it, q // 2, par)
                        part(it, q // 2, par)
                if last:
                    high(NG2, 4)
                elif n > 4:
                    high(it + 1, 0)

            act.wait_ge(zero, 2)
            high(0, 0)
            iteration(0, 4, 0)
            iteration(1, 6, 1)
            with act.Fori(0, (NG2 - 4) // 2) as j:
                for e in range(2):
                    iteration(j * 2 + (2 + e), 6, e)
            iteration(NG2 - 2, 6, 0)
            iteration(NG2 - 1, 6, 1, last=True)
            high(NG2, 5)
            act.wait_ge(k_turned, 1)
            act.activation(kept[:, 0:8, :], ps[0:FT, 6:8, :].rearrange("t b (r p) -> t (b r) p", p=P), ACT.Copy)
            act.activation(kept[:, 8:10, :], ps[0:FT, 0, 0:2 * P].rearrange("t (r p) -> t r p", p=P), ACT.Copy).then_inc(k_copied, 1)

        @block.vector
        def _(dve):
            def taps(it, q):
                u, r = it * 4 + q, q % 2
                tile = bass.ds(it * 2 + (q // 2 + r * (FT // 2)), 1)
                dve.wait_ge(tap0, u + 1)
                dve.tensor_copy(acc[:, r, NP:T], g.conv0[:, tile, :].rearrange("p a b -> p (a b)")).then_inc(tap0s, 1)
                dve.scalar_tensor_tensor(out=acc[:, r, 0:NP], in0=up[:, r, 1:1 + NP], scalar=g.cw[:, 1, tile],
                                         in1=acc[:, r, 0:NP], op0=ALU.mult, op1=ALU.add).then_inc(tap1, 1)
                dve.wait_ge(tap0s, u + 1)
                dve.wait_ge(tap1, u + 1)
                dve.scalar_tensor_tensor(out=acc[:, r, :], in0=up[:, r, 2:2 + T], scalar=g.cw[:, 2, tile],
                                         in1=acc[:, r, :], op0=ALU.mult, op1=ALU.add).then_inc(conv, 1)

            def product(it, r, par):
                m = it * 2 + r
                dve.wait_ge(gelu, m + 1)
                dve.wait_ge(conv, m * 2 + 2)
                dve.tensor_tensor(acc[:, 0, :], acc[:, 0, :], acc[:, 1, :], ALU.mult).then_inc(prod, 1)

            def low(it, r, par):
                m = it * 2 + r
                dve.wait_ge(g_hi, m + 1)
                dve.tensor_tensor(gl[:, par, r, :], acc[:, 0, :], gh[:, par, r, :].bitcast(F32), ALU.subtract).then_inc(g_lo, 1)

            def down(d, m):
                dve.wait_ge(down_done, d + 1)
                if not isinstance(d, int) or d >= 8:
                    dve.wait_ge(down_evac, d - 7)
                f = as_thirds(g.fT[:, m, :])
                dve.tensor_tensor(f, thirds(ps, m % 2), f, ALU.add).then_inc(down_evac, 1)

            def iteration(it, par, has_down):
                taps(it, 0)
                taps(it, 1)
                product(it, 0, par)
                low(it, 0, par)
                taps(it, 2)
                if has_down:
                    down(it * 8 - 8, 0)
                taps(it, 3)
                if has_down:
                    down(it * 8 - 7, 1)
                product(it, 1, par)
                if has_down:
                    down(it * 8 - 6, 2)
                low(it, 1, par)
                if has_down:
                    for m in range(3, 8):
                        down(it * 8 + (m - 8), m)

            dve.wait_ge(zero, 2)
            iteration(0, 0, False)
            iteration(1, 1, True)
            with dve.Fori(0, (NG2 - 2) // 2) as j:
                for e in range(2):
                    iteration(j * 2 + (2 + e), e, True)
            for m in range(8):
                down((NG2 - 1) * 8 + m, m)

        @block.tensor
        def _(pe):
            def ups(it, q, j, s):
                u, r = it * 4 + q, q % 2
                pe.wait_ge(w_lo, j + 1)
                if not isinstance(it, int) or it or q >= 2:
                    pe.wait_ge(up_evac, u - 1)
                if q < 2 and (not isinstance(it, int) or it >= 2):
                    pe.wait_ge(down_evac, it * 8 + (q - 9))
                w3, l3 = (w[:, s, :].rearrange("p (k n) -> p k n", k=KD) for w in (wh, wl))
                project(pe, ps, r, w3, l3, g.xT_h, g.xT_l, KD).then_inc(up_done, 1)

            def downs(it, j0, par, ups_before=True):
                pe.wait_ge(g_lo, it * 2)
                for m in range(8):
                    if m % 4 == 0:
                        pe.wait_ge(w_lo, j0 + (m // 4 + 1))
                    if m >= 2 or not ups_before:
                        pe.wait_ge(down_evac, it * 8 + (m - 9))
                    else:
                        pe.wait_ge(up_evac, it * 4 + (3 + m))
                    w3, l3 = (w[:, m // 4, :].rearrange("p (k n) -> p k n", k=2)[:, :, (m % 4) * P:(m % 4 + 1) * P]
                              for w in (wh, wl))
                    project(pe, ps, m % 2, w3, l3, gh[:, par, :, :], gl[:, par, :, :], 2).then_inc(down_done, 1)

            for q in range(4):
                ups(0, q, q, q % 2)
            for q in range(4):
                ups(1, q, job(1, q), q % 2)
            downs(1, job(1, 4), 0)
            with pe.Fori(0, (NG2 - 2) // 2) as j:
                for e in range(2):
                    for q in range(4):
                        ups(j * 2 + (2 + e), q, j * 12 + job(2 + e, q), q % 2)
                    downs(j * 2 + (2 + e), j * 12 + job(2 + e, 4), (1 + e) % 2)
            downs(NG2, job(NG2, 0), 1, ups_before=False)
            pe.wait_ge(kept_cols, FT)
            pe.wait_ge(down_evac, (NG2) * 8)
            for r in range(10):
                bank, o = (6 + r // 4, (r % 4) * P) if r < 8 else (0, (r - 8) * P)
                mm = pe.transpose(ps[0:FT, bank, o:o + P], keep[:, r, :], g.ident[:, :])
            mm.then_inc(k_turned, 1)


def phase_final(nc, g):
    with ExitStack() as ctx:
        sb = lambda n, s, d=F32: ctx.enter_context(nc.sbuf_tensor("y_" + n, s, d))
        ps, sem = g.ps, lambda n: g.sem("y_" + n)
        psf = ps[:, :, :].rearrange("p b c -> p (b c)")
        NR = 3
        gain = sb("gain", [P, D])
        x2 = sb("x2", [P, NR, D])
        y = sb("y", [P, NR, D])
        junk = sb("junk", [P, D])
        st = sb("st", [P, 4, 9])
        g_in, turned, ss_done, var_done, std_done, r_done, y_scaled, y_done = (
            sem(n) for n in ("g_in", "turned", "ss_done", "var_done", "std_done", "r_done", "y_scaled", "y_done"))
        x_in = [sem(f"x_in{i}") for i in range(NR)]
        y_out = [sem(f"y_out{i}") for i in range(NR)]
        block = ctx.enter_context(nc.Block())

        @block.sync
        def _(sp):
            sp.dma_start(gain[:, :], g.g_post_ffn.partition_broadcast(P)).then_inc(g_in, 16)

            def store(i):
                t0, n = TILES[i]
                sp.wait_ge(y_done, i + 1)
                dst = g.y_prompt[t0:t0 + n, :] if i < NT else g.y_sample
                sp.dma_start(dst, y[0:n, i % NR, :]).then_inc(y_out[i % NR], 16)

            for i, (t0, n) in enumerate(TILES):
                if i >= NR:
                    store(i - NR)
                sp.dma_start(x2[0:n, i % NR, :], g.d_x2[t0:t0 + n, :]).then_inc(x_in[i % NR], 16)
            for i in range(9 - NR, 9):
                store(i)
            for s in range(NR):
                sp.wait_ge(y_out[s], 16 * 3)

        @block.scalar
        def _(act):
            for i, (_, n) in enumerate(TILES):
                act.wait_ge(turned, i + 1)
                if i:
                    act.wait_ge(ss_done, i)
                act.activation(junk[0:n, :], psf[0:n, (i % 4) * D:(i % 4 + 1) * D], ACT.Square,
                               accum_out=st[0:n, 0, i:i + 1]).then_inc(ss_done, 1)
                act.wait_ge(var_done, i + 1)
                act.activation(st[0:n, 2, i:i + 1], st[0:n, 1, i:i + 1], ACT.Sqrt).then_inc(std_done, 1)

        @block.vector
        def _(dve):
            dve.wait_ge(g_in, 16)
            for i, (_, n) in enumerate(TILES):
                dve.wait_ge(ss_done, i + 1)
                dve.tensor_scalar(st[0:n, 1, i:i + 1], st[0:n, 0, i:i + 1], 1.0 / D, EPS, ALU.mult, ALU.add).then_inc(var_done, 1)
                dve.wait_ge(std_done, i + 1)
                newton_rstd(dve, st[0:n, 3, i:i + 1], st[0:n, 2, i:i + 1], st[0:n, 1, i:i + 1], r_done, 5 * i)
                if i >= NR:
                    dve.wait_ge(y_out[i % NR], 16 * (i // NR))
                yi = y[0:n, i % NR, :]
                dve.scalar_tensor_tensor(out=yi, in0=psf[0:n, (i % 4) * D:(i % 4 + 1) * D], scalar=st[0:n, 3, i:i + 1],
                                         in1=gain[0:n, :], op0=ALU.mult, op1=ALU.mult).then_inc(y_scaled, 1)
                dve.wait_ge(y_scaled, i + 1)
                dve.wait_ge(x_in[i % NR], 16 * (i // NR + 1))
                dve.tensor_tensor(yi, yi, x2[0:n, i % NR, :], ALU.add).then_inc(y_done, 1)

        @block.tensor
        def _(pe):
            for i, (t0, n) in enumerate(TILES):
                if i >= 4:
                    pe.wait_ge(y_scaled, i - 3)
                for k in range(KD):
                    o = (i % 4) * D + k * P
                    mm = pe.transpose(psf[0:n, o:o + P], g.fT[:, k, t0:t0 + n], g.ident[:, :])
                mm.then_inc(turned, 1)


PER_LAYER = ["cache_k", "cache_v", "cache_kidx", "state_ssm_re", "state_ssm_im", "state_conv", "w_in", "g_pre_mix",
             "g_post_mix", "lam_re", "lam_im", "log_dt", "b_re", "b_im", "c_re", "c_im", "d_skip", "w_glu", "b_glu",
             "w_att_out", "w_ssm_out", "w_o", "g_pre_ffn", "g_post_ffn", "w_up", "conv_w", "conv_b", "w_down"]


class Program:

    def __init__(self, ins, outs):
        self.x_prompt = ins["x_prompt"]
        self.x_sample = ins["x_sample"]
        self.page_table = ins["page_table"]
        self.rel_bias = ins["rel_bias"]
        self.cache_k = ins["cache_k"][0].rearrange("n p h d -> n p (h d)")
        self.cache_v = ins["cache_v"][0].rearrange("n p h d -> n p (h d)")
        self.cache_kidx = ins["cache_kidx"][0]
        self.state_re = ins["state_ssm_re"][0]
        self.state_im = ins["state_ssm_im"][0]
        self.state_conv = ins["state_conv"][0]
        self.w_in = ins["w_in"][0]
        self.g_pre_mix = ins["g_pre_mix"][0]
        self.g_post_mix = ins["g_post_mix"][0]
        self.lam_re = ins["lam_re"][0]
        self.lam_im = ins["lam_im"][0]
        self.log_dt = ins["log_dt"][0]
        self.b_re = ins["b_re"][0]
        self.b_im = ins["b_im"][0]
        self.c_re = ins["c_re"][0]
        self.c_im = ins["c_im"][0]
        self.d_skip = ins["d_skip"][0]
        self.w_glu = ins["w_glu"][0]
        self.b_glu = ins["b_glu"][0]
        self.w_att_out = ins["w_att_out"][0]
        self.w_ssm_out = ins["w_ssm_out"][0]
        self.w_o = ins["w_o"][0]
        self.g_pre_ffn = ins["g_pre_ffn"][0]
        self.g_post_ffn = ins["g_post_ffn"][0]
        self.w_up = ins["w_up"][0]
        self.conv_w = ins["conv_w"][0]
        self.conv_b = ins["conv_b"][0]
        self.w_down = ins["w_down"][0]
        self.c_ident = ins["c_ident"]
        self.c_not_causal = ins["c_not_causal"]
        self.c_sign = ins["c_sign"]
        self.c_swap = ins["c_swap"]
        self.c_onehot = ins["c_onehot"]
        self.c_onehot_s = ins["c_onehot_s"]
        self.c_own = ins["c_own"]
        self.c_own32 = ins["c_own32"]
        self.c_own64 = ins["c_own64"]
        self.c_jsel = ins["c_jsel"]
        self.c_headsel = ins["c_headsel"]
        self.y_prompt = outs["y_prompt"]
        self.y_sample = outs["y_sample"]
        self.k_prompt = outs["k_prompt"]
        self.v_prompt = outs["v_prompt"]
        self.kidx_prompt = outs["kidx_prompt"]
        self.ssm_re_prompt = outs["ssm_re_prompt"]
        self.ssm_im_prompt = outs["ssm_im_prompt"]
        self.conv_prompt = outs["conv_prompt"]
        self.k_sample = outs["k_sample"]
        self.v_sample = outs["v_sample"]
        self.kidx_sample = outs["kidx_sample"]
        self.ssm_re_sample = outs["ssm_re_sample"]
        self.ssm_im_sample = outs["ssm_im_sample"]
        self.conv_sample = outs["conv_sample"]


def build(nc, ins, outs):
    g = Program(ins, outs)

    def scratch(name, shape):
        return nc.dram_tensor(name, shape, F32, kind="Internal").ap()

    g.d_gates = scratch("d_gates", (P, 16, T))
    g.d_u, g.d_us = scratch("d_u", (NP, SW)), scratch("d_us", (NS, SW))
    g.d_bias, g.d_x2 = scratch("d_bias", (H, P * DIST)), scratch("d_x2", (T, D))
    taken = []

    def sem(name):
        taken.append(nc.alloc_semaphore(name))
        return taken[-1]

    g.sem = sem

    def place(stack, name, shape, dt=F32, side=None):
        return stack.enter_context(nc.sbuf_tensor("g_" + name, shape, dt, side=side))

    with ExitStack() as ctx:
        g.ps = ctx.enter_context(nc.psum_tensor("ps", [P, 8, BANK], F32))
        g.ident = place(ctx, "ident", [P, P])
        g.cw, g.conv0 = place(ctx, "cw", [P, 4, FT]), place(ctx, "conv0", [P, FT, NS])
        with ExitStack() as branches:
            with ExitStack() as att:
                g.qT, g.kT = place(att, "qT", [P, 4, T]), place(att, "kT", [P, 4, T])
                g.qiT, g.kwT = place(att, "qiT", [P, 2, T]), place(att, "kwT", [68, T])
                masks = place(att, "masks", [P, sum((i + 1) * P for i in range(2, NT))])
                starts = [sum((j + 1) * P for j in range(2, i)) for i in range(2, NT + 1)]
                g.mask = [masks[:, a:b] for a, b in zip(starts, starts[1:])]
                with ExitStack() as first:
                    g.kiT2 = place(first, "kiT2", [P, T])
                    g.hT_h, g.hT_l = (place(first, n, [P, KD, T], F32R) for n in ("hT_h", "hT_l"))
                    phase_norm(nc, g)
                    phase_project(nc, g)
                with ExitStack() as ssm:
                    g.gT = place(ssm, "gT", [P, 4, T])
                    phase_ssm(nc, g)
                    g.ys_h, g.ys_l = (place(branches, n, [P, 4, T], F32R, "right") for n in ("ys_h", "ys_l"))
                    phase_glu(nc, g)
                nc.clear_and_free_semaphores(taken[:])
                taken.clear()
                nc.all_engine_barrier()
                g.ya_h, g.ya_l = (place(branches, n, [P, 4, T], F32R, "right") for n in ("ya_h", "ya_l"))
                g.table, g.kx = place(att, "table", [1, NS * 2], I32), place(att, "kx", [P, NS, 2, ID])
                phase_attention(nc, g)
                phase_sample(nc, g)
            g.xT_h, g.xT_l = (place(ctx, n, [P, KD, T], F32R) for n in ("xT_h", "xT_l"))
            phase_merge(nc, g)
        phase_out(nc, g)
        phase_ffn_setup(nc, g)
        g.fT = place(ctx, "fT", [P, KD, T])
        phase_ffn(nc, g)
        phase_final(nc, g)


def shape_constants():
    f = np.float32
    starts = np.array(bucket_of_distance())
    own = np.eye(NS, dtype=f)
    bucket = lambda d: (starts[np.maximum(d, 0)][None] == np.arange(NB)[:, None]).astype(f)
    return {
        "c_ident": np.eye(P, dtype=f),
        "c_not_causal": np.triu(np.ones((P, P), f), 1),
        "c_sign": np.repeat(np.array([-1, 1], f), ST)[:, None].copy(),
        "c_swap": np.roll(np.eye(P, dtype=f), ST, 0),
        "c_onehot": bucket(2 * P - 1 - np.arange(DIST)),
        "c_onehot_s": bucket(PAST - np.arange(SK)),
        "c_own": np.concatenate([np.repeat(own, JH, 1), np.repeat(own, H, 1)], 1),
        "c_own32": np.repeat(own, JH, 0),
        "c_own64": np.repeat(own, H, 0),
        "c_headsel": np.tile(np.eye(H, dtype=f), (NS, 1)),
        "c_jsel": np.tile(np.eye(JH, dtype=f), (1, NS)),
    }


_INS = ["x_prompt", "x_sample", "page_table", "rel_bias"] + PER_LAYER
_OUTS = [
    ("y_prompt", (NP, D), (1, NP, D)), ("y_sample", (NS, D), (NS, 1, D)),
    ("k_prompt", (NP, AW), (1, 1, NP, H, HD)), ("v_prompt", (NP, AW), (1, 1, NP, H, HD)),
    ("kidx_prompt", (NP, ID), (1, 1, NP, ID)),
    ("ssm_re_prompt", (NG, ST), (1, 1, NG, ST)), ("ssm_im_prompt", (NG, ST), (1, 1, NG, ST)),
    ("conv_prompt", (2, 2 * FF), (1, 1, 2, 2 * FF)),
    ("k_sample", (NS, AW), (1, NS, 1, H, HD)), ("v_sample", (NS, AW), (1, NS, 1, H, HD)),
    ("kidx_sample", (NS, ID), (1, NS, 1, ID)),
    ("ssm_re_sample", (NS, NG, ST), (1, NS, NG, ST)), ("ssm_im_sample", (NS, NG, ST), (1, NS, NG, ST)),
    ("conv_sample", (NS, 2, 2 * FF), (1, NS, 2, 2 * FF)),
]


def kernel(**inputs):
    import concourse.bacc as _bacc
    from concourse.bass_utils import run_bass_kernel_spmd as _run

    nc = _bacc.Bacc("TRN2", target_bir_lowering=False, num_devices=1)
    arrays = {f"in_{n}": np.ascontiguousarray(inputs[n]) for n in _INS}
    arrays.update({f"in_{n}": np.ascontiguousarray(a) for n, a in shape_constants().items()})
    ins = {n[3:]: nc.dram_tensor(n, a.shape, mybir.dt.from_np(a.dtype), kind="ExternalInput").ap()
           for n, a in arrays.items()}
    outs = {n: nc.dram_tensor("out_" + n, shape, F32, kind="ExternalOutput").ap() for n, shape, _ in _OUTS}
    build(nc, ins, outs)
    r = _run(nc, [arrays], core_ids=[0])
    return tuple(np.asarray(r.results[0]["out_" + n]).reshape(shape) for n, _, shape in _OUTS)
```

```python
from contextlib import ExitStack
import math

import numpy as np
import concourse.bass as bass
from concourse import mybir

ALU = mybir.AluOpType
ACT = mybir.ActivationFunctionType
AX = mybir.AxisListType
F32 = mybir.dt.float32
F32R = mybir.dt.float32r
I32 = mybir.dt.int32

P = 128
D = 1024
KD = D // P
NP = 1024
NS = 8
T = NP + NS
NT = NP // P
TILES = [(i * P, P) for i in range(NT)] + [(NP, NS)]
CH = T // 3
BANK = 512
H, HD = 8, 64
AW = H * HD
JH, ID = 4, 64
TOPK = 256
PAST, PAGE = 256, 128
SK = PAST + 1
STOPK = SK // 4
NB = 32
SW, GC, NG, ST = 512, 16, 32, 64
L = 8
NC = NP // L
FF = 4096
EPS = 1e-6
NOT_CAUSAL = -3.0e38
LATE_ROUNDS = 12
TAKEN = -3.4e38
HIDE = -1.0e30
Q0, K0, V0, QI0, KI0, U0, GA0, GS0 = 0, 512, 1024, 1536, 1792, 1860, 2372, 3396


def split3(pe, out, wh, wl, xh, xl, first, last):
    pe.matmul(out, wh, xh, start=first, stop=False)
    pe.matmul(out, wh, xl, start=False, stop=False)
    return pe.matmul(out, wl, xh, start=False, stop=last)


def project(pe, ps, slot, wh, wl, xh, xl, kt, m=P, first=True, last=True):
    for k in range(kt):
        for n, (w, x) in enumerate(((wh, xh), (wh, xl), (wl, xh))):
            for c in range(3):
                mm = pe.matmul(ps[0:m, 3 * slot + c, 0:CH], w[:, k, 0:m], x[:, k, c * CH:(c + 1) * CH],
                               start=(first and k == 0 and n == 0), stop=(last and k == kt - 1 and n == 2))
    return mm


def thirds(ps, slot, m=P):
    return ps[0:m, 3 * slot:3 * slot + 3, 0:CH]


def as_thirds(ap):
    return ap.rearrange("p (c t) -> p c t", c=3)


def newton_rstd(dve, rstd, std, var, done, base=0):
    dve.reciprocal(rstd[:, :], std[:, :]).then_inc(done, 1)
    dve.wait_ge(done, base + 1)
    dve.tensor_tensor(std[:, :], rstd[:, :], rstd[:, :], ALU.mult).then_inc(done, 1)
    dve.wait_ge(done, base + 2)
    dve.tensor_tensor(std[:, :], std[:, :], var[:, :], ALU.mult).then_inc(done, 1)
    dve.wait_ge(done, base + 3)
    dve.tensor_scalar(std[:, :], std[:, :], -0.5, 1.5, ALU.mult, ALU.add).then_inc(done, 1)
    dve.wait_ge(done, base + 4)
    dve.tensor_tensor(rstd[:, :], rstd[:, :], std[:, :], ALU.mult).then_inc(done, 1)
    dve.wait_ge(done, base + 5)


def phase_norm(nc, g):
    with ExitStack() as ctx:
        sb = lambda n, s, d=F32: ctx.enter_context(nc.sbuf_tensor(n, s, d))
        x_all = sb("n_x", [P, 9, D])
        gain = sb("n_gain", [P, D])
        junk = sb("n_junk", [P, D])
        xn = sb("n_xn", [P, 2, D])
        ss = sb("n_ss", [P, 9])
        var = sb("n_var", [P, 9])
        std = sb("n_std", [P, 9])
        rstd = sb("n_rstd", [P, 9])
        psf = g.ps[:, :, :].rearrange("p b c -> p (b c)")
        sem = g.sem
        groups = [(0, 3), (3, 6), (6, 9)]
        x_in = [sem(f"n_x_in{i}") for i in range(3)]
        gain_in, ident_in = sem("n_gain_in"), sem("n_ident_in")
        ss_zero, ss_done, var_done, std_done, rstd_done = (sem("n_" + s) for s in
                                                           ("ss_zero", "ss_done", "var_done", "std_done", "rstd_done"))
        xn_done, turned, hi_done, lo_done = (sem("n_" + s) for s in ("xn_done", "turned", "hi_done", "lo_done"))
        block = ctx.enter_context(nc.Block())

        @block.sync
        def _(sp):
            xv = g.x_prompt.rearrange("b (i p) d -> p (b i) d", p=P)
            sp.dma_start(gain[:, :], g.g_pre_mix.partition_broadcast(P)).then_inc(gain_in, 16)
            sp.dma_start(g.ident[:, :], g.c_ident).then_inc(ident_in, 16)
            for q, (a, b) in enumerate(groups):
                for i in range(a, min(b, NT)):
                    sp.dma_start(x_all[:, i, :], xv[:, i, :]).then_inc(x_in[q], 16)
            sp.dma_start(x_all[0:NS, 8, :], g.x_sample.rearrange("b t d -> (b t) d")).then_inc(x_in[2], 16)

        @block.scalar
        def _(act):
            def squares(q):
                a, b = groups[q]
                act.wait_ge(x_in[q], 16 * (b - a))
                for i in range(a, b):
                    n = TILES[i][1]
                    if i:
                        act.wait_ge(ss_done, i)
                    act.activation(junk[0:n, :], x_all[0:n, i, :], ACT.Square,
                                   accum_out=ss[0:n, i:i + 1]).then_inc(ss_done, 1)

            def root(q):
                a, b = groups[q]
                act.wait_ge(var_done, q + 1)
                act.activation(std[:, a:b], var[:, a:b], ACT.Sqrt).then_inc(std_done, 1)

            act.wait_ge(ss_zero, 1)
            squares(0)
            root(0)
            squares(1)
            for i, (t0, n) in enumerate(TILES):
                if i == 1:
                    squares(2)
                for q in (1, 2):
                    if i + 1 == groups[q][0]:
                        root(q)
                act.wait_ge(turned, i + 1)
                act.activation(g.hT_h[:, :, t0:t0 + n],
                               psf[:, (i % 2) * 1024:(i % 2) * 1024 + 1024].rearrange(
                                   "p (k t) -> p k t", k=KD)[:, :, 0:n], ACT.Copy).then_inc(hi_done, 1)

        @block.vector
        def _(dve):
            dve.memset(ss[:, :], 1.0).then_inc(ss_zero, 1)
            dve.wait_ge(gain_in, 16)

            def norms(q):
                a, b = groups[q]
                dve.wait_ge(ss_done, b)
                dve.tensor_scalar(var[:, a:b], ss[:, a:b], 1.0 / D, EPS, ALU.mult, ALU.add).then_inc(var_done, 1)
                dve.wait_ge(std_done, q + 1)
                newton_rstd(dve, rstd[:, a:b], std[:, a:b], var[:, a:b], rstd_done, 5 * q)

            def low_part(i):
                t0, n = TILES[i]
                dve.wait_ge(hi_done, i + 1)
                dve.tensor_tensor(g.hT_l[:, :, t0:t0 + n],
                                  psf[:, (i % 2) * 1024:(i % 2) * 1024 + 1024].rearrange(
                                      "p (k t) -> p k t", k=KD)[:, :, 0:n],
                                  g.hT_h[:, :, t0:t0 + n].bitcast(F32), ALU.subtract).then_inc(lo_done, 1)

            for i, (_, n) in enumerate(TILES):
                for q, (a, _) in enumerate(groups):
                    if i == a:
                        norms(q)
                if i >= 2:
                    dve.wait_ge(turned, i - 1)
                dve.scalar_tensor_tensor(out=xn[0:n, i % 2, :], in0=x_all[0:n, i, :], scalar=rstd[0:n, i:i + 1],
                                         in1=gain[0:n, :], op0=ALU.mult, op1=ALU.mult).then_inc(xn_done, 1)
                if i:
                    low_part(i - 1)
            low_part(8)

        @block.tensor
        def _(pe):
            pe.wait_ge(ident_in, 16)
            for i, (_, n) in enumerate(TILES):
                pe.wait_ge(xn_done, i + 1)
                if i >= 2:
                    pe.wait_ge(lo_done, i - 1)
                for k in range(KD):
                    o = (i % 2) * 1024 + k * P
                    mm = pe.transpose(psf[:, o:o + n], xn[0:n, i % 2, k * P:(k + 1) * P], g.ident[0:n, 0:n])
                mm.then_inc(turned, 1)


def phase_project(nc, g):
    with ExitStack() as ctx:
        sb = lambda n, s, d=F32: ctx.enter_context(nc.sbuf_tensor(n, s, d))
        ps, sem = g.ps, g.sem
        wst = sb("j_wst", [P, 2, KD, P])
        wh = sb("j_wh", [P, 2, KD, P], F32R)
        wl = sb("j_wl", [P, 2, KD, P], F32R)
        ring = sb("j_ring", [P, 2, T])
        tok = sb("j_tok", [P, 2, NT, P])
        tok_s = sb("j_tok_s", [NS, 3, AW])
        kvs = sb("j_kvs", [P, 3, 4, NS])
        kw_tok = sb("j_kw_tok", [P, 9, 68])
        rel = sb("j_rel", [P, 2, NP])
        m8 = sb("j_m8", [P, 8])
        nci = sb("j_nci", [P, P])
        g.par.place(tok[:, :, :, :].rearrange("p s i c -> p s (i c)"), ring[:, 0, :], ring[:, 1, :])
        psf = ps[:, :, :].rearrange("p b c -> p (b c)")

        units = [(QI0, P, "qi"), (QI0 + P, P, "qi"), (KI0, 68, "kw")]
        units += [(Q0 + m * P, P, "q") for m in range(4)]
        units += [(GA0 + m * P, P, "g") for m in range(4)]
        NLEAD = len(units)
        NLOOP = 12
        tail = [(base + m * P, P, kind) for base, kind in ((K0, "k"), (V0, "v"), (U0, "u")) for m in range(4)]
        NU = NLEAD + NLOOP + len(tail)
        TAIL0 = NLEAD + NLOOP
        GATE0 = 7

        w_in = [sem(f"j_w_in{i}") for i in range(2)]
        w_hi, w_lo, unit_done, evac = (sem("j_" + s) for s in ("w_hi", "w_lo", "unit_done", "evac"))
        gate_out = [sem(f"j_gate_out{i}") for i in range(2)]
        kw_turned, kw_copied, kw_out = sem("j_kw_turned"), sem("j_kw_copied"), sem("j_kw_out")
        s_done, rel_done, acc_done, dve_step = (sem("j_" + s) for s in ("s_done", "rel_done", "acc_done", "dve_step"))
        tok_turned, tok_copied, sam_turned, sam_copied = (sem("j_" + s) for s in
                                                          ("tok_turned", "tok_copied", "sam_turned", "sam_copied"))
        tok_out = [sem(f"j_tok_out{i}") for i in range(2)]
        sam_out, nci_in = sem("j_sam_out"), sem("j_nci_in")
        kvs_done = sem("j_kvs_done")
        block = ctx.enter_context(nc.Block())

        wv = g.w_in.rearrange("(k p) n -> p k n", p=P)
        scores = [(i, h) for i in range(2, NT) for h in range(JH)]
        SU = 4

        def scores_of(u):
            return [s for s in range(4 * (u - SU), 4 * (u - SU) + 4) if 0 <= s < len(scores)]

        def kvs_count(n):
            return n + 1 + min(n + 1, 4)

        @block.sync
        def _(sp):
            sp.dma_start(nci[:, :], g.c_not_causal).then_inc(nci_in, 16)

            def load_w(u, s, cols, n):
                sp.dma_start(wst[:, s, :, 0:n], cols).then_inc(w_in[s], 16)

            def gate_store(gt, u, s):
                sp.wait_ge(evac, u + 1)
                sp.dma_start(gt, ring[:, s, :]).then_inc(gate_out[s], 16)

            for u in range(NLEAD):
                if u >= 2:
                    sp.wait_ge(w_lo, u - 1)
                load_w(u, u % 2, wv[:, :, units[u][0]:units[u][0] + units[u][1]], units[u][1])
                if u == 0:
                    g.par.load_small(sp, g)
                if u == 1:
                    g.par.load_large(sp, g)
                if u - 1 >= GATE0:
                    gate_store(g.d_gates[:, u - 1 - GATE0, :], u - 1, (u - 1) % 2)
            with sp.Fori(0, NLOOP // 2) as j:
                for e in range(2):
                    u = NLEAD + e
                    sp.wait_ge(w_lo, j * 2 + (u - 1))
                    load_w(u, u % 2, wv[:, :, bass.ds(GA0 + 4 * P + j * (2 * P) + e * P, P)], P)
                    gate_store(g.d_gates[:, bass.ds(j * 2 + (u - 1 - GATE0), 1), :].rearrange("p a t -> p (a t)"),
                               j * 2 + (u - 1), (u - 1) % 2)
            outs = {"k": (g.k_prompt, g.k_sample, 0), "v": (g.v_prompt, g.v_sample, 1)}

            def tok_store(n):
                _, _, kind = tail[n]
                m = n % 4
                sp.wait_ge(tok_copied, n + 1)
                if kind == "u":
                    dst = g.d_u.rearrange("(k l) c -> k l c", l=L)[:, :, m * P:(m + 1) * P]
                else:
                    dst = outs[kind][0].rearrange("(i p) c -> p i c", p=P)[:, :, m * P:(m + 1) * P]
                sp.dma_start(dst, tok[:, n % 2, :, :]).then_inc(tok_out[n % 2], 16)
                if m == 3:
                    q = n // 4
                    sp.wait_ge(sam_copied, q + 1)
                    dst = g.d_us if kind == "u" else outs[kind][1]
                    sp.dma_start(dst, tok_s[:, q, :]).then_inc(sam_out, 16)

            for n in range(len(tail)):
                u = TAIL0 + n
                sp.wait_ge(w_lo, u - 1)
                load_w(u, u % 2, wv[:, :, tail[n][0]:tail[n][0] + P], P)
                if n == 0:
                    gate_store(g.d_gates[:, u - 1 - GATE0, :], u - 1, (u - 1) % 2)
                if n == 1:
                    sp.wait_ge(kw_copied, 2)
                    sp.dma_start(g.kidx_prompt.rearrange("(i p) c -> p i c", p=P),
                                 kw_tok[:, 0:NT, 0:ID]).then_inc(kw_out, 16)
                    sp.dma_start(g.kidx_sample, kw_tok[0:NS, NT, 0:ID]).then_inc(kw_out, 16)
                if n >= 2:
                    tok_store(n - 2)
            tok_store(len(tail) - 2)
            tok_store(len(tail) - 1)
            for s in range(2):
                sp.wait_ge(gate_out[s], 16 * 8)
                sp.wait_ge(tok_out[s], 16 * 6)
            sp.wait_ge(sam_out, 48)
            sp.wait_ge(kw_out, 32)

        @block.gpsimd
        def _(pool):
            def low(u, s, n):
                pool.wait_ge(w_hi, u + 1)
                pool.tensor_tensor(wl[:, s, :, 0:n], wst[:, s, :, 0:n], wh[:, s, :, 0:n].bitcast(F32),
                                   ALU.subtract).then_inc(w_lo, 1)
            for u in range(NLEAD):
                low(u, u % 2, units[u][1])
            with pool.Fori(0, NLOOP // 2) as j:
                for e in range(2):
                    low(j * 2 + (NLEAD + e), (NLEAD + e) % 2, P)
            for n in range(len(tail)):
                u = TAIL0 + n
                if n == 0:
                    low(u, u % 2, P)
                if n + 1 < len(tail):
                    low(u + 1, (u + 1) % 2, P)
                pool.wait_ge(evac, u + 1)
                if tail[n][2] == "k":
                    pool.tensor_copy(g.kT[:, n % 4, :], ring[:, u % 2, :]).then_inc(kvs_done, 1)
                pool.tensor_copy(kvs[:, n // 4, n % 4, :], ring[:, u % 2, NP:T]).then_inc(kvs_done, 1)

        @block.scalar
        def _(act):
            def high(u, s, n, half):
                act.wait_ge(w_in[s], half)
                if not isinstance(u, int) or u >= 2:
                    act.wait_ge(unit_done, u - 1)
                act.activation(wh[:, s, :, 0:n], wst[:, s, :, 0:n], ACT.Copy).then_inc(w_hi, 1)

            def relu(s):
                i, _ = scores[s]
                n = (i + 1) * P
                act.wait_ge(s_done, s + 1)
                if s >= 2:
                    act.wait_ge(acc_done, s - 1)
                act.activation(rel[:, s % 2, 0:n], psf[:, 6 * BANK:6 * BANK + n], ACT.Relu).then_inc(rel_done, 1)

            def gate_evac(u, s, uses):
                act.wait_ge(unit_done, u + 1)
                if uses is not None:
                    act.wait_ge(gate_out[s], uses)
                act.activation(as_thirds(ring[:, s, :]), thirds(ps, s), ACT.Sigmoid).then_inc(evac, 1)

            high(0, 0, P, 16)
            for u in range(NLEAD):
                col, n, kind = units[u]
                for s in scores_of(u)[0:2]:
                    relu(s)
                nxt = u + 1
                high(nxt, nxt % 2, units[nxt][1] if nxt < NLEAD else P, 16 * (nxt // 2 + 1))
                for s in scores_of(u)[2:]:
                    relu(s)
                if kind == "g":
                    if u == GATE0:
                        act.wait_ge(g.par.setup_done, 1)
                    gate_evac(u, u % 2, 16 * ((u - GATE0) // 2) if u - GATE0 >= 2 else None)
                    continue
                act.wait_ge(unit_done, u + 1)
                dst = {"qi": lambda: g.qiT[:, u, :], "kw": lambda: g.kwT[:, :], "q": lambda: g.qT[:, u - 3, :]}[kind]()
                if kind == "kw":
                    act.activation(as_thirds(g.kiT2[ID:P, :]), thirds(ps, u % 2, ID), ACT.Copy)
                act.activation(as_thirds(dst), thirds(ps, u % 2, n), ACT.Copy).then_inc(evac, 1)
                if u == 0:
                    g.par.sines(act)
                if u == 3:
                    act.wait_ge(kw_turned, 1)
                    act.activation(kw_tok[:, 0:7, :], ps[:, 6, 0:7 * 68].rearrange("p (i c) -> p i c", c=68),
                                   ACT.Copy).then_inc(kw_copied, 1)
                    act.activation(kw_tok[:, 7, :], ps[:, 7, 0:68], ACT.Copy)
                    act.activation(kw_tok[0:NS, 8, :], ps[0:NS, 7, 68:2 * 68], ACT.Copy).then_inc(kw_copied, 1)
            with act.Fori(0, NLOOP // 2) as j:
                for e in range(2):
                    u = NLEAD + e
                    nxt = u + 1
                    high(j * 2 + nxt, nxt % 2, P, j * 16 + 16 * (nxt // 2 + 1))
                    gate_evac(j * 2 + u, u % 2, j * 16 + 16 * ((u - GATE0) // 2))

            def tok_copy(n):
                act.wait_ge(tok_turned, n + 1)
                if n >= 2:
                    act.wait_ge(tok_out[n % 2], 16 * ((n - 2) // 2 + 1))
                act.activation(tok[:, n % 2, :, :].rearrange("p i c -> p (i c)"), psf[:, 6 * BANK:8 * BANK],
                               ACT.Copy).then_inc(tok_copied, 1)
                if n % 4 == 3:
                    q = n // 4
                    act.wait_ge(sam_turned, q + 1)
                    act.activation(tok_s[:, q, :], ps[0:NS, 6, 0:AW], ACT.Copy).then_inc(sam_copied, 1)

            for n in range(len(tail)):
                u = TAIL0 + n
                kind = tail[n][2]
                if n + 1 < len(tail):
                    high(u + 1, (u + 1) % 2, P, 16 * ((u + 1) // 2 + 1))
                act.wait_ge(unit_done, u + 1)
                if n < 2:
                    act.wait_ge(gate_out[u % 2], 16 * 8)
                if n >= 2:
                    act.wait_ge(tok_turned, n - 1)
                    act.wait_ge(kvs_done, kvs_count(n - 2))
                act.activation(as_thirds(ring[:, u % 2, :]), thirds(ps, u % 2), ACT.Copy).then_inc(evac, 1)
                if n:
                    tok_copy(n - 1)
            tok_copy(len(tail) - 1)

        @block.vector
        def _(dve):
            steps = [0]

            def step(ins):
                ins.then_inc(dve_step, 1)
                steps[0] += 1
                dve.wait_ge(dve_step, steps[0])

            at = [2, 0]

            def top_rounds(n, last):
                while n > 0 and at[0] <= last:
                    sc = g.mask[at[0] - 2]
                    rounds = TOPK // 8 - (LATE_ROUNDS if at[0] == NT - 1 else 0)
                    m = min(n, rounds - at[1])
                    for _ in range(m):
                        step(dve.max(m8[:, :], sc))
                        step(dve.match_replace(out=sc, in_to_replace=m8[:, :], in_values=sc, imm_value=TAKEN))
                    n -= m
                    at[1] += m
                    if at[1] == rounds:
                        if rounds == TOPK // 8:
                            step(dve.tensor_scalar(sc, sc, -3.2e38, HIDE, ALU.is_gt, ALU.mult))
                        at[0] += 1
                        at[1] = 0

            g.par.discretise(dve, g)
            dve.wait_ge(kw_copied, 2)
            dve.wait_ge(nci_in, 16)
            for s, (i, h) in enumerate(scores):
                sc, n = g.mask[i - 2], (i + 1) * P
                w = kw_tok[:, i, ID + h:ID + h + 1]
                dve.wait_ge(rel_done, s + 1)
                if h == 0:
                    ins = dve.tensor_scalar(sc, rel[:, s % 2, 0:n], w, None, ALU.mult)
                else:
                    ins = dve.scalar_tensor_tensor(out=sc, in0=rel[:, s % 2, 0:n], scalar=w, in1=sc,
                                                   op0=ALU.mult, op1=ALU.add)
                ins.then_inc(acc_done, 1)
                dve.wait_ge(acc_done, s + 1)
                if h == JH - 1:
                    step(dve.scalar_tensor_tensor(out=sc[:, i * P:n], in0=nci[:, :], scalar=NOT_CAUSAL,
                                                  in1=sc[:, i * P:n], op0=ALU.mult, op1=ALU.add))
                top_rounds(2, i if h == JH - 1 else i - 1)
            top_rounds(10 ** 6, NT - 1)

        @block.tensor
        def _(pe):
            def unit(u, s, n):
                pe.wait_ge(w_lo, u + 1)
                if not isinstance(u, int) or u >= 2:
                    pe.wait_ge(evac, u - 1)
                for k in range(KD):
                    if isinstance(u, int) and k % 2 == 0 and k // 2 < len(scores_of(u)):
                        score(scores_of(u)[k // 2])
                    for q, (w, x) in enumerate(((wh, g.hT_h), (wh, g.hT_l), (wl, g.hT_h))):
                        for c in range(3):
                            mm = pe.matmul(ps[0:n, 3 * s + c, 0:CH], w[:, s, k, 0:n], x[:, k, c * CH:(c + 1) * CH],
                                           start=(k == 0 and q == 0), stop=(k == KD - 1 and q == 2))
                mm.then_inc(unit_done, 1)

            def score(s):
                i, h = scores[s]
                if s >= 1:
                    pe.wait_ge(rel_done, s)
                else:
                    pe.wait_ge(kw_copied, 2)
                r = (h % 2) * ID
                keys = g.kwT if h % 2 == 0 else g.kiT2
                for c in range(0, (i + 1) * P, BANK):
                    n = min(BANK, (i + 1) * P - c)
                    mm = pe.matmul(psf[:, 6 * BANK + c:6 * BANK + c + n], g.qiT[r:r + ID, h // 2, i * P:(i + 1) * P],
                                   keys[r:r + ID, c:c + n], start=True, stop=True)
                mm.then_inc(s_done, 1)

            g.par.turn_lambda(pe, g)
            for u in range(NLEAD):
                unit(u, u % 2, units[u][1])
                if u == 0:
                    g.par.turn_c(pe, g)
                if u == 3:
                    pe.wait_ge(g.par.c_copied, 2)
                    pe.wait_ge(evac, 3)
                    for i, (t0, n) in enumerate(TILES):
                        o = (6 if i < 7 else 7) * BANK + (i if i < 7 else i - 7) * 68
                        mm = pe.transpose(psf[0:n, o:o + 68], g.kwT[:, t0:t0 + n], g.ident[0:68, 0:68])
                    mm.then_inc(kw_turned, 1)
            with pe.Fori(0, NLOOP // 2) as j:
                for e in range(2):
                    unit(j * 2 + (NLEAD + e), (NLEAD + e) % 2, P)

            def turn(n):
                u = TAIL0 + n
                kind = tail[n][2]
                pe.wait_ge(evac, u + 1)
                if n >= 1:
                    pe.wait_ge(tok_copied, n)
                    if n % 4 == 0:
                        pe.wait_ge(sam_copied, n // 4)
                else:
                    pe.wait_ge(rel_done, len(scores))
                for i in range(NT):
                    src = ring[:, u % 2, i:NP:L] if kind == "u" else ring[:, u % 2, i * P:(i + 1) * P]
                    o = 6 * BANK + i * P
                    mm = pe.transpose(psf[:, o:o + P], src, g.ident[:, :])
                mm.then_inc(tok_turned, 1)
                if n % 4 == 3:
                    pe.wait_ge(tok_copied, n + 1)
                    pe.wait_ge(kvs_done, kvs_count(n))
                    for m in range(4):
                        mm = pe.transpose(ps[0:NS, 6, m * P:(m + 1) * P], kvs[:, n // 4, m, :], g.ident[:, :])
                    mm.then_inc(sam_turned, 1)

            for n in range(len(tail)):
                u = TAIL0 + n
                unit(u, u % 2, P)
                if n:
                    turn(n - 1)
            turn(len(tail) - 1)


def over(ap, n):
    return ap.unsqueeze(len(ap.shape)).broadcast_to([*ap.shape, n])


def mid(ap, n):
    p, gg, c = ap.shape
    return ap.unsqueeze(2).broadcast_to([p, gg, n, c])


class SsmParameters:

    def __init__(self, nc, stack, sem):
        sb = lambda n, s, d=F32: stack.enter_context(nc.sbuf_tensor("r_" + n, s, d, side="right"))
        self.sgn, self.swap = sb("sgn", [P, 1]), sb("swap", [P, P])
        self.bb_x, self.bb_s = sb("bb_x", [P, NG, GC]), sb("bb_s", [P, NG, GC])
        self.c_x, self.c_s = sb("c_x", [P, NG, GC]), sb("c_s", [P, NG, GC])
        self.pr, self.pi = sb("pr", [P, NG, L + 1]), sb("pi", [P, NG, L + 1])
        self.qr, self.qi = sb("qr", [P, NG, L]), sb("qi", [P, NG, L])
        self.wr, self.wi = sb("wr", [P, NG]), sb("wi", [P, NG])
        self.rad = sb("rad", [P, NG])
        self.dsk = sb("dsk", [GC, NG])
        self.lr, self.li, self.dt = sb("lr", [P, NG]), sb("li", [P, NG]), sb("dt", [P, NG])
        self.ki = sb("ki", [P, NG], I32)
        (self.par_in, self.bc_in, self.lam_turned, self.lam_copied, self.c_turned, self.c_copied, self.act_par,
         self.dve_par, self.steps, self.setup_done) = (sem("r_" + n) for n in (
             "par_in", "bc_in", "lam_turned", "lam_copied", "c_turned", "c_copied", "act_par", "dve_par", "steps",
             "setup_done"))

    def place(self, big, small, wide):
        self.c_st = big[:, 0, :].rearrange("p (q a c) -> p q a c", q=2, a=4)
        self.b_x = big[:, 1, 0:NG * GC].rearrange("p (g c) -> p g c", c=GC)
        self.b_s = big[:, 1, NG * GC:2 * NG * GC].rearrange("p (g c) -> p g c", c=GC)
        self.v = small[:, 0:16 * NG].rearrange("p (n g) -> p n g", g=NG)
        self.bt = small[:, 16 * NG:16 * NG + NG * GC].rearrange("p (g c) -> p g c", c=GC)
        self.lam_st = wide[0:NG, 0:4 * ST].rearrange("g (q a p) -> g q a p", q=2, a=2)
        self.t1, self.t2 = (wide[:, (2 + n) * P:(3 + n) * P].rearrange("p (g l) -> p g l", g=NG) for n in range(2))

    def value(self, n):
        return self.v[:, n, :]

    def load_small(self, sp, g):
        for q, src in enumerate((g.lam_re, g.lam_im)):
            for half in range(2):
                sp.dma_start(self.lam_st[:, q, half, :], src).then_inc(self.par_in, 16)
        sp.dma_start(self.dt[:, :], g.log_dt.partition_broadcast(P)).then_inc(self.par_in, 16)
        sp.dma_start(self.sgn[:, :], g.c_sign).then_inc(self.par_in, 16)
        sp.dma_start(self.swap[:, :], g.c_swap).then_inc(self.par_in, 16)
        sp.dma_start(self.dsk[:, :], g.d_skip.rearrange("(g c) -> c g", c=GC),
                     allow_slow_non_contiguous=True).then_inc(self.par_in, 16)

    def load_large(self, sp, g):
        for dst, lo_, hi_ in ((self.b_x, g.b_re, g.b_im), (self.b_s, g.b_im, g.b_re)):
            sp.dma_start(dst[0:ST, :, :], lo_.rearrange("g p c -> p g c")).then_inc(self.bc_in, 16)
            sp.dma_start(dst[ST:P, :, :], hi_.rearrange("g p c -> p g c")).then_inc(self.bc_in, 16)
        for q, (lo_, hi_) in enumerate(((g.c_re, g.c_im), (g.c_im, g.c_re))):
            for half, src in enumerate((lo_, hi_)):
                sp.dma_start(self.c_st[:, q, :, half * ST:(half + 1) * ST],
                             src.rearrange("(a g) c p -> (g c) a p", a=4)).then_inc(self.bc_in, 16)

    def sines(self, act):
        act.wait_ge(self.dve_par, 1)
        act.activation(self.value(8), self.value(6), ACT.Sin).then_inc(self.act_par, 1)
        act.activation(self.value(9), self.value(6), ACT.Sin, scale=0.5).then_inc(self.act_par, 1)

    def turn_lambda(self, pe, g):
        ps = g.ps
        pe.wait_ge(self.par_in, 16 * 8)
        for q in range(2):
            mm = pe.transpose(ps[:, 6, q * NG:(q + 1) * NG], self.lam_st[:, q, :, :].rearrange("g a p -> g (a p)"),
                              g.ident[0:NG, 0:NG])
        mm.then_inc(self.lam_turned, 1)

    def turn_c(self, pe, g):
        ps = g.ps
        pe.wait_ge(self.bc_in, 16 * 8)
        pe.wait_ge(self.lam_copied, 1)
        for q in range(2):
            for a in range(4):
                mm = pe.transpose(ps[:, 7 - q, a * P:(a + 1) * P], self.c_st[:, q, a, :], g.ident[:, :])
        mm.then_inc(self.c_turned, 1)

    def discretise(self, dve, g):
        ps, steps = g.ps, [0]

        def step(ins):
            ins.then_inc(self.steps, 1)
            steps[0] += 1
            dve.wait_ge(self.steps, steps[0])

        def tt(out, a, b, op=ALU.mult):
            step(dve.tensor_tensor(out, a, b, op))

        def tsc(out, a, s1, s2, op0, op1=ALU.bypass):
            step(dve.tensor_scalar(out, a, s1, s2, op0, op1))

        def stt(out, a, s, b, op0, op1):
            step(dve.scalar_tensor_tensor(out=out, in0=a, scalar=s, in1=b, op0=op0, op1=op1))

        def rounded(out, x, per):
            tsc(out, x, 1.0 / per, 12582912.0, ALU.mult, ALU.add)
            tsc(out, out, -12582912.0, None, ALU.add)

        def exp_parts(x, em, two_k, n, tmp):
            rounded(n, x, math.log(2.0))
            tsc(n, n, 126.0, -126.0, ALU.min, ALU.max)
            stt(tmp, n, -0.693359375, x, ALU.mult, ALU.add)
            stt(tmp, n, 2.12194440e-4, tmp, ALU.mult, ALU.add)
            tsc(tmp, tmp, 40.0, -40.0, ALU.min, ALU.max)
            tsc(em, tmp, 1 / 5040.0, 1 / 720.0, ALU.mult, ALU.add)
            for c in (1 / 120.0, 1 / 24.0, 1 / 6.0, 0.5, 1.0):
                tt(em, em, tmp)
                tsc(em, em, c, None, ALU.add)
            tt(em, em, tmp)
            tsc(self.ki[:, :], n, 127.0, None, ALU.add)
            step(dve.tensor_scalar(two_k.bitcast(I32), self.ki[:, :], 23, None, ALU.logical_shift_left))

        dve.wait_ge(self.lam_turned, 1)
        step(dve.tensor_copy(self.lr[:, :], ps[:, 6, 0:NG]))
        dve.tensor_copy(self.li[:, :], ps[:, 6, NG:2 * NG]).then_inc(self.lam_copied, 1)
        dve.wait_ge(self.lam_copied, 1)
        dve.wait_ge(self.par_in, 16 * 8)
        exp_parts(self.dt[:, :], self.value(0), self.value(1), self.value(2), self.value(3))
        stt(self.dt[:, :], self.value(0), 1.0, self.value(1), ALU.add, ALU.mult)
        tt(self.value(4), self.lr[:, :], self.dt[:, :])
        tt(self.value(5), self.li[:, :], self.dt[:, :])
        rounded(self.value(7), self.value(5), 2 * math.pi)
        stt(self.value(6), self.value(7), -6.28125, self.value(5), ALU.mult, ALU.add)
        stt(self.value(6), self.value(7), -0.0019350051879882812, self.value(6), ALU.mult, ALU.add)
        stt(self.value(6), self.value(7), -3.019916e-07, self.value(6), ALU.mult, ALU.add)
        dve.tensor_scalar(self.value(6), self.value(6), 3.141592, -3.141592, ALU.min, ALU.max).then_inc(self.dve_par, 1)
        exp_parts(self.value(4), self.value(0), self.value(1), self.value(2), self.value(3))
        dve.wait_ge(self.act_par, 2)
        tt(self.value(9), self.value(9), self.value(9))
        tsc(self.value(9), self.value(9), -2.0, None, ALU.mult)
        tsc(self.value(10), self.value(9), 1.0, None, ALU.add)
        tsc(self.value(11), self.value(1), -1.0, None, ALU.add)
        tt(self.value(12), self.value(0), self.value(1))
        tt(self.value(12), self.value(12), self.value(11), ALU.add)
        tsc(self.value(13), self.value(12), 1.0, None, ALU.add)
        tt(self.value(14), self.value(12), self.value(10))
        tt(self.value(14), self.value(14), self.value(9), ALU.add)
        tt(self.value(15), self.value(13), self.value(8))
        tt(self.value(0), self.lr[:, :], self.lr[:, :])
        tt(self.value(1), self.li[:, :], self.li[:, :])
        tt(self.value(0), self.value(0), self.value(1), ALU.add)
        step(dve.reciprocal(self.value(1), self.value(0)))
        tt(self.value(2), self.value(14), self.lr[:, :])
        tt(self.value(3), self.value(15), self.li[:, :])
        tt(self.value(2), self.value(2), self.value(3), ALU.add)
        tt(self.value(2), self.value(2), self.value(1))
        tt(self.value(3), self.value(15), self.lr[:, :])
        tt(self.value(4), self.value(14), self.li[:, :])
        tt(self.value(3), self.value(3), self.value(4), ALU.subtract)
        tt(self.value(3), self.value(3), self.value(1))
        tsc(self.value(3), self.value(3), self.sgn[:, 0:1], None, ALU.mult)
        dve.wait_ge(self.bc_in, 16 * 8)
        cr, ci = over(self.value(2), GC), over(self.value(3), GC)
        tt(self.bb_x[:, :, :], self.b_x[:, :, :], cr)
        tt(self.bt[:, :, :], self.b_s[:, :, :], ci)
        tt(self.bb_x[:, :, :], self.bb_x[:, :, :], self.bt[:, :, :], ALU.add)
        tt(self.bb_s[:, :, :], self.b_s[:, :, :], cr)
        tt(self.bt[:, :, :], self.b_x[:, :, :], ci)
        tt(self.bb_s[:, :, :], self.bb_s[:, :, :], self.bt[:, :, :], ALU.subtract)
        dve.wait_ge(self.c_turned, 1)
        for dst, bank in ((self.c_x, 7), (self.c_s, 6)):
            dve.tensor_scalar(dst[:, :, :].rearrange("p g c -> p (g c)"), ps[:, bank, :], self.sgn[:, 0:1], -1.0,
                              ALU.mult, ALU.mult).then_inc(self.c_copied, 1)
        step(dve.memset(self.pr[:, :, 0:1], 1.0))
        step(dve.memset(self.pi[:, :, 0:1], 0.0))
        tsc(self.pr[:, :, 1:2], self.value(14).unsqueeze(2), 1.0, None, ALU.add)
        tsc(self.pi[:, :, 1:2], self.value(15).unsqueeze(2), self.sgn[:, 0:1], None, ALU.mult)

        def double(re, im, n, fr, fi, a, b):
            tt(a, re[:, :, 1:n + 1], fr)
            tt(b, im[:, :, 1:n + 1], fi)
            tt(re[:, :, n + 1:2 * n + 1], a, b, ALU.subtract)
            tt(a, im[:, :, 1:n + 1], fr)
            tt(b, re[:, :, 1:n + 1], fi)
            tt(im[:, :, n + 1:2 * n + 1], a, b, ALU.add)

        for n in (1, 2, 4):
            double(self.pr, self.pi, n, self.pr[:, :, n:n + 1].broadcast_to([P, NG, n]),
                   self.pi[:, :, n:n + 1].broadcast_to([P, NG, n]), self.t1[:, :, 0:n], self.t2[:, :, 0:n])
        for l in range(L):
            step(dve.tensor_copy(self.qr[:, :, l:l + 1], self.pr[:, :, L - 1 - l:L - l]))
            step(dve.tensor_copy(self.qi[:, :, l:l + 1], self.pi[:, :, L - 1 - l:L - l]))
        step(dve.tensor_copy(self.wr[:, :], self.value(10)))
        tsc(self.wi[:, :], self.value(8), self.sgn[:, 0:1], None, ALU.mult)
        step(dve.tensor_copy(self.rad[:, :], self.value(13)))
        for _ in range(3):
            tt(self.value(0), self.wr[:, :], self.wr[:, :])
            tt(self.value(1), self.wi[:, :], self.wi[:, :])
            tt(self.value(2), self.wr[:, :], self.wi[:, :])
            tt(self.wr[:, :], self.value(0), self.value(1), ALU.subtract)
            tsc(self.wi[:, :], self.value(2), 2.0, None, ALU.mult)
            tt(self.rad[:, :], self.rad[:, :], self.rad[:, :])
        dve.tensor_copy(self.li[:, :], self.rad[:, :]).then_inc(self.setup_done, 1)


def phase_ssm(nc, g):
    GB, NBATCH = 8, NG // 8
    US0 = 32
    with ExitStack() as ctx:
        sb = lambda n, s, d=F32: ctx.enter_context(nc.sbuf_tensor("s_" + n, s, d))
        ps, sem0 = g.ps, g.sem
        sem = lambda n: sem0("s_" + n)
        psf = ps[:, :, :].rearrange("p b c -> p (b c)")
        par = g.par
        bb_x, c_x, c_s, bb_s = par.bb_x, par.c_x, par.c_s, par.bb_s
        pr, pi, qr, qi, wr, wi, rad, dsk, swap = par.pr, par.pi, par.qr, par.qi, par.wr, par.wi, par.rad, par.dsk, par.swap
        u_tok, us_tok = sb("u_tok", [P, L, P]), sb("us_tok", [NS, P])
        u_grp = sb("u_grp", [P, GB, L, GC])
        u = sb("u", [P, 2, GB, P + NS])
        bl, cl = sb("bl", [P, 2, GB, L, GC]), sb("cl", [P, 2, GB, L + 1, GC])
        ta = sb("ta", [P, GB, L + 1, GC])
        bst = sb("bst", [P, GB, P])
        low = sb("low", [P, GB, L, GC])
        kt, us_grp = low[0:GC, :, :, :], low[US0:US0 + NS, :, :, :]
        skip = sb("skip", [GC, GB, GC])
        mi = sb("mi", [P, 2, GB, P])
        tc, ts = sb("tc", [P, NG, NC]), sb("ts", [P, NG, NC])
        xin, xin_s = sb("xin", [P, GB, P]), sb("xin_s", [P, NG, NS])
        z, tb = sb("z", [P, GB, NC]), sb("tb", [P, GB, NC])
        xall = sb("xall", [P, GB, NC + 1])
        t3, t4 = tb[:, 0:GB // 2, :], tb[:, GB // 2:, :]
        x_last = sb("x_last", [P, NG])
        x0, x0s, x1 = (sb(n, [P, NS, NG]) for n in ("x0", "x0s", "x1"))
        xlt = sb("xlt", [NG, P])
        y, ys = sb("y", [P, L, P]), sb("ys", [NS, P])
        st = y[:, 0:4, :].rearrange("p (t q) c -> p t q c", t=2)
        x1t = xin[:, 0:2, :]

        zeroed, u_in, st_in, u_grouped, bl_ready, cl_ready, kt_ready = (
            sem(n) for n in ("zeroed", "u_in", "st_in", "u_grouped", "bl_ready", "cl_ready", "kt_ready"))
        st_turned, st_copied, u_turned, u_copied, b_turned, b_copied, kt_done, kt_copied = (
            sem(n) for n in ("st_turned", "st_copied", "u_turned", "u_copied", "b_turned", "b_copied", "kt_done", "kt_copied"))
        xin_done, xin_copied, xs_done, z_ready, zs_done, x_ready, x1_ready = (
            sem(n) for n in ("xin_done", "xin_copied", "xs_done", "z_ready", "zs_done", "x_ready", "x1_ready"))
        y_done, y_gelu, y_turned, y_copied, last_turned, last_copied, last_out = (
            sem(n) for n in ("y_done", "y_gelu", "y_turned", "y_copied", "last_turned", "last_copied", "last_out"))
        mi_in = [sem(f"mi_in{i}") for i in range(2)]
        dv, pv = sem("dve_step"), sem("pool_step")
        block = ctx.enter_context(nc.Block())

        @block.sync
        def _(sp):
            uv = g.d_u.rearrange("(k l) c -> k l c", l=L)

            def load_u(b):
                if b:
                    sp.wait_ge(u_grouped, b)
                cs = slice(b * P, (b + 1) * P)
                sp.dma_start(u_tok[:, :, :], uv[:, :, cs]).then_inc(u_in, 16)
                sp.dma_start(us_tok[:, :], g.d_us[:, cs]).then_inc(u_in, 16)

            load_u(0)
            for q, parts in enumerate(((g.state_re, g.state_im), (g.state_im, g.state_re))):
                for half, src in enumerate(parts):
                    rows = src.rearrange("s g p -> (s g) p").rearrange("(t r) p -> r t p", r=P)
                    sp.dma_start(st[:, :, q, half * ST:(half + 1) * ST], rows).then_inc(st_in, 16)
            sp.wait_ge(zeroed, 1)
            for b in range(NBATCH):
                if b + 1 < NBATCH:
                    load_u(b + 1)
                sp.wait_ge(kt_ready, b + 1)
                if b >= 2:
                    sp.wait_ge(y_done, b - 1)
                for l in range(L):
                    sp.dma_start(mi[l * GC:(l + 1) * GC, b % 2, :, l * GC:P],
                                 kt[:, :, 0:L - l, :].rearrange("c g l d -> c g (l d)")).then_inc(mi_in[b % 2], 16)
            sp.wait_ge(last_copied, 1)
            for half, (pd, sd) in enumerate(((g.ssm_re_prompt, g.ssm_re_sample), (g.ssm_im_prompt, g.ssm_im_sample))):
                cs = slice(half * ST, (half + 1) * ST)
                sp.dma_start(pd, xlt[:, cs]).then_inc(last_out, 16)
                sp.dma_start(sd.rearrange("s g p -> (s g) p").rearrange("(t r) p -> r t p", r=P),
                             x1t[:, :, cs]).then_inc(last_out, 16)
            sp.wait_ge(last_out, 16 * 4)

        @block.gpsimd
        def _(pool):
            steps = [0]

            def step(ins):
                ins.then_inc(pv, 1)
                steps[0] += 1
                pool.wait_ge(pv, steps[0])

            def group(b):
                pool.wait_ge(u_in, 32 * (b + 1))
                if b:
                    pool.wait_ge(u_turned, b)
                step(pool.tensor_copy(us_grp[:, :, L - 1, :], us_tok[:, :].rearrange("p (g c) -> p g c", c=GC)))
                pool.tensor_copy(u_grp[:, :, :, :],
                                 u_tok[:, :, :].rearrange("p l (g c) -> p g l c", c=GC)).then_inc(u_grouped, 1)

            def input_weights(b):
                gs, s = slice(b * GB, (b + 1) * GB), b % 2
                if b >= 2:
                    pool.wait_ge(b_turned, b - 1)
                step(pool.tensor_tensor(bl[:, s, :, :, :], over(qr[:, gs, :], GC), mid(bb_x[:, gs, :], L), ALU.mult))
                step(pool.tensor_tensor(ta[:, :, 0:L, :], over(qi[:, gs, :], GC), mid(bb_s[:, gs, :], L), ALU.mult))
                pool.tensor_tensor(bl[:, s, :, :, :], bl[:, s, :, :, :], ta[:, :, 0:L, :], ALU.add).then_inc(bl_ready, 1)
                pool.wait_ge(bl_ready, b + 1)

            def output_weights(b):
                gs, s = slice(b * GB, (b + 1) * GB), b % 2
                if b >= 2:
                    pool.wait_ge(y_done, b - 1)
                step(pool.tensor_tensor(cl[:, s, :, :, :], over(pr[:, gs, :], GC), mid(c_x[:, gs, :], L + 1), ALU.mult))
                step(pool.tensor_tensor(ta[:, :, :, :], over(pi[:, gs, :], GC), mid(c_s[:, gs, :], L + 1), ALU.mult))
                pool.tensor_tensor(cl[:, s, :, :, :], cl[:, s, :, :, :], ta[:, :, :, :], ALU.add).then_inc(cl_ready, 1)
                pool.wait_ge(cl_ready, b + 1)

            def skip_weights(b):
                gs = slice(b * GB, (b + 1) * GB)
                step(pool.tensor_tensor(skip[:, :, :], g.ident[0:GC, 0:GC].unsqueeze(1).broadcast_to([GC, GB, GC]),
                                        over(dsk[:, gs], GC), ALU.mult))
                pool.wait_ge(kt_copied, b + 1)
                pool.tensor_tensor(kt[:, :, 0, :], kt[:, :, 0, :], skip[:, :, :], ALU.add).then_inc(kt_ready, 1)
                pool.wait_ge(kt_ready, b + 1)

            step(pool.memset(us_grp[:, :, :, :], 0.0))
            input_weights(0)
            group(0)
            output_weights(0)
            pool.memset(mi[:, :, :, :], 0.0).then_inc(zeroed, 1)
            input_weights(1)
            for b in range(NBATCH):
                skip_weights(b)
                if b + 1 < NBATCH:
                    group(b + 1)
                    output_weights(b + 1)
                if b + 2 < NBATCH:
                    input_weights(b + 2)

        @block.scalar
        def _(act):
            def b_copy(b):
                act.wait_ge(b_turned, b + 1)
                if b:
                    act.wait_ge(xin_done, b)
                act.activation(bst[:, :, :].rearrange("p g k -> p (g k)"), psf[:, 4 * BANK:6 * BANK],
                               ACT.Copy).then_inc(b_copied, 1)

            def u_copy(b):
                act.wait_ge(u_turned, b + 1)
                if b >= 2:
                    act.wait_ge(y_done, b - 1)
                for h in range(2):
                    act.activation(u[:, b % 2, 4 * h:4 * h + 4, 0:P], ps[:, 4 + h, :].rearrange("p (g k) -> p g k", g=4),
                                   ACT.Copy)
                act.activation(u[:, b % 2, :, P:P + NS], ps[:, 6, 0:GB * NS].rearrange("p (g k) -> p g k", g=GB),
                               ACT.Copy).then_inc(u_copied, 1)

            act.wait_ge(st_turned, 1)
            for q, dst in enumerate((x0, x0s)):
                ins = act.activation(dst[:, :, :].rearrange("p s g -> p (s g)"), ps[:, 7, q * 2 * P:(q + 1) * 2 * P], ACT.Copy)
            ins.then_inc(st_copied, 1)
            b_copy(0)
            u_copy(0)
            for b in range(NBATCH):
                act.wait_ge(xin_done, b + 1)
                if b:
                    act.wait_ge(z_ready, b)
                    act.wait_ge(xs_done, b)
                for h in range(2):
                    act.activation(xin[:, 4 * h:4 * h + 4, :], ps[:, h, :].rearrange("p (g k) -> p g k", g=4), ACT.Copy)
                act.activation(xin_s[:, b * GB:(b + 1) * GB, :], ps[:, 7, 0:GB * NS].rearrange("p (g k) -> p g k", g=GB),
                               ACT.Copy).then_inc(xin_copied, 1)
                act.wait_ge(kt_done, b + 1)
                if b:
                    act.wait_ge(mi_in[(b - 1) % 2], 16 * L * ((b - 1) // 2 + 1))
                act.activation(kt[:, :, :, :].rearrange("c g l d -> c (g l d)"), psf[0:GC, 4 * BANK:6 * BANK],
                               ACT.Copy).then_inc(kt_copied, 1)
                if b + 1 < NBATCH:
                    b_copy(b + 1)
                    u_copy(b + 1)
                act.wait_ge(y_done, b + 1)
                if b:
                    act.wait_ge(y_turned, b)
                for h in range(2):
                    act.activation(y[:, :, h * 64:(h + 1) * 64].rearrange("p l (g c) -> p g l c", c=GC),
                                   ps[:, 2 + h, :].rearrange("p (g l c) -> p g l c", g=4, l=L), ACT.Gelu_apprx_tanh)
                act.activation(ys[:, :], ps[0:NS, 7, 0:P], ACT.Gelu_apprx_tanh).then_inc(y_gelu, 1)
                act.wait_ge(y_turned, b + 1)
                act.activation(g.gT[:, b, 0:NP].rearrange("p (k l) -> p l k", l=L),
                               psf[:, 0:2 * BANK].rearrange("p (l k) -> p l k", l=L), ACT.Copy)
                act.activation(g.gT[:, b, NP:T], ps[:, 7, 0:NS], ACT.Copy).then_inc(y_copied, 1)
            act.wait_ge(last_turned, 1)
            act.activation(xlt[:, :], ps[0:NG, 4, 0:P], ACT.Copy)
            act.activation(x1t[:, :, :].rearrange("p t c -> p (t c)"), ps[:, 5, 0:2 * P], ACT.Copy).then_inc(last_copied, 1)

        @block.vector
        def _(dve):
            steps = [0]

            def step(ins):
                ins.then_inc(dv, 1)
                steps[0] += 1
                dve.wait_ge(dv, steps[0])

            def tt(out, a, b, op=ALU.mult):
                step(dve.tensor_tensor(out, a, b, op))

            def phasors(gs, first, last):
                tcs, tss = tc[:, gs, :], ts[:, gs, :]
                n, ng = first, gs.stop - gs.start
                while n <= last:
                    m = min(n, NC - 1 - n)
                    fr, fi = (a[:, :, n:n + 1].broadcast_to([P, ng, m]) for a in (tcs, tss))
                    a, b = (t[:, :, :].rearrange("p g c -> p (g c)")[:, 0:ng * m].rearrange("p (g c) -> p g c", g=ng)
                            for t in (t3, t4))
                    tt(a, tcs[:, :, 1:m + 1], fr)
                    tt(b, tss[:, :, 1:m + 1], fi)
                    tt(tcs[:, :, n + 1:n + m + 1], a, b, ALU.subtract)
                    tt(a, tss[:, :, 1:m + 1], fr)
                    tt(b, tcs[:, :, 1:m + 1], fi)
                    tt(tss[:, :, n + 1:n + m + 1], a, b, ALU.add)
                    n *= 2

            def batch(b):
                return slice(b * GB, (b + 1) * GB)

            step(dve.memset(tc[:, :, 0:1], 1.0))
            step(dve.memset(ts[:, :, 0:1], 0.0))
            step(dve.tensor_copy(tc[:, :, 1:2], wr[:, :].unsqueeze(2)))
            step(dve.tensor_copy(ts[:, :, 1:2], wi[:, :].unsqueeze(2)))
            phasors(slice(0, NG), 1, 8)
            phasors(batch(0), 16, NC // 2)
            for b in range(NBATCH):
                tcs, tss = tc[:, batch(b), :], ts[:, batch(b), :]
                dve.wait_ge(xin_copied, b + 1)
                tt(z[:, :, :], xin[:, :, :], tcs)
                dve.wait_ge(xs_done, b + 1)
                tt(tb[:, :, :], psf[:, 2 * BANK:4 * BANK].rearrange("p (g k) -> p g k", g=GB), tss)
                tt(z[:, :, :], z[:, :, :], tb[:, :, :], ALU.subtract)
                for q in range(GB):
                    r = rad[:, b * GB + q:b * GB + q + 1].broadcast_to([P, NC])
                    ins = dve.tensor_tensor_scan(z[:, q, :], r, z[:, q, :], 0.0, ALU.mult, ALU.add)
                ins.then_inc(z_ready, 1)
                if b + 1 < NBATCH:
                    phasors(batch(b + 1), 16, 16)
                dve.wait_ge(z_ready, b + 1)
                if b:
                    dve.wait_ge(y_done, b)
                step(dve.memset(xall[:, :, 0:1], 0.0))
                tt(xall[:, :, 1:NC + 1], z[:, :, :], tcs)
                dve.wait_ge(zs_done, b + 1)
                tt(tb[:, :, :], psf[:, 0:2 * BANK].rearrange("p (g k) -> p g k", g=GB), tss)
                dve.tensor_tensor(xall[:, :, 1:NC + 1], xall[:, :, 1:NC + 1], tb[:, :, :], ALU.add).then_inc(x_ready, 1)
                dve.wait_ge(x_ready, b + 1)
                step(dve.tensor_copy(x_last[:, b * GB:(b + 1) * GB].unsqueeze(2), xall[:, :, NC:NC + 1]))
                if b + 1 < NBATCH:
                    phasors(batch(b + 1), 32, NC // 2)
            dve.wait_ge(st_copied, 1)
            tbs = tb[:, 0:2, :].rearrange("p a c -> p (a c)").rearrange("p (s g) -> p s g", g=NG)
            tt(x1[:, :, :], x0[:, :, :], pr[:, :, 1].unsqueeze(1).broadcast_to([P, NS, NG]))
            tt(tbs, x0s[:, :, :], pi[:, :, 1].unsqueeze(1).broadcast_to([P, NS, NG]))
            tt(x1[:, :, :], x1[:, :, :], tbs, ALU.add)
            dve.tensor_tensor(x1[:, :, :], x1[:, :, :], xin_s[:, :, :].rearrange("p g b -> p b g"),
                              ALU.add).then_inc(x1_ready, 1)

        @block.tensor
        def _(pe):
            def b_turn(b):
                pe.wait_ge(bl_ready, b + 1)
                if b:
                    pe.wait_ge(kt_copied, b)
                for q in range(GB):
                    o = 4 * BANK + q * P
                    mm = pe.transpose(psf[:, o:o + P], bl[:, b % 2, q, :, :].rearrange("p l c -> p (l c)"), g.ident[:, :])
                mm.then_inc(b_turned, 1)

            def u_turn(b):
                pe.wait_ge(u_grouped, b + 1)
                pe.wait_ge(b_copied, b + 1)
                for q in range(GB):
                    o = 4 * BANK + q * P
                    pe.transpose(psf[:, o:o + P], u_grp[:, q, :, :].rearrange("p l c -> p (l c)"), g.ident[:, :])
                for q in range(GB):
                    mm = pe.transpose(ps[:, 6, q * NS:(q + 1) * NS],
                                      us_grp[:, q, :, :].rearrange("p l c -> p (l c)"), g.ident[US0:US0 + NS, US0:US0 + NS])
                mm.then_inc(u_turned, 1)

            b_turn(0)
            pe.wait_ge(st_in, 16 * 4)
            for q in range(2):
                for t in range(2):
                    o = (2 * q + t) * P
                    mm = pe.transpose(ps[:, 7, o:o + P], st[:, t, q, :], g.ident[:, :])
            mm.then_inc(st_turned, 1)
            u_turn(0)
            pe.wait_ge(st_copied, 1)
            for b in range(NBATCH):
                s = b % 2
                pe.wait_ge(b_copied, b + 1)
                pe.wait_ge(u_copied, b + 1)
                if b:
                    pe.wait_ge(y_copied, b)
                for q in range(GB):
                    pe.matmul(psf[:, q * P:(q + 1) * P], bst[:, q, :], u[:, s, q, 0:P], start=True, stop=True)
                for q in range(GB):
                    mm = pe.matmul(ps[:, 7, q * NS:(q + 1) * NS], bst[:, q, :], u[:, s, q, P:P + NS], start=True, stop=True)
                mm.then_inc(xin_done, 1)
                pe.wait_ge(cl_ready, b + 1)
                for q in range(GB):
                    o = 4 * BANK + q * P
                    mm = pe.matmul(psf[0:GC, o:o + P], bb_x[:, b * GB + q, :],
                                   cl[:, s, q, 0:L, :].rearrange("p l c -> p (l c)"), start=True, stop=True)
                mm.then_inc(kt_done, 1)
                pe.wait_ge(xin_copied, b + 1)
                if b:
                    pe.wait_ge(y_gelu, b)
                for h in range(2):
                    mm = pe.matmul(ps[:, 2 + h, :], swap[:, :], xin[:, 4 * h:4 * h + 4, :], start=True, stop=True)
                mm.then_inc(xs_done, 1)
                if b + 1 < NBATCH:
                    b_turn(b + 1)
                pe.wait_ge(z_ready, b + 1)
                for h in range(2):
                    mm = pe.matmul(ps[:, h, :], swap[:, :], z[:, 4 * h:4 * h + 4, :], start=True, stop=True)
                mm.then_inc(zs_done, 1)
                if b + 1 < NBATCH:
                    u_turn(b + 1)
                pe.wait_ge(x_ready, b + 1)
                pe.wait_ge(mi_in[s], 16 * L * (b // 2 + 1))
                for q in range(GB):
                    o = 2 * BANK + q * P
                    pe.matmul(psf[:, o:o + P], u[:, s, q, 0:P], mi[:, s, q, :], start=True, stop=False)
                    pe.matmul(psf[:, o:o + P], xall[:, q, 0:NC], cl[:, s, q, 1:L + 1, :].rearrange("p l c -> p (l c)"),
                              start=False, stop=True)
                for q in range(GB):
                    cs = slice(q * GC, (q + 1) * GC)
                    pe.matmul(ps[0:NS, 7, cs], u[:, s, q, P:P + NS], mi[:, s, q, P - GC:P], start=True, stop=False)
                    mm = pe.matmul(ps[0:NS, 7, cs], x0[:, :, b * GB + q], cl[:, s, q, 1, :], start=False, stop=True)
                mm.then_inc(y_done, 1)
                pe.wait_ge(y_gelu, b + 1)
                for l in range(L):
                    pe.transpose(psf[:, l * P:(l + 1) * P], y[:, l, :], g.ident[:, :])
                pe.transpose(ps[:, 7, 0:NS], ys[:, :], g.ident[0:NS, 0:NS]).then_inc(y_turned, 1)
            pe.wait_ge(x1_ready, 1)
            pe.transpose(ps[0:NG, 4, 0:P], x_last[:, :], g.ident[:, :])
            for t in range(2):
                mm = pe.transpose(ps[:, 5, t * P:(t + 1) * P],
                                  x1[:, 4 * t:4 * t + 4, :].rearrange("p s g -> p (s g)"), g.ident[:, :])
            mm.then_inc(last_turned, 1)


DIST = 383


def bucket_of_distance():
    exact = NB // 2

    def bucket(n):
        return n if n < exact else min(NB - 1, exact + int(math.log(n / exact) / math.log(128 / exact) * (NB - exact)))
    return [bucket(max(n, 0)) for n in range(1024)]


def phase_glu(nc, g):
    with ExitStack() as ctx:
        sb = lambda n, s, d=F32: ctx.enter_context(nc.sbuf_tensor("l_" + n, s, d))
        ps, sem = g.ps, lambda n: g.sem("l_" + n)
        wst = sb("wst", [P, 4, SW])
        wh, wl = sb("wh", [P, 4, SW], F32R), sb("wl", [P, 4, SW], F32R)
        xh, xl = sb("xh", [P, 4, T], F32R), sb("xl", [P, 4, T], F32R)
        bias = sb("bias", [P, 4])
        sg = sb("sg", [P, 2, T])
        rel_t, onehot = sb("rel", [NB, H]), sb("onehot", [NB, DIST])
        rel_rep = sb("rel_rep", [NB, H, P])
        drow = sb("drow", [P, 2, DIST])
        c_in, rel_ready, d_done, d_copied = (sem(n) for n in ("c_in", "rel_ready", "d_done", "d_copied"))
        d_out = [sem(f"d_out{i}") for i in range(2)]
        w_in, b_in, w_hi, w_lo, x_hi, x_lo, done, sig, prod, y_hi, y_lo = (
            sem(n) for n in ("w_in", "b_in", "w_hi", "w_lo", "x_hi", "x_lo", "done", "sig", "prod", "y_hi", "y_lo"))
        block = ctx.enter_context(nc.Block())

        @block.sync
        def _(sp):
            sp.dma_start(wst[:, :, :], g.w_glu.rearrange("(k p) n -> p k n", p=P)).then_inc(w_in, 16)
            sp.dma_start(bias[:, :], g.b_glu.rearrange("(m p) -> p m", p=P), allow_slow_non_contiguous=True).then_inc(b_in, 16)
            sp.dma_start(rel_t[:, :], g.rel_bias).then_inc(c_in, 16)
            sp.dma_start(onehot[:, :], g.c_onehot).then_inc(c_in, 16)
            for h in range(H):
                sp.wait_ge(d_copied, h + 1)
                sp.dma_start(g.d_bias[h, :].rearrange("(p m) -> p m", m=DIST), drow[:, h % 2, :]).then_inc(d_out[h % 2], 16)
            for i in range(2):
                sp.wait_ge(d_out[i], 16 * H // 2)

        @block.scalar
        def _(act):
            def unit(m):
                act.wait_ge(done, m + 1)
                if m >= 2:
                    act.wait_ge(prod, m - 1)
                if m == 0:
                    act.wait_ge(b_in, 16)
                act.activation(as_thirds(sg[:, m % 2, :]), thirds(ps, m % 2), ACT.Sigmoid, bias=bias[:, m:m + 1]).then_inc(sig, 1)
                act.wait_ge(prod, m + 1)
                act.activation(g.ys_h[:, m, :], sg[:, m % 2, :], ACT.Copy).then_inc(y_hi, 1)

            act.activation(xh[:, 0:2, :], g.gT[:, 0:2, :], ACT.Copy).then_inc(x_hi, 1)
            act.wait_ge(w_in, 16)
            act.activation(wh[:, :, :], wst[:, :, :], ACT.Copy).then_inc(w_hi, 1)
            act.activation(xh[:, 2:4, :], g.gT[:, 2:4, :], ACT.Copy).then_inc(x_hi, 1)
            for h in range(H):
                act.wait_ge(d_done, h + 1)
                if h >= 2:
                    act.wait_ge(d_out[h % 2], 16 * (h // 2))
                act.activation(drow[:, h % 2, :], ps[:, 6 + h % 2, 0:DIST], ACT.Copy, scale=8.0).then_inc(d_copied, 1)
                if h % 2:
                    unit(h // 2)

        @block.vector
        def _(dve):
            dve.wait_ge(c_in, 32)
            dve.tensor_copy(rel_rep[:, :, :], over(rel_t[:, :], P)).then_inc(rel_ready, 1)
            dve.wait_ge(x_hi, 1)
            dve.tensor_tensor(xl[:, 0:2, :], g.gT[:, 0:2, :], xh[:, 0:2, :].bitcast(F32), ALU.subtract).then_inc(x_lo, 1)
            dve.wait_ge(w_hi, 1)
            dve.tensor_tensor(wl[:, :, :], wst[:, :, :], wh[:, :, :].bitcast(F32), ALU.subtract).then_inc(w_lo, 1)
            dve.wait_ge(x_hi, 2)
            dve.tensor_tensor(xl[:, 2:4, :], g.gT[:, 2:4, :], xh[:, 2:4, :].bitcast(F32), ALU.subtract).then_inc(x_lo, 1)
            for m in range(4):
                dve.wait_ge(sig, m + 1)
                dve.tensor_tensor(sg[:, m % 2, :], sg[:, m % 2, :], g.gT[:, m, :], ALU.mult).then_inc(prod, 1)
                dve.wait_ge(y_hi, m + 1)
                dve.tensor_tensor(g.ys_l[:, m, :], sg[:, m % 2, :], g.ys_h[:, m, :].bitcast(F32), ALU.subtract).then_inc(y_lo, 1)

        @block.tensor
        def _(pe):
            pe.wait_ge(c_in, 32)
            pe.wait_ge(rel_ready, 1)
            for m in range(4):
                for h in (2 * m, 2 * m + 1):
                    if h >= 2:
                        pe.wait_ge(d_copied, h - 1)
                    pe.matmul(ps[:, 6 + h % 2, 0:DIST], rel_rep[:, h, :], onehot[:, :], start=True, stop=True).then_inc(d_done, 1)
                if m >= 2:
                    pe.wait_ge(sig, m - 1)
                cs = slice(m * P, (m + 1) * P)
                if m:
                    project(pe, ps, m % 2, wh[:, :, cs], wl[:, :, cs], xh, xl, 4).then_inc(done, 1)
                    continue
                pe.wait_ge(w_lo, 1)
                for a in (0, 2):
                    pe.wait_ge(x_lo, a // 2 + 1)
                    mm = project(pe, ps, 0, wh[:, a:a + 2, cs], wl[:, a:a + 2, cs], xh[:, a:a + 2, :], xl[:, a:a + 2, :], 2,
                                 first=a == 0, last=a == 2)
                mm.then_inc(done, 1)


def phase_attention(nc, g):
    with ExitStack() as ctx:
        sb = lambda n, s, d=F32: ctx.enter_context(nc.sbuf_tensor("t_" + n, s, d))
        ps, sem = g.ps, lambda n: g.sem("t_" + n)
        psf = ps[:, :, :].rearrange("p b c -> p (b c)")
        NLG = 4
        vv = sb("v", [P, NT, AW])
        nci = sb("nci", [P, P])
        mask01 = sb("mask01", [P, P + 2 * P])
        b31 = sb("b31", [P, H])
        t8h, t8l = sb("t8h", [P, H, 2 * P], F32R), sb("t8l", [P, H, 2 * P], F32R)
        lg = sb("lg", [P, NLG, NP])
        t8 = lg[:, 0:2, :].rearrange("p s (h c) -> p (s h) c", c=2 * P)
        pt = sb("pt", [P, 2, NP])
        ident_r = sb("ident_r", [P, P], F32R)
        m8 = sb("m8", [P, 8])
        mx, nmx, den, rden = (sb(n, [P, NT * H]) for n in ("mx", "nmx", "den", "rden"))

        v_in, c_in, t_in, t_ready, m_ready = (sem(n) for n in ("v_in", "c_in", "t_in", "t_ready", "m_ready"))
        s_done, l_done, nmx_done, e_done, r_done, p_done, turned, pt_done, y_done, yh_done, yl_done = (
            sem(n) for n in ("s_done", "l_done", "nmx_done", "e_done", "r_done", "p_done", "turned", "pt_done", "y_done",
                             "yh_done", "yl_done"))
        th_done, tl_done, late, tab_in, kx_in = (sem(n) for n in ("th_done", "tl_done", "late", "tab_in", "kx_in"))
        block = ctx.enter_context(nc.Block())
        steps = [(i, h) for i in range(NT) for h in range(H)]
        NSTEP = len(steps)
        masks = [mask01[:, 0:P], mask01[:, P:3 * P]] + list(g.mask)

        @block.sync
        def _(sp):
            table = g.d_bias[:, P - 1:P - 1 + P * (DIST - 1)].rearrange("h (p m) -> p h m", m=DIST - 1)
            for h in range(0, H, 4):
                sp.dma_start(t8[:, h:h + 4, :], table[:, h:h + 4, 0:2 * P]).then_inc(t_in, 16)
            sp.dma_start(b31[:, :], g.rel_bias[NB - 1, :].partition_broadcast(P)).then_inc(c_in, 16)
            sp.dma_start(nci[:, :], g.c_not_causal).then_inc(c_in, 16)
            sp.dma_start(vv[:, :, :], g.v_prompt.rearrange("(i p) c -> p i c", p=P)).then_inc(v_in, 16)
            sp.dma_start(g.table[:, :], g.page_table.rearrange("b n -> (b n)").unsqueeze(0)).then_inc(tab_in, 16)
            sp.wait_ge(tab_in, 16)
            for b in range(NS):
                for q in range(2):
                    page = sp.value_load(g.table[0:1, 2 * b + q:2 * b + q + 1], min_val=0, max_val=g.cache_k.shape[0] - 1)
                    sp.dma_start(g.kx[:, b, q, :], g.cache_kidx[bass.ds(page, 1), :, :].rearrange(
                        "a p c -> p (a c)")).then_inc(kx_in, 16)
            sp.wait_ge(kx_in, 16 * 2 * NS)

        @block.scalar
        def _(act):
            act.activation(ident_r[:, :], g.ident[:, :], ACT.Copy)
            act.wait_ge(t_ready, 1)
            act.activation(t8h[:, :, :], t8[:, :, :], ACT.Copy).then_inc(th_done, 1)

            def probs(n):
                i = steps[n][0]
                act.wait_ge(nmx_done, n + 1)
                act.activation(lg[:, n % NLG, 0:(i + 1) * P], lg[:, n % NLG, 0:(i + 1) * P], ACT.Exp,
                               bias=nmx[:, n:n + 1], accum_out=den[:, n:n + 1]).then_inc(e_done, 1)

            def pt_copy(n):
                w = (steps[n][0] + 1) * P
                act.wait_ge(turned, n + 1)
                if n >= 2:
                    act.wait_ge(y_done, n - 1)
                act.activation(pt[:, n % 2, 0:w], psf[:, 4 * BANK:4 * BANK + w], ACT.Copy).then_inc(pt_done, 1)

            def y_high(n):
                i, h = steps[n]
                act.wait_ge(y_done, n + 1)
                act.activation(g.ya_h[:, h // 2, i * P:(i + 1) * P], ps[:, 6 + (n // 2) % 2, 0:P], ACT.Copy).then_inc(yh_done, 1)

            for n in range(NSTEP + 3):
                if n < NSTEP:
                    probs(n)
                if 2 <= n < NSTEP + 2:
                    pt_copy(n - 2)
                if n >= 3 and n % 2 == 0:
                    y_high(n - 3)
            assert (NSTEP + 2) % 2 == 0

        @block.vector
        def _(dve):
            dve.wait_ge(c_in, 32)
            dve.memset(mask01[:, P:2 * P], 0.0)
            dve.tensor_scalar(mask01[:, 0:P], nci[:, :], HIDE, None, ALU.mult)
            dve.tensor_scalar(mask01[:, 2 * P:3 * P], nci[:, :], HIDE, None, ALU.mult).then_inc(m_ready, 1)
            dve.tensor_scalar(b31[:, :], b31[:, :], 8.0, None, ALU.mult).then_inc(m_ready, 1)
            dve.wait_ge(m_ready, 2)
            dve.wait_ge(t_in, 16 * 2)
            dve.tensor_tensor(t8[:, :, :], t8[:, :, :], over(b31[:, :], 2 * P), ALU.subtract).then_inc(t_ready, 1)
            dve.wait_ge(th_done, 1)
            dve.tensor_tensor(t8l[:, :, :], t8[:, :, :], t8h[:, :, :].bitcast(F32), ALU.subtract).then_inc(tl_done, 1)

            def logits(n):
                i = steps[n][0]
                w = (i + 1) * P
                dve.wait_ge(s_done, n + 1)
                if n >= NLG:
                    dve.wait_ge(turned, n - NLG + 1)
                dve.tensor_tensor_reduce(out=lg[:, n % NLG, 0:w], in0=psf[:, (n % 2) * 1024:(n % 2) * 1024 + w],
                                         in1=masks[i], scale=0.125, scalar=-3.0e38, op0=ALU.add, op1=ALU.max,
                                         accum_out=mx[:, n:n + 1]).then_inc(l_done, 1)
                dve.wait_ge(l_done, n + 1)
                dve.tensor_scalar(nmx[:, n:n + 1], mx[:, n:n + 1], -1.0, None, ALU.mult).then_inc(nmx_done, 1)

            def scale(n):
                w = (steps[n][0] + 1) * P
                dve.wait_ge(e_done, n + 1)
                dve.reciprocal(rden[:, n:n + 1], den[:, n:n + 1]).then_inc(r_done, 1)
                dve.wait_ge(r_done, n + 1)
                dve.tensor_scalar(lg[:, n % NLG, 0:w], lg[:, n % NLG, 0:w], rden[:, n:n + 1], None,
                                  ALU.mult).then_inc(p_done, 1)

            def y_low(n):
                i, h = steps[n]
                dve.wait_ge(yh_done, n // 2 + 1)
                o = g.ya_h[:, h // 2, i * P:(i + 1) * P]
                dve.tensor_tensor(g.ya_l[:, h // 2, i * P:(i + 1) * P], ps[:, 6 + (n // 2) % 2, 0:P], o.bitcast(F32),
                                  ALU.subtract).then_inc(yl_done, 1)

            def late_round(k):
                sc = g.mask[NT - 3]
                dve.max(m8[:, :], sc).then_inc(late, 1)
                dve.wait_ge(late, 2 * k + 1)
                dve.match_replace(out=sc, in_to_replace=m8[:, :], in_values=sc, imm_value=TAKEN).then_inc(late, 1)
                dve.wait_ge(late, 2 * k + 2)
                if k == LATE_ROUNDS - 1:
                    dve.tensor_scalar(sc, sc, -3.2e38, HIDE, ALU.is_gt, ALU.mult).then_inc(late, 1)
                    dve.wait_ge(late, 2 * k + 3)

            for n in range(NSTEP + 4):
                if n < NSTEP:
                    logits(n)
                if 1 <= n <= NSTEP:
                    scale(n - 1)
                if n >= 4 and n % 2 == 1:
                    y_low(n - 4)
                k = n - (NSTEP - H - 2 * LATE_ROUNDS)
                if k >= 0 and k % 2 == 0 and k // 2 < LATE_ROUNDS:
                    late_round(k // 2)

        @block.tensor
        def _(pe):
            pe.wait_ge(th_done, 1)
            pe.wait_ge(tl_done, 1)
            pe.wait_ge(m_ready, 2)

            def scores(n):
                i, h = steps[n]
                w, r, o = (i + 1) * P, (h % 2) * HD, (n % 2) * 1024
                if n >= 2:
                    pe.wait_ge(l_done, n - 1)
                for c in range(0, w, BANK):
                    m = min(BANK, w - c)
                    pe.matmul(psf[:, o + c:o + c + m], g.qT[r:r + HD, h // 2, i * P:(i + 1) * P],
                              g.kT[r:r + HD, h // 2, c:c + m], start=True, stop=False, skip_group_check=True)
                cuts = [(0, 1)] if i == 0 else [(i - 1, i), (i, i + 1)] if i * P % BANK == 0 else [(i - 1, i + 1)]
                for a, b in cuts:
                    ts = slice((a - i + 1) * P, (b - i + 1) * P)
                    for t in (t8h, t8l):
                        mm = pe.matmul(psf[:, o + a * P:o + b * P], ident_r[:, :], t[:, h, ts],
                                       start=False, stop=t is t8l, skip_group_check=True)
                mm.then_inc(s_done, 1)

            def turn(n):
                i = steps[n][0]
                pe.wait_ge(p_done, n + 1)
                if n:
                    pe.wait_ge(pt_done, n)
                for j in range(i + 1):
                    mm = pe.transpose(psf[:, 4 * BANK + j * P:4 * BANK + (j + 1) * P], lg[:, n % NLG, j * P:(j + 1) * P],
                                      g.ident[:, :])
                mm.then_inc(turned, 1)

            def weigh(n):
                i, h = steps[n]
                pe.wait_ge(pt_done, n + 1)
                if n == 0:
                    pe.wait_ge(v_in, 16)
                if n >= 4 and h % 2 == 0:
                    pe.wait_ge(yl_done, n // 2 - 1)
                r = (h % 2) * HD
                for j in range(i + 1):
                    mm = pe.matmul(ps[r:r + HD, 6 + (n // 2) % 2, 0:P], vv[:, j, h * HD:(h + 1) * HD],
                                   pt[:, n % 2, j * P:(j + 1) * P], start=(j == 0), stop=(j == i), skip_group_check=True)
                mm.then_inc(y_done, 1)

            for n in range(NSTEP + 3):
                if n < NSTEP:
                    scores(n)
                if 2 <= n < NSTEP + 2:
                    turn(n - 2)
                if n >= 3:
                    weigh(n - 3)


def phase_sample(nc, g):
    BH = NS * H
    with ExitStack() as ctx:
        sb = lambda n, s, d=F32: ctx.enter_context(nc.sbuf_tensor("a_" + n, s, d))
        ps, sem = g.ps, lambda n: g.sem("a_" + n)
        psf = ps[:, :, :].rearrange("p b c -> p (b c)")
        kk, vv = sb("k", [P, 2, 2, AW]), sb("v", [P, NS, 2, AW])
        vs = sb("vs", [NS, AW])
        own = sb("own", [NS, NS * JH + BH])
        ownT32, ownT64 = sb("ownT32", [NS * JH, NS]), sb("ownT64", [BH, NS])
        jsel = sb("jsel", [P, NS * JH])
        rel_t, onehot = sb("rel", [NB, H]), sb("onehot", [NB, SK])
        rel_rep = sb("rel_rep", [NB, NS, H])
        bias = sb("bias", [BH, SK])
        wcol, wtmp = sb("wcol", [NS * JH, 1]), sb("wtmp", [NS * JH, NS])
        qm = sb("qm", [ID, NS, NS * JH])
        kxT = sb("kxT", [ID, 2, SK])
        sc32 = sb("sc32", [NS * JH, SK])
        sc = sb("sc", [NS, SK])
        m8 = sb("m8", [NS, 8])
        qb = sb("qb", [P, 4, NS, BH])
        kTb = sb("kT", [P, 2, 4, SK])
        lg, dmsk = sb("lg", [BH, SK]), sb("dmsk", [BH, SK])
        mx, nmx, den, rden = (sb(n, [BH, 1]) for n in ("mx", "nmx", "den", "rden"))
        pself = sb("pself", [BH, NS])
        hsel = sb("hsel", [BH, H])
        pT = sb("pT", [P, 2, NS, BH])
        psT = sb("psT", [NS, BH])
        yb = sb("yb", [BH, AW])
        yf = sb("yf", [P, 4, NS])

        c_in, vs_in = (sem(n) for n in ("c_in", "vs_in"))
        v_in = [sem(f"v_in{b}") for b in range(NS)]
        k_in = [sem(f"k_in{i}") for i in range(2)]
        zero, setup, w_done, w_ready, kx_turned, kx_copied, sc_done, sc_ready, sum_done, sel = (
            sem(n) for n in ("zero", "setup", "w_done", "w_ready", "kx_turned", "kx_copied", "sc_done", "sc_ready",
                             "sum_done", "sel"))
        k_turned, k_copied, lg_done, msk_done, msk_ready, bias_done, bias_ready, exp_done, p_ready, p_turned, p_copied, y_done, y_own, y_summed = (
            sem(n) for n in ("k_turned", "k_copied", "lg_done", "msk_done", "msk_ready", "bias_done", "bias_ready",
                             "exp_done", "p_ready", "p_turned", "p_copied", "y_done", "y_own", "y_summed"))
        dv, nmx_done, kc = sem("dve_step"), sem("nmx_done"), sem("kcol")
        block = ctx.enter_context(nc.Block())

        @block.sync
        def _(sp):
            for n, (dst, src) in enumerate(((own[:, :], g.c_own), (ownT32[:, :], g.c_own32), (ownT64[:, :], g.c_own64),
                                            (jsel[ID:ID + JH, :], g.c_jsel), (rel_t[:, :], g.rel_bias),
                                            (onehot[:, :], g.c_onehot_s), (hsel[:, :], g.c_headsel))):
                sp.dma_start(dst, src).then_inc(c_in, 16)
            sp.dma_start(vs[:, :], g.v_sample).then_inc(vs_in, 16)
            pages = [sp.value_load(g.table[0:1, n:n + 1], min_val=0, max_val=g.cache_k.shape[0] - 1) for n in range(2 * NS)]
            for b in range(NS):
                if b >= 2:
                    sp.wait_ge(k_turned, 2 * (b - 1))
                for q in range(2):
                    pg = bass.ds(pages[2 * b + q], 1)
                    sp.dma_start(kk[:, b % 2, q, :], g.cache_k[pg, :, :].rearrange("a p c -> p (a c)")).then_inc(k_in[b % 2], 16)

        @block.gpsimd
        def _(pool):
            pool.memset(qm[:, :, :], 0.0).then_inc(zero, 1)
            pool.memset(qb[:, :, :, :], 0.0).then_inc(zero, 1)
            pool.memset(pT[:, :, :, :], 0.0).then_inc(zero, 1)
            pages = [pool.value_load(g.table[0:1, n:n + 1], min_val=0, max_val=g.cache_v.shape[0] - 1) for n in range(2 * NS)]
            for b in range(NS):
                for q in range(2):
                    pool.dma_start(vv[:, b, q, :], g.cache_v[bass.ds(pages[2 * b + q], 1), :, :].rearrange(
                        "a p c -> p (a c)")).then_inc(v_in[b], 16)

        @block.scalar
        def _(act):
            for b in range(NS):
                act.wait_ge(kx_turned, b + 1)
                if b >= 2:
                    act.wait_ge(sc_done, b - 1)
                act.activation(kxT[:, b % 2, 0:PAST], ps[0:ID, b % 2, 0:PAST], ACT.Copy)
                act.activation(kxT[:, b % 2, PAST:SK], g.kwT[0:ID, NP + b:NP + b + 1], ACT.Copy).then_inc(kx_copied, 1)
            for b in range(NS):
                act.wait_ge(k_turned, 2 * (b + 1))
                if b >= 2:
                    act.wait_ge(lg_done, b - 1)
                o = (2 + 2 * (b % 2)) * BANK
                act.activation(kTb[:, b % 2, :, 0:PAST], psf[:, o:o + 4 * PAST].rearrange("p (m s) -> p m s", m=4), ACT.Copy)
                act.activation(kTb[:, b % 2, :, PAST:SK], g.kT[:, :, NP + b:NP + b + 1], ACT.Copy).then_inc(k_copied, 1)
            act.wait_ge(nmx_done, 1)
            act.activation(lg[:, :], lg[:, :], ACT.Exp, bias=nmx[:, 0:1], accum_out=den[:, 0:1]).then_inc(exp_done, 1)
            act.wait_ge(p_turned, 1)
            act.wait_ge(zero, 3)
            for q in range(2):
                for b in range(NS):
                    hs = slice(b * H, (b + 1) * H)
                    act.activation(pT[:, q, b, hs], ps[:, 0, q * BH + b * H:q * BH + (b + 1) * H], ACT.Copy)
            act.activation(psT[:, :], ps[0:NS, 0, 2 * BH:3 * BH], ACT.Copy).then_inc(p_copied, 1)

        @block.vector
        def _(dve):
            steps = [0]

            def step(ins):
                ins.then_inc(dv, 1)
                steps[0] += 1
                dve.wait_ge(dv, steps[0])

            dve.wait_ge(zero, 2)
            qmf = qm[:, :, :].rearrange("p b n -> p (b n)")
            for j in range(JH):
                r = (j % 2) * ID
                dve.tensor_copy(qmf[:, j:j + (NS * JH + JH) * (NS - 1) + 1:NS * JH + JH], g.qiT[r:r + ID, j // 2, NP:T])
            for h in range(H):
                r = (h % 2) * HD
                q = qb[r:r + HD, h // 2, :, :].rearrange("p b n -> p (b n)")
                ins = dve.tensor_copy(q[:, h:h + (BH + H) * (NS - 1) + 1:BH + H], g.qT[r:r + HD, h // 2, NP:T])
            dve.wait_ge(c_in, 16 * 7)
            dve.tensor_copy(rel_rep[:, :, :], rel_t[:, :].unsqueeze(1).broadcast_to([NB, NS, H])).then_inc(setup, 1)
            dve.wait_ge(w_done, 1)
            step(dve.tensor_tensor(wtmp[:, :], ps[0:NS * JH, 7, 0:NS], ownT32[:, :], ALU.mult))
            step(dve.tensor_reduce(wcol[:, :], wtmp[:, :], AX.X, ALU.add))
            dve.wait_ge(bias_done, 1)
            dve.tensor_copy(bias[:, :], ps[0:BH, 6, 0:SK]).then_inc(bias_ready, 1)
            dve.wait_ge(sc_done, NS)
            dve.tensor_scalar(sc32[:, :], ps[0:NS * JH, 7, 0:SK], 0.0, wcol[:, 0:1], ALU.max, ALU.mult).then_inc(sc_ready, 1)
            dve.wait_ge(sum_done, 1)
            step(dve.tensor_copy(sc[:, :], ps[0:NS, 6, 0:SK]))
            for _ in range(STOPK // 8):
                step(dve.max(m8[:, :], sc[:, :]))
                step(dve.match_replace(out=sc[:, :], in_to_replace=m8[:, :], in_values=sc[:, :], imm_value=TAKEN))
            dve.tensor_scalar(sc[:, :], sc[:, :], -3.2e38, HIDE, ALU.is_gt, ALU.mult).then_inc(sel, 1)
            dve.wait_ge(msk_done, 1)
            step(dve.tensor_tensor(dmsk[:, :], ps[0:BH, 6, 0:SK], bias[:, :], ALU.add))
            dve.wait_ge(lg_done, NS)
            step(dve.scalar_tensor_tensor(out=lg[:, :], in0=ps[0:BH, 7, 0:SK], scalar=0.125, in1=dmsk[:, :],
                                          op0=ALU.mult, op1=ALU.add))
            step(dve.tensor_reduce(mx[:, :], lg[:, :], AX.X, ALU.max))
            dve.tensor_scalar(nmx[:, :], mx[:, :], -1.0, None, ALU.mult).then_inc(nmx_done, 1)
            dve.wait_ge(exp_done, 1)
            step(dve.reciprocal(rden[:, :], den[:, :]))
            step(dve.tensor_scalar(lg[:, :], lg[:, :], rden[:, 0:1], None, ALU.mult))
            dve.tensor_scalar(pself[:, :], ownT64[:, :], lg[:, PAST:SK], None, ALU.mult).then_inc(p_ready, 1)
            dve.wait_ge(y_done, 1)
            dve.tensor_tensor(yb[:, :].rearrange("p (h c) -> p h c", h=H), ps[0:BH, 1, :].rearrange("p (h c) -> p h c", h=H),
                              over(hsel[:, :], HD), ALU.mult).then_inc(y_own, 1)
            dve.wait_ge(y_summed, 1)
            step(dve.tensor_copy(yf[:, :, :], ps[:, 0, 0:4 * NS].rearrange("p (m b) -> p m b", m=4)))
            step(dve.tensor_copy(g.ya_h[:, :, NP:T], yf[:, :, :]))
            step(dve.tensor_tensor(g.ya_l[:, :, NP:T], yf[:, :, :], g.ya_h[:, :, NP:T].bitcast(F32), ALU.subtract))

        @block.tensor
        def _(pe):
            pe.wait_ge(setup, 1)
            pe.wait_ge(c_in, 16 * 7)
            pe.matmul(ps[0:NS * JH, 7, 0:NS], jsel[ID:ID + JH, :], g.kwT[ID:ID + JH, NP:T], start=True, stop=True).then_inc(w_done, 1)
            pe.matmul(ps[0:BH, 6, 0:SK], rel_rep[:, :, :].rearrange("p b h -> p (b h)"), onehot[:, :],
                      start=True, stop=True).then_inc(bias_done, 1)

            def index_turn(b):
                if b >= 2:
                    pe.wait_ge(kx_copied, b - 1)
                for q in range(2):
                    mm = pe.transpose(ps[0:ID, b % 2, q * P:(q + 1) * P], g.kx[:, b, q, :], g.ident[:, :])
                mm.then_inc(kx_turned, 1)

            index_turn(0)
            for b in range(NS):
                if b + 1 < NS:
                    index_turn(b + 1)
                pe.wait_ge(kx_copied, b + 1)
                if b == 0:
                    pe.wait_ge(dv, 2)
                pe.matmul(ps[0:NS * JH, 7, 0:SK], qm[:, b, :], kxT[:, b % 2, :], start=(b == 0), stop=(b == NS - 1)).then_inc(sc_done, 1)
            pe.wait_ge(sc_ready, 1)
            pe.wait_ge(bias_ready, 1)
            pe.matmul(ps[0:NS, 6, 0:SK], ownT32[:, :], sc32[:, :], start=True, stop=True).then_inc(sum_done, 1)

            def key_turn(b):
                for q in range(2):
                    if q == 0:
                        pe.wait_ge(k_in[b % 2], 32 * (b // 2 + 1))
                        if b >= 2:
                            pe.wait_ge(k_copied, b - 1)
                    for m in range(4):
                        o = (2 + 2 * (b % 2)) * BANK + m * PAST + q * P
                        mm = pe.transpose(psf[:, o:o + P], kk[:, b % 2, q, m * P:(m + 1) * P], g.ident[:, :])
                    mm.then_inc(k_turned, 1)

            key_turn(0)
            for b in range(NS):
                if b + 1 < NS:
                    key_turn(b + 1)
                pe.wait_ge(k_copied, b + 1)
                for m in range(4):
                    mm = pe.matmul(ps[0:BH, 7, 0:SK], qb[:, m, b, :], kTb[:, b % 2, m, :],
                                   start=(b == 0 and m == 0), stop=(b == NS - 1 and m == 3))
                mm.then_inc(lg_done, 1)
            pe.wait_ge(sel, 1)
            pe.matmul(ps[0:BH, 6, 0:SK], own[:, NS * JH:], sc[:, :], start=True, stop=True).then_inc(msk_done, 1)
            pe.wait_ge(p_ready, 1)
            for q in range(2):
                pe.transpose(ps[:, 0, q * BH:(q + 1) * BH], lg[:, q * P:(q + 1) * P], g.ident[0:BH, 0:BH])
            pe.transpose(ps[0:NS, 0, 2 * BH:3 * BH], pself[:, :], g.ident[0:BH, 0:BH]).then_inc(p_turned, 1)
            pe.wait_ge(p_copied, 1)
            pe.wait_ge(vs_in, 16)
            pe.matmul(ps[0:BH, 1, :], psT[:, :], vs[:, :], start=True, stop=False)
            for b in range(NS):
                pe.wait_ge(v_in[b], 32)
                for q in range(2):
                    mm = pe.matmul(ps[0:BH, 1, :], pT[:, q, b, :], vv[:, b, q, :], start=False, stop=(b == NS - 1 and q == 1))
            mm.then_inc(y_done, 1)
            pe.wait_ge(y_own, 1)
            for m in range(4):
                mm = pe.matmul(ps[:, 0, m * NS:(m + 1) * NS], yb[:, m * P:(m + 1) * P], ownT64[:, :], start=True, stop=True)
            mm.then_inc(y_summed, 1)


FT = 2 * FF // P
NG2 = FF // P // 2


def phase_merge(nc, g):
    with ExitStack() as ctx:
        sb = lambda n, s, d=F32: ctx.enter_context(nc.sbuf_tensor("m_" + n, s, d))
        ps, sem = g.ps, lambda n: g.sem("m_" + n)
        wst = sb("wst", [P, 2, 8, P])
        wh, wl = sb("wh", [P, 2, 8, P], F32R), sb("wl", [P, 2, 8, P], F32R)
        gt = sb("gt", [P, 2, 2, T])
        ma, mb = sb("ma", [P, T]), sb("mb", [P, T])
        w_in = [sem(f"w_in{i}") for i in range(2)]
        g_in = [sem(f"g_in{i}") for i in range(2)]
        w_hi, w_lo, done, prod, merged, m_hi, m_lo = (
            sem(n) for n in ("w_hi", "w_lo", "done", "prod", "merged", "m_hi", "m_lo"))
        block = ctx.enter_context(nc.Block())

        @block.sync
        def _(sp):
            wa = g.w_att_out.rearrange("(k p) n -> p k n", p=P)
            wb = g.w_ssm_out.rearrange("(k p) n -> p k n", p=P)
            for m in range(8):
                s, cs = m % 2, slice(m * P, (m + 1) * P)
                if m >= 2:
                    sp.wait_ge(w_lo, m - 1)
                sp.dma_start(wst[:, s, 0:4, :], wa[:, :, cs]).then_inc(w_in[s], 16)
                sp.dma_start(wst[:, s, 4:8, :], wb[:, :, cs]).then_inc(w_in[s], 16)
                if m >= 2:
                    sp.wait_ge(merged, m - 1)
                sp.dma_start(gt[:, s, 0, :], g.d_gates[:, m, :]).then_inc(g_in[s], 16)
                sp.dma_start(gt[:, s, 1, :], g.d_gates[:, 8 + m, :]).then_inc(g_in[s], 16)

        @block.gpsimd
        def _(pool):
            for m in range(8):
                s = m % 2
                pool.wait_ge(w_hi, m + 1)
                pool.tensor_tensor(wl[:, s, :, :], wst[:, s, :, :], wh[:, s, :, :].bitcast(F32), ALU.subtract).then_inc(w_lo, 1)

        @block.scalar
        def _(act):
            for m in range(9):
                if m < 8:
                    act.wait_ge(w_in[m % 2], 32 * (m // 2 + 1))
                    if m >= 2:
                        act.wait_ge(done, 2 * (m - 1))
                    act.activation(wh[:, m % 2, :, :], wst[:, m % 2, :, :], ACT.Copy).then_inc(w_hi, 1)
                if m:
                    act.wait_ge(merged, m)
                    act.activation(g.xT_h[:, m - 1, :], ma[:, :], ACT.Copy).then_inc(m_hi, 1)

        @block.vector
        def _(dve):
            for m in range(8):
                s = m % 2
                dve.wait_ge(g_in[s], 32 * (m // 2 + 1))
                dve.wait_ge(done, 2 * m + 1)
                if m:
                    dve.wait_ge(m_lo, m)
                dve.tensor_tensor(as_thirds(ma[:, :]), thirds(ps, 0), as_thirds(gt[:, s, 0, :]), ALU.mult).then_inc(prod, 1)
                dve.wait_ge(done, 2 * m + 2)
                dve.tensor_tensor(as_thirds(mb[:, :]), thirds(ps, 1), as_thirds(gt[:, s, 1, :]), ALU.mult).then_inc(prod, 1)
                dve.wait_ge(prod, 2 * m + 2)
                dve.tensor_tensor(ma[:, :], ma[:, :], mb[:, :], ALU.add).then_inc(merged, 1)
                dve.wait_ge(m_hi, m + 1)
                dve.tensor_tensor(g.xT_l[:, m, :], ma[:, :], g.xT_h[:, m, :].bitcast(F32), ALU.subtract).then_inc(m_lo, 1)

        @block.tensor
        def _(pe):
            for m in range(8):
                s = m % 2
                pe.wait_ge(w_lo, m + 1)
                for q, (xh, xl) in enumerate(((g.ya_h, g.ya_l), (g.ys_h, g.ys_l))):
                    if m:
                        pe.wait_ge(prod, 2 * m - 1 + q)
                    project(pe, ps, q, wh[:, s, 4 * q:4 * q + 4, :], wl[:, s, 4 * q:4 * q + 4, :], xh, xl, 4).then_inc(done, 1)


def phase_out(nc, g):
    with ExitStack() as ctx:
        sb = lambda n, s, d=F32: ctx.enter_context(nc.sbuf_tensor("o_" + n, s, d))
        ps, sem = g.ps, lambda n: g.sem("o_" + n)
        psf = ps[:, :, :].rearrange("p b c -> p (b c)")
        wst = sb("wst", [P, 2, D])
        wh, wl = sb("wh", [P, KD, D], F32R), sb("wl", [P, KD, D], F32R)
        gpost, gffn = sb("gpost", [P, D]), sb("gffn", [P, D])
        x = sb("x", [P, 2, D])
        z = sb("z", [P, 2, D])
        xn = sb("xn", [P, D])
        junk = sb("junk", [P, D])
        st = sb("st", [P, 2, 4, 9])
        w_in = [sem(f"w_in{i}") for i in range(2)]
        x_in = [sem(f"x_in{i}") for i in range(2)]
        w_hi, w_lo, g_in, done, z_done, ss_done, var_done, std_done, r_done, x2_done, xn_done, turned, hi_done, lo_done = (
            sem(n) for n in ("w_hi", "w_lo", "g_in", "done", "z_done", "ss_done", "var_done", "std_done", "r_done",
                             "x2_done", "xn_done", "turned", "hi_done", "lo_done"))
        x2_out = [sem(f"x2_out{i}") for i in range(2)]
        zs_done, done_1 = sem("zs_done"), sem("done_1")
        cst = sb("cst", [FT, 4, P])
        sst = sb("sst", [FT, 2 * NS, P])
        sc = sb("sc", [P, NS, 2, FT])
        tmp = sb("tmp", [P, NS, FT])
        conv_in, conv_turned, conv_copied, conv_step, row_out = (
            sem(n) for n in ("conv_in", "conv_turned", "conv_copied", "conv_step", "row_out"))
        block = ctx.enter_context(nc.Block())

        def rows(i):
            return TILES[i][1]

        @block.sync
        def _(sp):
            wv = g.w_o.rearrange("(k p) n -> p k n", p=P)
            for k in range(KD):
                if k >= 2:
                    sp.wait_ge(w_lo, k - 1)
                sp.dma_start(wst[:, k % 2, :], wv[:, k, :]).then_inc(w_in[k % 2], 16)
                if k == 1:
                    sp.dma_start(gpost[:, :], g.g_post_mix.partition_broadcast(P)).then_inc(g_in, 16)
                    sp.dma_start(gffn[:, :], g.g_pre_ffn.partition_broadcast(P)).then_inc(g_in, 16)
                if k == 4:
                    for j in range(3):
                        sp.dma_start(cst[:, j, :], g.conv_w[j, :].rearrange("(t p) -> t p", p=P)).then_inc(conv_in, 16)
                    sp.dma_start(cst[:, 3, :], g.conv_b.rearrange("(t p) -> t p", p=P)).then_inc(conv_in, 16)
                    sp.dma_start(sst[:, :, :], g.state_conv.rearrange("b i (t p) -> t (b i) p", p=P)).then_inc(conv_in, 16)
                    sp.dma_start(g.conv_sample[:, 0, :], g.state_conv[:, 1, :]).then_inc(row_out, 16)

            def store(i):
                t0, n = TILES[i]
                sp.wait_ge(x2_done, i + 1)
                sp.dma_start(g.d_x2[t0:t0 + n, :], z[0:n, i % 2, :]).then_inc(x2_out[i % 2], 16)

            for i, (t0, n) in enumerate(TILES):
                if i >= 2:
                    store(i - 2)
                src = g.x_prompt.rearrange("b t d -> (b t) d")[t0:t0 + n, :] if i < NT else \
                    g.x_sample.rearrange("b t d -> (b t) d")
                sp.dma_start(x[0:n, i % 2, :], src).then_inc(x_in[i % 2], 16)
            store(7)
            store(8)
            sp.wait_ge(x2_out[0], 16 * 5)
            sp.wait_ge(x2_out[1], 16 * 4)
            sp.wait_ge(row_out, 16)

        @block.gpsimd
        def _(pool):
            for k in range(KD):
                pool.wait_ge(w_hi, k + 1)
                pool.tensor_tensor(wl[:, k, :], wst[:, k % 2, :], wh[:, k, :].bitcast(F32), ALU.subtract).then_inc(w_lo, 1)

        @block.scalar
        def _(act):
            for k in range(KD):
                act.wait_ge(w_in[k % 2], 16 * (k // 2 + 1))
                act.activation(wh[:, k, :], wst[:, k % 2, :], ACT.Copy).then_inc(w_hi, 1)

            def square(i, q):
                n = rows(i)
                c = 2 * i + q
                if c:
                    act.wait_ge(ss_done, c)
                act.activation(junk[0:n, :], z[0:n, i % 2, :], ACT.Square, accum_out=st[0:n, q, 0, i:i + 1]).then_inc(ss_done, 1)
                act.wait_ge(var_done, c + 1)
                act.activation(st[0:n, q, 2, i:i + 1], st[0:n, q, 1, i:i + 1], ACT.Sqrt).then_inc(std_done, 1)

            def high(i):
                t0, n = TILES[i]
                act.wait_ge(turned, i + 1)
                act.activation(g.xT_h[:, :, t0:t0 + n], psf[:, 4 * BANK:6 * BANK].rearrange(
                    "p (k t) -> p k t", k=KD)[:, :, 0:n], ACT.Copy).then_inc(hi_done, 1)

            for i in range(9):
                n = rows(i)
                if i == 1:
                    act.wait_ge(done_1, 1)
                else:
                    act.wait_ge(done, max(i, 1))
                if i >= 2:
                    act.wait_ge(x2_out[i % 2], 16 * (i // 2))
                    act.wait_ge(xn_done, i - 1)
                act.activation(z[0:n, i % 2, :], psf[0:n, (i % 2) * 1024:(i % 2) * 1024 + D], ACT.Copy).then_inc(z_done, 1)
                if i == 0:
                    act.wait_ge(conv_turned, 1)
                    act.activation(g.cw[:, :, :].rearrange("p j t -> p (j t)"), ps[:, 6, 0:4 * FT], ACT.Copy)
                    act.activation(sc[:, :, :, :].rearrange("p b i t -> p (b i t)"),
                                   psf[:, 4 * BANK:4 * BANK + 2 * NS * FT], ACT.Copy).then_inc(conv_copied, 1)
                act.wait_ge(z_done, i + 1)
                square(i, 0)
                act.wait_ge(x2_done, i + 1)
                square(i, 1)
                if i:
                    high(i - 1)
            high(8)

        @block.vector
        def _(dve):
            rc = [0]

            def norm(i, q):
                n = rows(i)
                c = 2 * i + q
                dve.wait_ge(ss_done, c + 1)
                dve.tensor_scalar(st[0:n, q, 1, i:i + 1], st[0:n, q, 0, i:i + 1], 1.0 / D, EPS, ALU.mult, ALU.add).then_inc(var_done, 1)
                dve.wait_ge(std_done, c + 1)
                newton_rstd(dve, st[0:n, q, 3, i:i + 1], st[0:n, q, 2, i:i + 1], st[0:n, q, 1, i:i + 1], r_done, rc[0])
                rc[0] += 5

            def low(i):
                t0, n = TILES[i]
                dve.wait_ge(hi_done, i + 1)
                dve.tensor_tensor(g.xT_l[:, :, t0:t0 + n], psf[:, 4 * BANK:6 * BANK].rearrange(
                    "p (k t) -> p k t", k=KD)[:, :, 0:n], g.xT_h[:, :, t0:t0 + n].bitcast(F32), ALU.subtract).then_inc(lo_done, 1)

            def sample_taps():
                def w(j):
                    return g.cw[:, j, :].unsqueeze(1).broadcast_to([P, NS, FT])

                dve.wait_ge(conv_copied, 1)
                dve.tensor_tensor(tmp[:, :, :], sc[:, :, 0, :], w(0), ALU.mult).then_inc(conv_step, 1)
                dve.tensor_tensor(sc[:, :, 1, :], sc[:, :, 1, :], w(1), ALU.mult).then_inc(conv_step, 1)
                dve.wait_ge(conv_step, 2)
                dve.tensor_tensor(tmp[:, :, :], tmp[:, :, :], sc[:, :, 1, :], ALU.add).then_inc(conv_step, 1)
                dve.wait_ge(conv_step, 3)
                dve.tensor_tensor(g.conv0[:, :, :].rearrange("p t b -> p b t"), tmp[:, :, :], w(3), ALU.add).then_inc(conv_step, 1)

            dve.wait_ge(g_in, 32)
            for i in range(9):
                n = rows(i)
                zi = z[0:n, i % 2, :]
                norm(i, 0)
                dve.scalar_tensor_tensor(out=zi, in0=zi, scalar=st[0:n, 0, 3, i:i + 1], in1=gpost[0:n, :],
                                         op0=ALU.mult, op1=ALU.mult).then_inc(zs_done, 1)
                dve.wait_ge(zs_done, i + 1)
                dve.wait_ge(x_in[i % 2], 16 * (i // 2 + 1))
                dve.tensor_tensor(zi, zi, x[0:n, i % 2, :], ALU.add).then_inc(x2_done, 1)
                dve.wait_ge(x2_done, i + 1)
                norm(i, 1)
                if i:
                    dve.wait_ge(turned, i)
                dve.scalar_tensor_tensor(out=xn[0:n, :], in0=zi, scalar=st[0:n, 1, 3, i:i + 1], in1=gffn[0:n, :],
                                         op0=ALU.mult, op1=ALU.mult).then_inc(xn_done, 1)
                if i:
                    low(i - 1)
                if i == 3:
                    sample_taps()
            low(8)

        @block.tensor
        def _(pe):
            def turn(i):
                n = rows(i)
                pe.wait_ge(xn_done, i + 1)
                if i:
                    pe.wait_ge(lo_done, i)
                for k in range(KD):
                    o = 4 * BANK + k * P
                    mm = pe.transpose(psf[:, o:o + n], xn[0:n, k * P:(k + 1) * P], g.ident[0:n, 0:n])
                mm.then_inc(turned, 1)

            def products(i, k):
                t0, n = TILES[i]
                for q, (x_, w) in enumerate(((g.xT_h, wh), (g.xT_h, wl), (g.xT_l, wh))):
                    for c in range(2):
                        mm = pe.matmul(ps[0:n, (i % 2) * 2 + c, :], x_[:, k, t0:t0 + n], w[:, k, c * BANK:(c + 1) * BANK],
                                       start=(k == 0 and q == 0), stop=(k == KD - 1 and q == 2))
                return mm

            for k in range(KD):
                pe.wait_ge(w_lo, k + 1)
                mm0, mm1 = products(0, k), products(1, k)
            mm0.then_inc(done, 1)
            mm1.then_inc(done_1, 1)
            pe.wait_ge(conv_in, 16 * 5)
            for j in range(4):
                pe.transpose(ps[:, 6, j * FT:(j + 1) * FT], cst[:, j, :], g.ident[0:FT, 0:FT])
            for r in range(2 * NS):
                mm = pe.transpose(psf[:, 4 * BANK + r * FT:4 * BANK + (r + 1) * FT], sst[:, r, :], g.ident[0:FT, 0:FT])
            mm.then_inc(conv_turned, 1)
            for i in range(2, 9):
                pe.wait_ge(z_done, i - 1)
                for k in range(KD):
                    mm = products(i, k)
                mm.then_inc(done, 1)
                if i == 2:
                    pe.wait_ge(conv_copied, 1)
                    turn(0)
                turn(i - 1)
            turn(8)


def phase_ffn(nc, g):
    with ExitStack() as ctx:
        sb = lambda n, s, d=F32: ctx.enter_context(nc.sbuf_tensor("f_" + n, s, d))
        ps, sem = g.ps, lambda n: g.sem("f_" + n)
        wst = sb("wst", [P, 2, 8 * P])
        wh, wl = sb("wh", [P, 2, 8 * P], F32R), sb("wl", [P, 2, 8 * P], F32R)
        up = sb("up", [P, 2, 2 + T])
        acc = sb("acc", [P, 2, T])
        gh, gl = sb("gh", [P, 2, 2, T], F32R), sb("gl", [P, 2, 2, T], F32R)
        keep = sb("keep", [P, 10, FT])

        w_in = [sem(f"w_in{i}") for i in range(2)]
        w_hi, w_lo = sem("w_hi"), sem("w_lo")
        up_done, up_evac, down_done, down_evac = (sem(n) for n in ("up_done", "up_evac", "down_done", "down_evac"))
        tap0, tap0s, tap1, conv, gelu, prod, g_hi, g_lo, kept_cols, zero = (
            sem(n) for n in ("tap0", "tap0s", "tap1", "conv", "gelu", "prod", "g_hi", "g_lo", "kept_cols", "zero"))
        k_turned, k_copied = sem("k_turned"), sem("k_copied")
        block = ctx.enter_context(nc.Block())

        def job(it, q):
            return it * 6 + (q - 2)

        NJOB = 4 + 6 * (NG2 - 1) + 2
        up_v = g.w_up.rearrange("(k p) n -> p k n", p=P)
        down_v = g.w_down.rearrange("(k p) n -> p k n", p=P)

        def up_cols(it, q):
            return it * (2 * P) + ((q % 2) * FF + (q // 2) * P)

        @block.sync
        def _(sp):
            def load(j, s, it, q):
                if not isinstance(j, int) or j >= 2:
                    sp.wait_ge(w_lo, j - 1)
                if q < 4:
                    src = up_v[:, :, bass.ds(up_cols(it, q), P)]
                    dst = wst[:, s, :].rearrange("p (k n) -> p k n", k=KD)
                else:
                    src = down_v[:, bass.ds((it - 1) * 2, 2), (q - 4) * BANK:(q - 3) * BANK]
                    dst = wst[:, s, :].rearrange("p (k n) -> p k n", k=2)
                sp.dma_start(dst, src).then_inc(w_in[s], 16)

            for q in range(4):
                load(q, q % 2, 0, q)
            for q in range(6):
                load(job(1, q), q % 2, 1, q)
            with sp.Fori(0, (NG2 - 2) // 2) as j:
                for e in range(2):
                    for q in range(6):
                        load(j * 12 + job(2 + e, q), q % 2, j * 2 + (2 + e), q)
            for q in (4, 5):
                load(job(NG2, q - 4), q % 2, NG2, q)
            sp.wait_ge(k_copied, 1)
            sp.dma_start(g.conv_prompt.rearrange("i (t p) -> t i p", p=P), g.kept[:, 0:2, :]).then_inc(g.conv_out, 16)
            sp.dma_start(g.conv_sample[:, 1, :].rearrange("b (t p) -> t b p", p=P), g.kept[:, 2:10, :]).then_inc(g.conv_out, 16)

        @block.gpsimd
        def _(pool):
            def low(j, s):
                pool.wait_ge(w_hi, j + 1)
                pool.tensor_tensor(wl[:, s, :], wst[:, s, :], wh[:, s, :].bitcast(F32), ALU.subtract).then_inc(w_lo, 1)

            def keep_cols(it, q):
                u = it * 4 + q
                pool.wait_ge(up_evac, u + 1)
                tile = bass.ds(it * 2 + (q // 2 + (q % 2) * (FT // 2)), 1)
                pool.tensor_copy(keep[:, :, tile], up[:, q % 2, NP:NP + 10].unsqueeze(2)).then_inc(kept_cols, 1)

            pool.memset(g.fT[:, :, :], 0.0).then_inc(zero, 1)
            pool.memset(up[:, :, 0:2], 0.0).then_inc(zero, 1)
            low(0, 0)
            for q in range(4):
                low(q + 1, (q + 1) % 2)
                keep_cols(0, q)

            def iteration(it, j0):
                for q in range(6):
                    low(j0 + (q + 1), (q + 1) % 2)
                    if q < 4:
                        keep_cols(it, q)

            iteration(1, job(1, 0))
            with pool.Fori(0, (NG2 - 2) // 2) as j:
                for e in range(2):
                    iteration(j * 2 + (2 + e), j * 12 + job(2 + e, 0))
            low(NJOB - 1, 1)

        @block.scalar
        def _(act):
            def high(it, q):
                if isinstance(it, int) and it in (0, NG2):
                    s, uses = (q % 2, 16 * (q // 2 + 1)) if it == 0 else (q % 2, 16 * (NJOB // 2))
                else:
                    s, uses = q % 2, it * 48 + 16 * ((q - 2) // 2 + 1)
                act.wait_ge(w_in[s], uses)
                if isinstance(it, int) and it == NG2:
                    act.wait_ge(down_done, (NG2 - 2) * 8 + 4 * (q - 3))
                elif q >= 2:
                    act.wait_ge(up_done, it * 4 + (q - 1))
                elif isinstance(it, int) and it == 1:
                    act.wait_ge(up_done, q + 3)
                elif not isinstance(it, int) or it > 1:
                    act.wait_ge(down_done, it * 8 + (4 * q - 12))
                act.activation(wh[:, s, :], wst[:, s, :], ACT.Copy).then_inc(w_hi, 1)

            def evacuate(it, q):
                u, r = it * 4 + q, q % 2
                tile = bass.ds(it * 2 + (q // 2 + r * (FT // 2)), 1)
                act.wait_ge(up_done, u + 1)
                if not isinstance(it, int) or it or q >= 2:
                    act.wait_ge(conv, u - 1)
                    act.wait_ge(kept_cols, u - 1)
                act.activation(as_thirds(up[:, r, 2:2 + T]), thirds(ps, r), ACT.Copy).then_inc(up_evac, 1)
                act.wait_ge(up_evac, u + 1)
                if not isinstance(it, int) or it or q >= 2:
                    act.wait_ge(g_lo, it * 2 + q // 2)
                act.activation(acc[:, r, 0:NP], up[:, r, 0:NP], ACT.Identity, scale=g.cw[:, 0, tile],
                               bias=g.cw[:, 3, tile]).then_inc(tap0, 1)

            def gate(it, r, par):
                m = it * 2 + r
                act.wait_ge(conv, m * 2 + 1)
                act.activation(acc[:, 0, :], acc[:, 0, :], ACT.Gelu_apprx_tanh).then_inc(gelu, 1)

            def part(it, r, par):
                m = it * 2 + r
                act.wait_ge(prod, m + 1)
                if not isinstance(it, int) or it >= 2:
                    act.wait_ge(down_done, (it - 1) * 8)
                act.activation(gh[:, par, r, :], acc[:, 0, :], ACT.Copy).then_inc(g_hi, 1)

            def iteration(it, n, par, last=False):
                high(it, 1)
                for q in range(4):
                    evacuate(it, q)
                    if q + 2 < n:
                        high(it, q + 2)
                    elif q + 2 == n:
                        high(it + 1, 0)
                    if q % 2 == 1:
                        gate(it, q // 2, par)
                        part(it, q // 2, par)
                if last:
                    high(NG2, 4)
                elif n > 4:
                    high(it + 1, 0)

            act.wait_ge(zero, 2)
            high(0, 0)
            iteration(0, 4, 0)
            iteration(1, 6, 1)
            with act.Fori(0, (NG2 - 4) // 2) as j:
                for e in range(2):
                    iteration(j * 2 + (2 + e), 6, e)
            iteration(NG2 - 2, 6, 0)
            iteration(NG2 - 1, 6, 1, last=True)
            high(NG2, 5)
            act.wait_ge(k_turned, 1)
            act.activation(g.kept[:, 0:8, :], ps[0:FT, 6:8, :].rearrange("t b (r p) -> t (b r) p", p=P), ACT.Copy)
            act.activation(g.kept[:, 8:10, :], ps[0:FT, 0, 0:2 * P].rearrange("t (r p) -> t r p", p=P), ACT.Copy).then_inc(k_copied, 1)

        @block.vector
        def _(dve):
            def taps(it, q):
                u, r = it * 4 + q, q % 2
                tile = bass.ds(it * 2 + (q // 2 + r * (FT // 2)), 1)
                dve.wait_ge(tap0, u + 1)
                dve.tensor_copy(acc[:, r, NP:T], g.conv0[:, tile, :].rearrange("p a b -> p (a b)")).then_inc(tap0s, 1)
                dve.scalar_tensor_tensor(out=acc[:, r, 0:NP], in0=up[:, r, 1:1 + NP], scalar=g.cw[:, 1, tile],
                                         in1=acc[:, r, 0:NP], op0=ALU.mult, op1=ALU.add).then_inc(tap1, 1)
                dve.wait_ge(tap0s, u + 1)
                dve.wait_ge(tap1, u + 1)
                dve.scalar_tensor_tensor(out=acc[:, r, :], in0=up[:, r, 2:2 + T], scalar=g.cw[:, 2, tile],
                                         in1=acc[:, r, :], op0=ALU.mult, op1=ALU.add).then_inc(conv, 1)

            def product(it, r, par):
                m = it * 2 + r
                dve.wait_ge(gelu, m + 1)
                dve.wait_ge(conv, m * 2 + 2)
                dve.tensor_tensor(acc[:, 0, :], acc[:, 0, :], acc[:, 1, :], ALU.mult).then_inc(prod, 1)

            def low(it, r, par):
                m = it * 2 + r
                dve.wait_ge(g_hi, m + 1)
                dve.tensor_tensor(gl[:, par, r, :], acc[:, 0, :], gh[:, par, r, :].bitcast(F32), ALU.subtract).then_inc(g_lo, 1)

            def down(d, m):
                dve.wait_ge(down_done, d + 1)
                if not isinstance(d, int) or d >= 8:
                    dve.wait_ge(down_evac, d - 7)
                f = as_thirds(g.fT[:, m, :])
                dve.tensor_tensor(f, thirds(ps, m % 2), f, ALU.add).then_inc(down_evac, 1)

            def iteration(it, par, has_down):
                taps(it, 0)
                taps(it, 1)
                product(it, 0, par)
                low(it, 0, par)
                taps(it, 2)
                if has_down:
                    down(it * 8 - 8, 0)
                taps(it, 3)
                if has_down:
                    down(it * 8 - 7, 1)
                product(it, 1, par)
                if has_down:
                    down(it * 8 - 6, 2)
                low(it, 1, par)
                if has_down:
                    for m in range(3, 8):
                        down(it * 8 + (m - 8), m)

            dve.wait_ge(zero, 2)
            iteration(0, 0, False)
            iteration(1, 1, True)
            with dve.Fori(0, (NG2 - 2) // 2) as j:
                for e in range(2):
                    iteration(j * 2 + (2 + e), e, True)
            for m in range(8):
                down((NG2 - 1) * 8 + m, m)

        @block.tensor
        def _(pe):
            def ups(it, q, j, s):
                u, r = it * 4 + q, q % 2
                pe.wait_ge(w_lo, j + 1)
                if not isinstance(it, int) or it or q >= 2:
                    pe.wait_ge(up_evac, u - 1)
                if q < 2 and (not isinstance(it, int) or it >= 2):
                    pe.wait_ge(down_evac, it * 8 + (q - 9))
                w3, l3 = (w[:, s, :].rearrange("p (k n) -> p k n", k=KD) for w in (wh, wl))
                project(pe, ps, r, w3, l3, g.xT_h, g.xT_l, KD).then_inc(up_done, 1)

            def downs(it, j0, par, ups_before=True):
                pe.wait_ge(g_lo, it * 2)
                for m in range(8):
                    if m % 4 == 0:
                        pe.wait_ge(w_lo, j0 + (m // 4 + 1))
                    if m >= 2 or not ups_before:
                        pe.wait_ge(down_evac, it * 8 + (m - 9))
                    else:
                        pe.wait_ge(up_evac, it * 4 + (3 + m))
                    w3, l3 = (w[:, m // 4, :].rearrange("p (k n) -> p k n", k=2)[:, :, (m % 4) * P:(m % 4 + 1) * P]
                              for w in (wh, wl))
                    project(pe, ps, m % 2, w3, l3, gh[:, par, :, :], gl[:, par, :, :], 2).then_inc(down_done, 1)

            for q in range(4):
                ups(0, q, q, q % 2)
            for q in range(4):
                ups(1, q, job(1, q), q % 2)
            downs(1, job(1, 4), 0)
            with pe.Fori(0, (NG2 - 2) // 2) as j:
                for e in range(2):
                    for q in range(4):
                        ups(j * 2 + (2 + e), q, j * 12 + job(2 + e, q), q % 2)
                    downs(j * 2 + (2 + e), j * 12 + job(2 + e, 4), (1 + e) % 2)
            downs(NG2, job(NG2, 0), 1, ups_before=False)
            pe.wait_ge(kept_cols, FT)
            pe.wait_ge(down_evac, (NG2) * 8)
            for r in range(10):
                bank, o = (6 + r // 4, (r % 4) * P) if r < 8 else (0, (r - 8) * P)
                mm = pe.transpose(ps[0:FT, bank, o:o + P], keep[:, r, :], g.ident[:, :])
            mm.then_inc(k_turned, 1)


def phase_final(nc, g):
    with ExitStack() as ctx:
        sb = lambda n, s, d=F32: ctx.enter_context(nc.sbuf_tensor("y_" + n, s, d))
        ps, sem = g.ps, lambda n: g.sem("y_" + n)
        psf = ps[:, :, :].rearrange("p b c -> p (b c)")
        NR = 3
        gain = sb("gain", [P, D])
        x2 = sb("x2", [P, NR, D])
        y = sb("y", [P, NR, D])
        junk = sb("junk", [P, D])
        st = sb("st", [P, 4, 9])
        g_in, turned, ss_done, var_done, std_done, r_done, y_scaled, y_done = (
            sem(n) for n in ("g_in", "turned", "ss_done", "var_done", "std_done", "r_done", "y_scaled", "y_done"))
        x_in = [sem(f"x_in{i}") for i in range(NR)]
        y_out = [sem(f"y_out{i}") for i in range(NR)]
        block = ctx.enter_context(nc.Block())

        @block.sync
        def _(sp):
            sp.dma_start(gain[:, :], g.g_post_ffn.partition_broadcast(P)).then_inc(g_in, 16)

            def store(i):
                t0, n = TILES[i]
                sp.wait_ge(y_done, i + 1)
                dst = g.y_prompt[t0:t0 + n, :] if i < NT else g.y_sample
                sp.dma_start(dst, y[0:n, i % NR, :]).then_inc(y_out[i % NR], 16)

            for i, (t0, n) in enumerate(TILES):
                if i >= NR:
                    store(i - NR)
                sp.dma_start(x2[0:n, i % NR, :], g.d_x2[t0:t0 + n, :]).then_inc(x_in[i % NR], 16)
            for i in range(9 - NR, 9):
                store(i)
            for s in range(NR):
                sp.wait_ge(y_out[s], 16 * 3)
            sp.wait_ge(g.conv_out, 32)

        @block.scalar
        def _(act):
            for i, (_, n) in enumerate(TILES):
                act.wait_ge(turned, i + 1)
                if i:
                    act.wait_ge(ss_done, i)
                act.activation(junk[0:n, :], psf[0:n, (i % 4) * D:(i % 4 + 1) * D], ACT.Square,
                               accum_out=st[0:n, 0, i:i + 1]).then_inc(ss_done, 1)
                act.wait_ge(var_done, i + 1)
                act.activation(st[0:n, 2, i:i + 1], st[0:n, 1, i:i + 1], ACT.Sqrt).then_inc(std_done, 1)

        @block.gpsimd
        def _(pool):
            for i, (_, n) in enumerate(TILES):
                pool.wait_ge(y_scaled, i + 1)
                pool.wait_ge(x_in[i % NR], 16 * (i // NR + 1))
                if i:
                    pool.wait_ge(y_done, i)
                yi = y[0:n, i % NR, :]
                pool.tensor_tensor(yi, yi, x2[0:n, i % NR, :], ALU.add).then_inc(y_done, 1)

        @block.vector
        def _(dve):
            dve.wait_ge(g_in, 16)
            for i, (_, n) in enumerate(TILES):
                dve.wait_ge(ss_done, i + 1)
                dve.tensor_scalar(st[0:n, 1, i:i + 1], st[0:n, 0, i:i + 1], 1.0 / D, EPS, ALU.mult, ALU.add).then_inc(var_done, 1)
                dve.wait_ge(std_done, i + 1)
                newton_rstd(dve, st[0:n, 3, i:i + 1], st[0:n, 2, i:i + 1], st[0:n, 1, i:i + 1], r_done, 5 * i)
                if i >= NR:
                    dve.wait_ge(y_out[i % NR], 16 * (i // NR))
                yi = y[0:n, i % NR, :]
                dve.scalar_tensor_tensor(out=yi, in0=psf[0:n, (i % 4) * D:(i % 4 + 1) * D], scalar=st[0:n, 3, i:i + 1],
                                         in1=gain[0:n, :], op0=ALU.mult, op1=ALU.mult).then_inc(y_scaled, 1)

        @block.tensor
        def _(pe):
            for i, (t0, n) in enumerate(TILES):
                if i >= 4:
                    pe.wait_ge(y_scaled, i - 3)
                for k in range(KD):
                    o = (i % 4) * D + k * P
                    mm = pe.transpose(psf[0:n, o:o + P], g.fT[:, k, t0:t0 + n], g.ident[:, :])
                mm.then_inc(turned, 1)


PER_LAYER = ["cache_k", "cache_v", "cache_kidx", "state_ssm_re", "state_ssm_im", "state_conv", "w_in", "g_pre_mix",
             "g_post_mix", "lam_re", "lam_im", "log_dt", "b_re", "b_im", "c_re", "c_im", "d_skip", "w_glu", "b_glu",
             "w_att_out", "w_ssm_out", "w_o", "g_pre_ffn", "g_post_ffn", "w_up", "conv_w", "conv_b", "w_down"]


class Program:

    def __init__(self, ins, outs):
        self.x_prompt = ins["x_prompt"]
        self.x_sample = ins["x_sample"]
        self.page_table = ins["page_table"]
        self.rel_bias = ins["rel_bias"]
        self.cache_k = ins["cache_k"][0].rearrange("n p h d -> n p (h d)")
        self.cache_v = ins["cache_v"][0].rearrange("n p h d -> n p (h d)")
        self.cache_kidx = ins["cache_kidx"][0]
        self.state_re = ins["state_ssm_re"][0]
        self.state_im = ins["state_ssm_im"][0]
        self.state_conv = ins["state_conv"][0]
        self.w_in = ins["w_in"][0]
        self.g_pre_mix = ins["g_pre_mix"][0]
        self.g_post_mix = ins["g_post_mix"][0]
        self.lam_re = ins["lam_re"][0]
        self.lam_im = ins["lam_im"][0]
        self.log_dt = ins["log_dt"][0]
        self.b_re = ins["b_re"][0]
        self.b_im = ins["b_im"][0]
        self.c_re = ins["c_re"][0]
        self.c_im = ins["c_im"][0]
        self.d_skip = ins["d_skip"][0]
        self.w_glu = ins["w_glu"][0]
        self.b_glu = ins["b_glu"][0]
        self.w_att_out = ins["w_att_out"][0]
        self.w_ssm_out = ins["w_ssm_out"][0]
        self.w_o = ins["w_o"][0]
        self.g_pre_ffn = ins["g_pre_ffn"][0]
        self.g_post_ffn = ins["g_post_ffn"][0]
        self.w_up = ins["w_up"][0]
        self.conv_w = ins["conv_w"][0]
        self.conv_b = ins["conv_b"][0]
        self.w_down = ins["w_down"][0]
        self.c_ident = ins["c_ident"]
        self.c_not_causal = ins["c_not_causal"]
        self.c_sign = ins["c_sign"]
        self.c_swap = ins["c_swap"]
        self.c_onehot = ins["c_onehot"]
        self.c_onehot_s = ins["c_onehot_s"]
        self.c_own = ins["c_own"]
        self.c_own32 = ins["c_own32"]
        self.c_own64 = ins["c_own64"]
        self.c_jsel = ins["c_jsel"]
        self.c_headsel = ins["c_headsel"]
        self.y_prompt = outs["y_prompt"]
        self.y_sample = outs["y_sample"]
        self.k_prompt = outs["k_prompt"]
        self.v_prompt = outs["v_prompt"]
        self.kidx_prompt = outs["kidx_prompt"]
        self.ssm_re_prompt = outs["ssm_re_prompt"]
        self.ssm_im_prompt = outs["ssm_im_prompt"]
        self.conv_prompt = outs["conv_prompt"]
        self.k_sample = outs["k_sample"]
        self.v_sample = outs["v_sample"]
        self.kidx_sample = outs["kidx_sample"]
        self.ssm_re_sample = outs["ssm_re_sample"]
        self.ssm_im_sample = outs["ssm_im_sample"]
        self.conv_sample = outs["conv_sample"]


def build(nc, ins, outs):
    g = Program(ins, outs)

    def scratch(name, shape):
        return nc.dram_tensor(name, shape, F32, kind="Internal").ap()

    g.d_gates = scratch("d_gates", (P, 16, T))
    g.d_u, g.d_us = scratch("d_u", (NP, SW)), scratch("d_us", (NS, SW))
    g.d_bias, g.d_x2 = scratch("d_bias", (H, P * DIST)), scratch("d_x2", (T, D))
    taken = []

    def sem(name):
        taken.append(nc.alloc_semaphore(name))
        return taken[-1]

    g.sem = sem

    def place(stack, name, shape, dt=F32, side=None):
        return stack.enter_context(nc.sbuf_tensor("g_" + name, shape, dt, side=side))

    with ExitStack() as ctx:
        g.ps = ctx.enter_context(nc.psum_tensor("ps", [P, 8, BANK], F32))
        g.ident = place(ctx, "ident", [P, P])
        g.cw, g.conv0 = place(ctx, "cw", [P, 4, FT]), place(ctx, "conv0", [P, FT, NS])
        with ExitStack() as branches:
            with ExitStack() as att:
                g.qT, g.kT = place(att, "qT", [P, 4, T]), place(att, "kT", [P, 4, T])
                g.qiT, g.kwT = place(att, "qiT", [P, 2, T]), place(att, "kwT", [68, T])
                masks = place(att, "masks", [P, sum((i + 1) * P for i in range(2, NT))])
                starts = [sum((j + 1) * P for j in range(2, i)) for i in range(2, NT + 1)]
                g.mask = [masks[:, a:b] for a, b in zip(starts, starts[1:])]
                with ExitStack() as ssm:
                    with ExitStack() as par:
                        g.par = SsmParameters(nc, par, sem)
                        with ExitStack() as first:
                            g.kiT2 = place(first, "kiT2", [P, T])
                            g.hT_h, g.hT_l = (place(first, n, [P, KD, T], F32R) for n in ("hT_h", "hT_l"))
                            phase_norm(nc, g)
                            phase_project(nc, g)
                        g.gT = place(ssm, "gT", [P, 4, T])
                        phase_ssm(nc, g)
                    g.ys_h, g.ys_l = (place(branches, n, [P, 4, T], F32R, "right") for n in ("ys_h", "ys_l"))
                    phase_glu(nc, g)
                nc.clear_and_free_semaphores(taken[:])
                taken.clear()
                nc.all_engine_barrier()
                g.ya_h, g.ya_l = (place(branches, n, [P, 4, T], F32R, "right") for n in ("ya_h", "ya_l"))
                g.table, g.kx = place(att, "table", [1, NS * 2], I32), place(att, "kx", [P, NS, 2, ID])
                phase_attention(nc, g)
                phase_sample(nc, g)
            g.xT_h, g.xT_l = (place(ctx, n, [P, KD, T], F32R) for n in ("xT_h", "xT_l"))
            phase_merge(nc, g)
        phase_out(nc, g)
        g.fT, g.kept, g.conv_out = place(ctx, "fT", [P, KD, T]), place(ctx, "kept", [FT, 10, P]), sem("conv_out")
        phase_ffn(nc, g)
        phase_final(nc, g)


def shape_constants():
    f = np.float32
    starts = np.array(bucket_of_distance())
    own = np.eye(NS, dtype=f)
    bucket = lambda d: (starts[np.maximum(d, 0)][None] == np.arange(NB)[:, None]).astype(f)
    return {
        "c_ident": np.eye(P, dtype=f),
        "c_not_causal": np.triu(np.ones((P, P), f), 1),
        "c_sign": np.repeat(np.array([-1, 1], f), ST)[:, None].copy(),
        "c_swap": np.roll(np.eye(P, dtype=f), ST, 0),
        "c_onehot": bucket(2 * P - 1 - np.arange(DIST)),
        "c_onehot_s": bucket(PAST - np.arange(SK)),
        "c_own": np.concatenate([np.repeat(own, JH, 1), np.repeat(own, H, 1)], 1),
        "c_own32": np.repeat(own, JH, 0),
        "c_own64": np.repeat(own, H, 0),
        "c_headsel": np.tile(np.eye(H, dtype=f), (NS, 1)),
        "c_jsel": np.tile(np.eye(JH, dtype=f), (1, NS)),
    }


_INS = ["x_prompt", "x_sample", "page_table", "rel_bias"] + PER_LAYER
_OUTS = [
    ("y_prompt", (NP, D), (1, NP, D)), ("y_sample", (NS, D), (NS, 1, D)),
    ("k_prompt", (NP, AW), (1, 1, NP, H, HD)), ("v_prompt", (NP, AW), (1, 1, NP, H, HD)),
    ("kidx_prompt", (NP, ID), (1, 1, NP, ID)),
    ("ssm_re_prompt", (NG, ST), (1, 1, NG, ST)), ("ssm_im_prompt", (NG, ST), (1, 1, NG, ST)),
    ("conv_prompt", (2, 2 * FF), (1, 1, 2, 2 * FF)),
    ("k_sample", (NS, AW), (1, NS, 1, H, HD)), ("v_sample", (NS, AW), (1, NS, 1, H, HD)),
    ("kidx_sample", (NS, ID), (1, NS, 1, ID)),
    ("ssm_re_sample", (NS, NG, ST), (1, NS, NG, ST)), ("ssm_im_sample", (NS, NG, ST), (1, NS, NG, ST)),
    ("conv_sample", (NS, 2, 2 * FF), (1, NS, 2, 2 * FF)),
]


def kernel(**inputs):
    import concourse.bacc as _bacc
    from concourse.bass_utils import run_bass_kernel_spmd as _run

    nc = _bacc.Bacc("TRN2", target_bir_lowering=False, num_devices=1)
    arrays = {f"in_{n}": np.ascontiguousarray(inputs[n]) for n in _INS}
    arrays.update({f"in_{n}": np.ascontiguousarray(a) for n, a in shape_constants().items()})
    ins = {n[3:]: nc.dram_tensor(n, a.shape, mybir.dt.from_np(a.dtype), kind="ExternalInput").ap()
           for n, a in arrays.items()}
    outs = {n: nc.dram_tensor("out_" + n, shape, F32, kind="ExternalOutput").ap() for n, shape, _ in _OUTS}
    build(nc, ins, outs)
    r = _run(nc, [arrays], core_ids=[0])
    return tuple(np.asarray(r.results[0]["out_" + n]).reshape(shape) for n, _, shape in _OUTS)
```
